# Optimizing a Trainium2 kernel written in Bass

```python
import math, functools
import jax, jax.numpy as jnp
from jax import lax
import numpy as np

D_MODEL = 1024
BATCH = 1
SEQ = 128
DEPTH = 2
DEC_BATCH = 1
DEC_SEQ = 256
PAST_LEN = 128

GRID_W = 64
A_WIDTH = D_MODEL // 4
B_WIDTH = D_MODEL // 4
C_WIDTH = D_MODEL // 2
MIX_WIDTH = A_WIDTH + B_WIDTH + C_WIDTH
N_HEADS_ATTN = 8
HEAD_DIM = C_WIDTH // N_HEADS_ATTN
POOL_WINDOWS = (2, 4, 8, 16)
N_POOL_GROUPS = 4
POOL_GROUP_C = B_WIDTH // N_POOL_GROUPS
NA_ROWS_MAX = 8
NA_COLS = 16
NA_QB = NA_COLS
NA_KB = 2 * NA_COLS
PEER_HEADS = 8
PEER_KEYS = 128
PEER_EXPERTS = PEER_KEYS * PEER_KEYS
PEER_TOPK = 16
PEER_QDIM = 256
PEER_HALF = PEER_QDIM // 2
PEER_CHUNK = 128
IN_COLS = 3 * A_WIDTH + B_WIDTH + 3 * C_WIDTH
IN_SPLITS = [A_WIDTH, 2 * A_WIDTH, 3 * A_WIDTH, 3 * A_WIDTH + B_WIDTH,
             3 * A_WIDTH + B_WIDTH + C_WIDTH, 3 * A_WIDTH + B_WIDTH + 2 * C_WIDTH]
N_MOD = 6
EPS = 1e-6
NEG_INF = -1e30

kernel_name = 'hybrid_conv_pool_natten_peer_diffusion_step'

def _rmsnorm(x, g):
    xf = x.astype(jnp.float32)
    y = xf * lax.rsqrt(jnp.mean(xf * xf, axis=-1, keepdims=True) + EPS)
    return (y * g.astype(jnp.float32)).astype(x.dtype)

def _modulation(cvec, w_ada_l, b_ada_l):
    m = jax.nn.silu(cvec) @ w_ada_l + b_ada_l
    return [t[:, None, :] for t in jnp.split(m, N_MOD, axis=-1)]

def _short_conv(a_in, a_b, a_c, conv_w):
    u = a_c * a_in
    L = u.shape[1]
    up = jnp.pad(u, ((0, 0), (1, 1), (0, 0)))
    y = conv_w[0] * up[:, :L] + conv_w[1] * up[:, 1:L + 1] + conv_w[2] * up[:, 2:]
    return a_b * y

def _multi_pool(p, pool_w, pool_scale):
    Bn, L, _ = p.shape
    t = np.arange(L)[:, None]
    w = np.array(POOL_WINDOWS)[None, :]
    lo = np.clip(t - w // 2, 0, L - 1)
    hi = np.clip(t + w - 1 - w // 2, 0, L - 1)
    lo_c = np.repeat(lo, POOL_GROUP_C, axis=1)
    hi_c = np.repeat(hi, POOL_GROUP_C, axis=1)
    cnt = (hi_c - lo_c + 1).astype(np.float32)
    ch = np.arange(B_WIDTH)[None, :]
    pf = p.astype(jnp.float32)
    csum = jnp.concatenate([jnp.zeros_like(pf[:, :1]), jnp.cumsum(pf, axis=1)], axis=1)
    mean = (csum[:, hi_c + 1, ch] - csum[:, lo_c, ch]) / cnt
    d = (mean - pf).astype(p.dtype).reshape(Bn, L, N_POOL_GROUPS, POOL_GROUP_C)
    y = jnp.einsum('blgc,gcd->blgd', d, pool_w).reshape(Bn, L, B_WIDTH)
    return y * pool_scale

def _heads(t):
    Bn, L, _ = t.shape
    return t.reshape(Bn, L, N_HEADS_ATTN, HEAD_DIM).transpose(0, 2, 1, 3)

def _ctx_attention(q, k, v):
    Bn, L, _ = q.shape
    qh, kh, vh = _heads(q), _heads(k), _heads(v)
    s = jnp.einsum('bhqd,bhkd->bhqk', qh, kh).astype(jnp.float32) * (HEAD_DIM ** -0.5)
    pr = jax.nn.softmax(s, axis=-1).astype(v.dtype)
    o = jnp.einsum('bhqk,bhkd->bhqd', pr, vh)
    return o.transpose(0, 2, 1, 3).reshape(Bn, L, C_WIDTH), (kh, vh)

def _na_tables(rows):
    nrow = min(NA_ROWS_MAX, rows)
    r = np.arange(rows)
    rs = np.clip(r - nrow // 2, 0, rows - nrow)
    row_idx = rs[:, None] + np.arange(nrow)[None, :]
    dr_idx = row_idx - r[:, None] + NA_ROWS_MAX - 1
    ncb = GRID_W // NA_QB
    cb0 = np.arange(ncb) * NA_QB
    kb = np.clip(cb0 - NA_COLS // 2, 0, GRID_W - NA_KB)
    col_idx = kb[:, None] + np.arange(NA_KB)[None, :]
    qcol = cb0[:, None] + np.arange(NA_QB)[None, :]
    cs = np.clip(qcol - NA_COLS // 2, 0, GRID_W - NA_COLS)
    kc = col_idx[:, None, :]
    valid = (kc >= cs[..., None]) & (kc < cs[..., None] + NA_COLS)
    dc_idx = np.clip(kc - qcol[..., None], -(NA_COLS - 1), NA_COLS - 1) + NA_COLS - 1
    return nrow, ncb, row_idx, dr_idx, col_idx, valid, dc_idx

def _latent_attention(q, k, v, ck, cv, rpb):
    Bn, N, _ = q.shape
    rows = N // GRID_W
    nrow, ncb, row_idx, dr_idx, col_idx, valid, dc_idx = _na_tables(rows)
    nw = nrow * NA_KB
    qh, kh, vh = _heads(q), _heads(k), _heads(v)
    qb = qh.reshape(Bn, N_HEADS_ATTN, rows, ncb, NA_QB, HEAD_DIM)
    ri = row_idx[:, None, :, None]
    ci = col_idx[None, :, None, :]
    kg = kh.reshape(Bn, N_HEADS_ATTN, rows, GRID_W, HEAD_DIM)[:, :, ri, ci].reshape(
        Bn, N_HEADS_ATTN, rows, ncb, nw, HEAD_DIM)
    vg = vh.reshape(Bn, N_HEADS_ATTN, rows, GRID_W, HEAD_DIM)[:, :, ri, ci].reshape(
        Bn, N_HEADS_ATTN, rows, ncb, nw, HEAD_DIM)
    scale = HEAD_DIM ** -0.5
    s_win = jnp.einsum('bhrcqd,bhrckd->bhrcqk', qb, kg).astype(jnp.float32) * scale
    bias = rpb[:, dr_idx[:, None, None, :, None], dc_idx[None, :, :, None, :]].reshape(
        N_HEADS_ATTN, rows, ncb, NA_QB, nw)
    mask = np.broadcast_to(valid[:, :, None, :], (ncb, NA_QB, nrow, NA_KB)).reshape(ncb, NA_QB, nw)
    s_win = jnp.where(mask, s_win + bias.astype(jnp.float32)[None], NEG_INF)
    Lc = ck.shape[2]
    s_ctx = (jnp.einsum('bhnd,bhmd->bhnm', qh, ck).astype(jnp.float32) * scale).reshape(
        Bn, N_HEADS_ATTN, rows, ncb, NA_QB, Lc)
    pr = jax.nn.softmax(jnp.concatenate([s_win, s_ctx], axis=-1), axis=-1).astype(v.dtype)
    o = (jnp.einsum('bhrcqk,bhrckd->bhrcqd', pr[..., :nw], vg)
         + jnp.einsum('bhrcqm,bhmd->bhrcqd', pr[..., nw:], cv))
    o = o.reshape(Bn, N_HEADS_ATTN, N, HEAD_DIM).transpose(0, 2, 1, 3).reshape(Bn, N, C_WIDTH)
    return o, None

def _peer(x, w_q, sub_keys, u, v):
    Bn, L, D = x.shape
    T = Bn * L
    xt = x.reshape(T, D)
    q = (xt @ w_q).reshape(T, PEER_HEADS, 2, PEER_HALF)
    s = jnp.einsum('thpd,hpkd->thpk', q, sub_keys).astype(jnp.float32)
    sv, si = lax.top_k(s, PEER_TOPK)
    cand = (sv[:, :, 0, :, None] + sv[:, :, 1, None, :]).reshape(T, PEER_HEADS, PEER_TOPK * PEER_TOPK)
    top, f = lax.top_k(cand, PEER_TOPK)
    i1 = jnp.take_along_axis(si[:, :, 0], f // PEER_TOPK, axis=-1)
    i2 = jnp.take_along_axis(si[:, :, 1], f % PEER_TOPK, axis=-1)
    nch = T // PEER_CHUNK
    experts = (i1 * PEER_KEYS + i2).reshape(nch, PEER_CHUNK, PEER_HEADS * PEER_TOPK)
    gates = jax.nn.softmax(top, axis=-1).astype(x.dtype).reshape(nch, PEER_CHUNK, PEER_HEADS * PEER_TOPK)

    def _chunk(args):
        xc, ec, gc = args
        h = jax.nn.gelu(jnp.einsum('tkd,td->tk', u[ec], xc))
        return jnp.einsum('tk,tkd->td', gc * h, v[ec])

    out = lax.map(_chunk, (xt.reshape(nch, PEER_CHUNK, D), experts, gates))
    return out.reshape(Bn, L, D)

def _layer(x, mods, params, attend):
    g1, g2, w_in_l, conv_l, pool_w_l, pool_s_l, w_out_l, wq_l, sk_l, u_l, v_l = params
    sh1, sc1, gt1, sh2, sc2, gt2 = mods
    h = _rmsnorm(x, g1) * (1 + sc1) + sh1
    a_in, a_b, a_c, p_in, q, k, v = jnp.split(h @ w_in_l, IN_SPLITS, axis=-1)
    y_attn, ctx_kv = attend(q, k, v)
    y = jnp.concatenate([_short_conv(a_in, a_b, a_c, conv_l),
                         _multi_pool(p_in, pool_w_l, pool_s_l),
                         y_attn], axis=-1)
    x = x + gt1 * (y @ w_out_l)
    h = _rmsnorm(x, g2) * (1 + sc2) + sh2
    x = x + gt2 * _peer(h, wq_l, sk_l, u_l, v_l)
    return x, ctx_kv

def setup_inputs(seed: int = 0) -> dict:
    key = jax.random.key(seed)
    ks = jax.random.split(key, 21)
    nrm = jax.random.normal
    f32 = jnp.float32
    D = D_MODEL
    return {
        'x_prompt': nrm(ks[0], (BATCH, SEQ, D), f32),
        'x_sample': nrm(ks[1], (DEC_BATCH, DEC_SEQ, D), f32),
        'c': nrm(ks[2], (DEC_BATCH, D), f32),
        'cache_k': nrm(ks[3], (DEC_BATCH, DEPTH, N_HEADS_ATTN, PAST_LEN, HEAD_DIM), f32),
        'cache_v': nrm(ks[4], (DEC_BATCH, DEPTH, N_HEADS_ATTN, PAST_LEN, HEAD_DIM), f32),
        'c_ctx': nrm(ks[5], (D,), f32),
        'norm1_g': 1.0 + 0.1 * nrm(ks[6], (DEPTH, D), f32),
        'norm2_g': 1.0 + 0.1 * nrm(ks[7], (DEPTH, D), f32),
        'w_ada': nrm(ks[8], (DEPTH, D, N_MOD * D), f32) * (0.5 * D ** -0.5),
        'b_ada': 0.02 * nrm(ks[9], (DEPTH, N_MOD * D), f32),
        'w_in': nrm(ks[10], (DEPTH, D, IN_COLS), f32) * D ** -0.5,
        'conv_w': nrm(ks[11], (DEPTH, 3, A_WIDTH), f32) * 3 ** -0.5,
        'pool_w': nrm(ks[12], (DEPTH, N_POOL_GROUPS, POOL_GROUP_C, POOL_GROUP_C), f32) * POOL_GROUP_C ** -0.5,
        'pool_scale': 1.0 + 0.1 * nrm(ks[13], (DEPTH, B_WIDTH), f32),
        'rpb': 0.1 * nrm(ks[14], (DEPTH, N_HEADS_ATTN, 2 * NA_ROWS_MAX - 1, 2 * NA_COLS - 1), f32),
        'w_out': nrm(ks[15], (DEPTH, MIX_WIDTH, D), f32) * MIX_WIDTH ** -0.5,
        'peer_wq': nrm(ks[16], (DEPTH, D, PEER_HEADS * PEER_QDIM), f32) * D ** -0.5,
        'peer_subkeys': nrm(ks[17], (DEPTH, PEER_HEADS, 2, PEER_KEYS, PEER_HALF), f32) * PEER_HALF ** -0.5,
        'peer_u': nrm(ks[18], (DEPTH, PEER_EXPERTS, D), f32) * D ** -0.5,
        'peer_v': nrm(ks[19], (DEPTH, PEER_EXPERTS, D), f32) * 0.5,
        'final_g': 1.0 + 0.1 * nrm(ks[20], (D,), f32),
    }

def reference(x_prompt, x_sample, c, cache_k, cache_v, c_ctx, norm1_g, norm2_g, w_ada, b_ada,
              w_in, conv_w, pool_w, pool_scale, rpb, w_out, peer_wq, peer_subkeys, peer_u, peer_v,
              final_g):
    xp, xs = x_prompt, x_sample
    cp = c_ctx[None, :]
    ks_new, vs_new = [], []
    for l in range(DEPTH):
        params = (norm1_g[l], norm2_g[l], w_in[l], conv_w[l], pool_w[l], pool_scale[l], w_out[l],
                  peer_wq[l], peer_subkeys[l], peer_u[l], peer_v[l])
        xp, (k_l, v_l) = _layer(xp, _modulation(cp, w_ada[l], b_ada[l]), params, _ctx_attention)
        ks_new.append(k_l)
        vs_new.append(v_l)
        attend = functools.partial(_latent_attention, ck=cache_k[:, l], cv=cache_v[:, l], rpb=rpb[l])
        xs, _ = _layer(xs, _modulation(c, w_ada[l], b_ada[l]), params, attend)
    y_prompt = _rmsnorm(xp, final_g)
    y_sample = _rmsnorm(xs, final_g)
    new_cache_k = jnp.stack(ks_new, axis=1)
    new_cache_v = jnp.stack(vs_new, axis=1)
    return (y_prompt, y_sample, new_cache_k, new_cache_v)


_drawn_inputs = setup_inputs


def setup_inputs(seed=0):
    import zlib

    import numpy as np

    out = dict(_drawn_inputs(seed))
    spreads = {}
    factors = {'rpb': 7.575}
    for name, (base, spread) in spreads.items():
        noise = np.random.default_rng([zlib.crc32(name.encode()), seed]).standard_normal(out[name].shape)
        drawn = base * np.exp(spread * noise) if base else spread * noise
        out[name] = __import__('jax').numpy.asarray(drawn.astype(out[name].dtype))
    for name, factor in factors.items():
        out[name] = (out[name] * factor).astype(out[name].dtype)
    return out
```

```python
from contextlib import ExitStack

import numpy as np

import concourse.bass as bass
from concourse import mybir

F32 = mybir.dt.float32
F32R = mybir.dt.float32r
U32 = mybir.dt.uint32
ALU = mybir.AluOpType
ACT = mybir.ActivationFunctionType
AX = mybir.AxisListType

P = 128
D = 1024
KC = D // P
DEPTH = 2
TCTX, TLAT = 128, 256
T = TCTX + TLAT
TB = T // P
SEGS = ((0, TCTX), (TCTX, T))
EPS = 1e-6
WCOLS = 256
AW = D // 4
CW = D // 2
NH, HD = 8, 64
SCALE = HD ** -0.5
GRID = 64
ROWS = TLAT // GRID
NCOLS = 16
DR, DC = 15, 31
TPW = 2 * GRID - 1
KEYS = TLAT + 128
PAD = 8
PW = T + 4 * PAD
SEG_AT = (PAD, TCTX + 3 * PAD)
PH, TOPK, NK = 8, 16, 128
HP = 2 * PH
NB = NK
G = 4
NG = NB // G
NEG = -3.0e38

ROW_ADA, ROW_G1, ROW_G2, ROW_PS, ROW_CONV, ROW_FG, NROWS = 0, 48, 56, 64, 66, 72, 80
SH1, SC1, GT1, SH2, SC2, GT2 = (KC * i for i in range(6))
C_ID, C_FLIP, C_ONE, C_IOTA, C_MASK, C_RCNT = 0, 128, 256, 384, 512, 576
NCONST = C_RCNT + 2 * T
N_ADA, N_IN, N_OUT, N_WQ = 24, 10, 4, 8
W_IN0 = N_ADA
W_OUT0 = W_IN0 + N_IN
W_WQ0 = W_OUT0 + N_OUT
W_SK0 = W_WQ0 + N_WQ
W_PER = W_SK0 + 2
WR = 4
assert W_PER % WR == 0
ROUTE_STEPS = 13
BASE = 16512


class Signal:

    def __init__(self, nc, ctx, name, per, credit=0):
        self.sem = ctx.enter_context(nc.semaphore(name))
        self.per, self.credit = per, credit

    def at(self, l, k):
        return l * self.per + (self.credit + k)


class Chain:

    def __init__(self, eng, sig, base, per):
        self.eng, self.sem, self.base, self.per, self.n = eng, sig.sem, base, per, 0

    def then(self, ins, passed=None):
        self.n += 1
        ins.then_inc(self.sem, 1)
        self.eng.wait_ge(self.sem, self.base + self.n)
        if passed is not None:
            self.eng.sem_inc(passed.sem, 1)

    def close(self):
        assert self.n == self.per, (self.n, self.per)


def build(nc, x_prompt, x_sample, c, cache_k, cache_v, c_ctx, norm1_g, norm2_g, w_ada, b_ada, w_in, conv_w,
          pool_w, pool_scale, rpb, w_out, peer_wq, peer_subkeys, peer_u, peer_v, final_g, consts,
          y_prompt, y_sample, new_k, new_v):
    ctx = ExitStack()
    place = [BASE]

    def at(name, shape, dtype=F32, offset=None):
        size = 4 * int(np.prod(shape[1:]))
        if offset is None:
            offset = place[0]
            place[0] += -(-size // 32) * 32
        assert offset + size <= nc.sbuf_usable_end, (name, offset + size)
        return nc.alloc_sbuf_tensor_at(name, list(shape), dtype, offset=offset)

    cst = at("cst", [P, NCONST])
    x = at("x", [P, KC, T])
    h = at("h", [P, KC, T])
    wring = at("wring", [P, WR, KC, WCOLS])
    vec_nat = at("vec_nat", [P, P])
    vecs = at("vecs", [P, NROWS])
    silu_c = at("silu_c", [P, KC, 2])
    mods = at("mods", [P, 6 * KC, 2])
    gs = at("gs", [P, 2, KC, 2])
    pool_blk = at("pool_blk", [P, 2, P])
    stat = at("stat", [P, 2, 4])
    arena = place[0]

    x_nat = at("x_nat", [P, TB, D], offset=arena)
    branch = at("branch", [P, 6, T])
    pool_in = at("pool_in", [P, 2, PW])
    pool_s = at("pool_s", [P, 2, PW])
    pool_r = at("pool_r", [P, 2, PW])
    pool_d = at("pool_d", [P, 2, T])
    conv_u = at("conv_u", [P, 2, T])
    qT = at("qT", [P, 4, T])
    kT = at("kT", [P, 4, T])
    vN = at("vN", [P, TB, CW])
    y = at("y", [P, KC, T])
    k_out = at("k_out", [P, CW])
    cK = at("cK", [P, CW])
    cV = at("cV", [P, CW])
    cKT = at("cKT", [P, 4, P])
    bias_tab = at("bias_tab", [P, TPW])
    bias = at("bias", [P, 2, NH, TLAT])
    norm_t = at("norm_t", [P, 3, T])
    pr = at("pr", [P, 2, KEYS])
    prT = at("prT", [P, 2, 3, P])
    c_nat = at("c_nat", [16, P])

    place[0] = arena
    pq = at("pq", [P, HP, T])
    skT = at("skT", [P, HP, NK])
    s_sb = at("s_sb", [P, HP, NK])
    left = at("left", [P, HP, NK])
    cand = at("cand", [P, PH, TOPK, TOPK])
    top_s = at("top_s", [P, HP, TOPK])
    top_iu = at("top_iu", [P, HP, TOPK], U32)
    top_i = at("top_i", [P, HP, TOPK])
    best = at("best", [P, PH, TOPK])
    best_iu = at("best_iu", [P, PH, TOPK], U32)
    part_u = at("part_u", [P, 2, PH, TOPK], U32)
    part = at("part", [P, 2, PH, TOPK])
    picked = at("picked", [P, 3, PH * TOPK])
    gsum = at("gsum", [P, 2, PH])
    pickT = at("pickT", [P, 3, T])
    one_a = at("one_a", [P, 8, P])
    one_b = at("one_b", [P, 8, P])
    g_all = at("g_all", [P, NK, P])

    place[0] = arena
    u_raw = at("u_raw", [P, 4, D])
    v_raw = at("v_raw", [P, 2 * G, 512])
    h_hi = at("h_hi", [P, KC, T], F32R)
    h_lo = at("h_lo", [P, KC, T], F32R)
    u_hi = at("u_hi", [P, 2, KC, P], F32R)
    u_lo = at("u_lo", [P, 2, KC, P], F32R)
    v_hi = at("v_hi", [P, 4, 512], F32R)
    v_lo = at("v_lo", [P, 4, 512], F32R)
    w_hi = at("w_hi", [P, 2 * G, T], F32R)
    w_lo = at("w_lo", [P, 2 * G, T], F32R)
    gate = at("gate", [P, 4, T])
    act_h = at("act_h", [P, 2, T])
    w32 = at("w32", [P, 2, T])
    acc = at("acc", [P, TB, D])
    y_nat = at("y_nat", [P, TB, D], offset=arena)

    ps = ctx.enter_context(nc.psum_tensor([P, 8, 512], F32))
    tab_dram = nc.dram_tensor("bias_scratch", (NH * DR, TPW), F32)
    gate_dram = nc.dram_tensor("gate_scratch", (NK, P, T), F32).ap()

    ident = cst[:, C_ID:C_ID + P]
    flip = cst[:, C_FLIP:C_FLIP + P]
    ones = cst[:, C_ONE:C_ONE + P]
    iota = cst[:, C_IOTA:C_IOTA + P]
    colmask = cst[:, C_MASK:C_MASK + GRID]
    rcnt = cst[:, C_RCNT:C_RCNT + 2 * T].rearrange("p (b t) -> p b t", b=2)

    bias_v = bias[:].rearrange("p a h (r c) -> p (a h r) c", c=GRID)

    def S(name, per, credit=0):
        return Signal(nc, ctx, name, per, credit)

    const_ld = S("const_ld", 0)
    x_ld = S("x_ld", 0)
    xi_mm = S("xi_mm", 0)
    xi_evac = S("xi_evac", 0)
    c_tr = S("c_tr", 0)
    silu_rdy = S("silu_rdy", 0)
    zero_rdy = S("zero_rdy", 0)
    vec_ld = S("vec_ld", 16 * 6)
    vec_tr = S("vec_tr", 1, credit=1)
    vec_rdy = S("vec_rdy", 1)
    w_ld = [S(f"w_ld{i}", 16 * (W_PER // WR)) for i in range(WR)]
    w_used = S("w_used", W_PER, credit=WR)
    sq_rdy = S("sq_rdy", 2)
    sum_mm = S("sum_mm", 2)
    var_rdy = S("var_rdy", 2)
    std_rdy = S("std_rdy", 2)
    xn_rdy = S("xn_rdy", 2)
    h_rdy = S("h_rdy", 2)
    norm_ch = S("norm_ch", 2 * 5)
    mods_rdy = S("mods_rdy", 1)
    mods_ch = S("mods_ch", 1)
    pj_mm = S("pj_mm", 22)
    pj_evac = S("pj_evac", 22, credit=2)
    kc_mm = S("kc_mm", 1)
    kc_evac = S("kc_evac", 1)
    kv_st = S("kv_st", 32)
    cache_ld = S("cache_ld", 32)
    ck_mm = S("ck_mm", 1)
    ck_evac = S("ck_evac", 1)
    tab_ld = S("tab_ld", 16)
    tab_st = S("tab_st", 16)
    bias_ld = S("bias_ld", 16 * ROWS * NH)
    bias_rdy = S("bias_rdy", 1)
    pad_rdy = S("pad_rdy", 1)
    poolw_ld = S("poolw_ld", 64)
    conv_ch = S("conv_ch", 4)
    pool_ch = S("pool_ch", 6)
    pd_rdy = S("pd_rdy", 1)
    pool_mm = S("pool_mm", 1)
    branch_rdy = S("branch_rdy", 1)
    NU = 3 * NH
    s_mm = S("s_mm", NU)
    att_ch = S("att_ch", 2 * NU)
    nmax_rdy = S("nmax_rdy", NU)
    exp_rdy = S("exp_rdy", NU, credit=2)
    pr_rdy = S("pr_rdy", NU)
    t_mm = S("t_mm", NU)
    t_evac = S("t_evac", NU, credit=2)
    o_mm = S("o_mm", NU)
    o_evac = S("o_evac", NU, credit=2)
    xo_mm = S("xo_mm", KC)
    xo_evac = S("xo_evac", KC, credit=2)
    pq_mm = S("pq_mm", HP)
    pq_evac = S("pq_evac", HP, credit=2)
    sk_mm = S("sk_mm", 4)
    sk_evac = S("sk_evac", 4)
    sc_mm = S("sc_mm", 4 * TB)
    sc_evac = S("sc_evac", 4 * TB)
    route_ch = S("route_ch", ROUTE_STEPS * TB)
    s_free = S("s_free", TB, credit=1)
    gexp_in = S("gexp_in", TB)
    gexp_rdy = S("gexp_rdy", TB)
    pk_rdy = S("pk_rdy", TB)
    pk_mm = S("pk_mm", TB)
    pk_evac = S("pk_evac", TB)
    NQ = T // 4
    one_rdy = S("one_rdy", NQ)
    gq_mm = S("gq_mm", NQ, credit=2)
    gq_evac = S("gq_evac", NQ, credit=2)
    g_st = S("g_st", 16 * TB)
    hh_rdy = S("hh_rdy", 1)
    hl_rdy = S("hl_rdy", 1)
    u_ld = [S(f"u_ld{i}", 16 * (NB // 4)) for i in range(4)]
    ut_mm = S("ut_mm", 2 * NB, credit=8)
    uhi_rdy = S("uhi_rdy", 2 * NB)
    ulo_rdy = S("ulo_rdy", 2 * NB, credit=2)
    h_mm = S("h_mm", NB, credit=2)
    gelu_rdy = S("gelu_rdy", NB, credit=2)
    g_ld = [S(f"g_ld{i}", 16 * (NB // 4)) for i in range(4)]
    w32_rdy = S("w32_rdy", NB, credit=4)
    whi_rdy = S("whi_rdy", NB)
    wlo_rdy = S("wlo_rdy", NB)
    NV = 2 * NB
    v_ld = [S(f"v_ld{i}", 16 * (NV // (2 * G))) for i in range(2 * G)]
    vhi_rdy = S("vhi_rdy", NV)
    vlo_rdy = S("vlo_rdy", NV, credit=2 * G)
    v_mm = S("v_mm", NV, credit=4)
    ac_evac = S("ac_evac", 2 * NG, credit=1)
    acc_zero = S("acc_zero", 1)
    xa_mm = S("xa_mm", KC)
    xa_evac = S("xa_evac", KC, credit=2)
    fo_mm = S("fo_mm", 0)
    fo_evac = S("fo_evac", 0)
    y_st = S("y_st", 0)

    dve_passed = S("dve_passed", 0)
    pool_passed = S("pool_passed", 0)

    block = ctx.enter_context(nc.Block())

    def seg_cols(v):
        return slice(SEGS[v][0], SEGS[v][1])

    def unit(n):
        head, b = divmod(n, 3)
        return head, b, (3 if b else 1), slice(b * P, (b + 1) * P)

    def has(what, jm):
        lo, hi = {"hidden": (0, NB), "transpose": (-1, NB - 1), "value": (G, NB + G)}[what]
        return lo <= jm < hi

    def expert_steps(eng, step):
        for jm in range(-1, G):
            step(jm, 0)
        with eng.Fori(0, (NB - 2 * G) // (2 * G)) as i:
            for jm in range(G, 3 * G):
                step(jm, i)
        for jm in range(NB - G, NB + G):
            step(jm, 0)

    def uses(jm, i, ring):
        return (jm // ring + 1) + i * (2 * G // ring)

    def v_part(s):
        return [divmod(2 * s + k, G) for k in range(2)]

    @block.sync
    def _(sp):
        sp.dma_start(cst[:], consts).then_inc(const_ld.sem, 16)
        for tb, src in ((0, x_prompt[0]), (1, x_sample[0, 0:P]), (2, x_sample[0, P:2 * P])):
            sp.dma_start(x_nat[:, tb], src).then_inc(x_ld.sem, 16)
        sp.dma_start(c_nat[0:KC], c_ctx.rearrange("(k p) -> k p", p=P)).then_inc(const_ld.sem, 16)
        sp.dma_start(c_nat[KC:16], c[0].rearrange("(k p) -> k p", p=P)).then_inc(const_ld.sem, 16)
        with sp.Fori(0, DEPTH) as l:
            sp.wait_ge(vec_tr.sem, vec_tr.at(l, 0))
            for row, n, src in ((ROW_ADA, 48, b_ada), (ROW_G1, 8, norm1_g), (ROW_G2, 8, norm2_g),
                                (ROW_PS, 2, pool_scale)):
                sp.dma_start(vec_nat[row:row + n], src[l].rearrange("(k p) -> k p", p=P)) \
                  .then_inc(vec_ld.sem, 16)
            sp.dma_start(vec_nat[ROW_CONV:ROW_CONV + 6], conv_w[l].rearrange("w (k p) -> (w k) p", p=P)) \
              .then_inc(vec_ld.sem, 16)
            sp.dma_start(vec_nat[ROW_FG:ROW_FG + 8], final_g.rearrange("(k p) -> k p", p=P)) \
              .then_inc(vec_ld.sem, 16)
            for n in range(W_PER):
                for first, count, src in ((0, N_ADA, w_ada), (W_IN0, N_IN, w_in), (W_OUT0, N_OUT, w_out),
                                          (W_WQ0, N_WQ, peer_wq)):
                    if first <= n < first + count:
                        tile = src[l].rearrange("(k p) n -> p k n", p=P)[:, :, (n - first) * WCOLS:
                                                                         (n - first + 1) * WCOLS]
                        dst = wring[:, n % WR]
                if n >= W_SK0:
                    tile = peer_subkeys[l].rearrange("h q k d -> k (h q) d")[:, (n - W_SK0) * 8:
                                                                             (n - W_SK0 + 1) * 8]
                    dst = wring[:, n % WR].rearrange("p k n -> p (k n)")[:, 0:8 * P] \
                        .rearrange("p (s d) -> p s d", s=8)
                sp.wait_ge(w_used.sem, w_used.at(l, n + 1 - WR))
                sp.dma_start(dst, tile).then_inc(w_ld[n % WR].sem, 16)
            for tb in range(TB):
                sp.wait_ge(gq_evac.sem, gq_evac.at(l, (tb + 1) * NQ // TB))
                sp.dma_start(gate_dram[:, :, tb * P:(tb + 1) * P].rearrange("a b t -> b a t"), g_all[:]) \
                  .then_inc(g_st.sem, 16)
            sp.wait_ge(g_st.sem, g_st.at(l, 16 * TB))

            def step(jm, i):
                j = jm + 2 * G * i
                J = l * NB + j
                if has("transpose", jm):
                    slot = (jm + 1) % 4
                    sp.wait_ge(ut_mm.sem, 2 * J + 4)
                    sp.dma_start(u_raw[:, slot], peer_u[l, bass.ds((j + 1) * P, P), :]) \
                      .then_inc(u_ld[slot].sem, 16)
                if has("hidden", jm):
                    slot = jm % 4
                    sp.wait_ge(w32_rdy.sem, J + 1)
                    sp.dma_start(gate[:, slot], gate_dram[j]).then_inc(g_ld[slot].sem, 16)
                if has("value", jm + 1):
                    s = (jm + 1) % G
                    for k, (half, b) in enumerate(v_part(s)):
                        M = 2 * (J + 1 - G) + k
                        slot = half * G + b
                        sp.wait_ge(vlo_rdy.sem, M + 1)
                        sp.dma_start(v_raw[:, slot],
                                     peer_v[l, bass.ds((j + 1 - s - G + b) * P, P), half * 512:(half + 1) * 512]) \
                          .then_inc(v_ld[slot].sem, 16)

            sp.wait_ge(sc_mm.sem, sc_mm.at(l, 4 * TB))
            expert_steps(sp, step)
        for tb, dst in ((0, y_prompt[0]), (1, y_sample[0, 0:P]), (2, y_sample[0, P:2 * P])):
            sp.wait_ge(fo_evac.sem, 2 * (tb + 1))
            sp.dma_start(dst, y_nat[:, tb]).then_inc(y_st.sem, 16)
        sp.wait_ge(y_st.sem, 16 * TB)

    @block.gpsimd
    def _(pool):
        nc.gpsimd.memset(pool_blk[:], 0.0).then_inc(zero_rdy.sem, 1)
        pool.wait_ge(zero_rdy.sem, 1)
        pool.sem_inc(pool_passed.sem, 1)
        with pool.Fori(0, DEPTH) as l:
            pool.wait_ge(xa_evac.sem, xa_evac.at(l, 0))
            pool.sem_inc(pool_passed.sem, 1)
            pool.wait_ge(xi_evac.sem, 2 * TB)
            pool.sem_inc(pool_passed.sem, 1)
            nc.gpsimd.memset(bias_tab[:], 0.0)
            nc.gpsimd.memset(pool_in[:], 0.0).then_inc(pad_rdy.sem, 1)
            pool.wait_ge(pad_rdy.sem, pad_rdy.at(l, 1))
            pool.sem_inc(pool_passed.sem, 1)
            pool.dma_start(bias_tab[0:NH * DR, GRID - NCOLS:GRID - NCOLS + DC],
                           rpb[l].rearrange("h r c -> (h r) c")).then_inc(tab_ld.sem, 16)
            for g in range(4):
                half = slice((g % 2) * 64, (g % 2) * 64 + 64)
                pool.dma_start(pool_blk[half, g // 2, half], pool_w[l, g]).then_inc(poolw_ld.sem, 16)
            pool.dma_start(cK[:].rearrange("m (h d) -> m h d", h=NH), cache_k[0, l].rearrange("h m d -> m h d")) \
                .then_inc(cache_ld.sem, 16)
            pool.dma_start(cV[:].rearrange("m (h d) -> m h d", h=NH), cache_v[0, l].rearrange("h m d -> m h d")) \
                .then_inc(cache_ld.sem, 16)
            pool.wait_ge(tab_ld.sem, tab_ld.at(l, 16))
            pool.sem_inc(pool_passed.sem, 1)
            pool.dma_start(tab_dram.ap(), bias_tab[0:NH * DR, :]).then_inc(tab_st.sem, 16)
            pool.wait_ge(tab_st.sem, tab_st.at(l, 16))
            pool.sem_inc(pool_passed.sem, 1)
            for r in range(ROWS):
                for hd in range(NH):
                    src = bass.AP(tab_dram, (hd * DR + 7 - r) * TPW, [[1, GRID], [TPW, ROWS], [1, GRID]])
                    dst = bias[(r % 2) * GRID:(r % 2 + 1) * GRID, r // 2, hd].rearrange(
                        "p (a b) -> p a b", a=ROWS)
                    pool.dma_start(dst, src).then_inc(bias_ld.sem, 16)
            pool.wait_ge(bias_ld.sem, bias_ld.at(l, 16 * ROWS * NH))
            pool.sem_inc(pool_passed.sem, 1)
            nc.gpsimd.tensor_tensor(bias_v, bias_v, colmask.unsqueeze(1).to_broadcast([P, 2 * NH * ROWS, GRID]),
                                    ALU.add).then_inc(bias_rdy.sem, 1)
            pool.wait_ge(pj_evac.sem, pj_evac.at(l, 22))
            pool.sem_inc(pool_passed.sem, 1)
            pool.dma_start(new_v[0, l].rearrange("h t d -> t h d"),
                           vN[:, 0].rearrange("t (h d) -> t h d", h=NH)).then_inc(kv_st.sem, 16)
            pool.wait_ge(kc_evac.sem, kc_evac.at(l, 1))
            pool.sem_inc(pool_passed.sem, 1)
            pool.dma_start(new_k[0, l].rearrange("h t d -> t h d"),
                           k_out[:].rearrange("t (h d) -> t h d", h=NH)).then_inc(kv_st.sem, 16)
            pool.wait_ge(kv_st.sem, kv_st.at(l, 32))
            pool.sem_inc(pool_passed.sem, 1)
            pool.wait_ge(g_st.sem, g_st.at(l, 16 * TB))
            pool.sem_inc(pool_passed.sem, 1)
            nc.gpsimd.memset(acc[:], 0.0).then_inc(acc_zero.sem, 1)

    @block.tensor
    def _(pe):
        for sig in (vec_tr, w_used, gq_mm, ut_mm, h_mm, v_mm):
            pe.sem_inc(sig.sem, sig.credit)

        def sums(N):
            pe.wait_ge(sq_rdy.sem, N + 1)
            for k in range(KC):
                last = nc.tensor.matmul(ps[:, 5, 0:T], ones, h[:, k], start=(k == 0), stop=(k == KC - 1))
            last.then_inc(sum_mm.sem, 1)

        pe.wait_ge(const_ld.sem, 48)
        pe.wait_ge(x_ld.sem, 16 * TB)
        nc.tensor.transpose(ps[:, 7, 0:16], c_nat[:], ident[0:16, 0:16]).then_inc(c_tr.sem, 1)
        for n in range(2 * TB):
            tb, half = divmod(n, 2)
            for k in range(4):
                src = x_nat[:, tb, (half * 4 + k) * P:(half * 4 + k + 1) * P]
                last = nc.tensor.transpose(ps[:, n, k * P:(k + 1) * P], src, ident)
            last.then_inc(xi_mm.sem, 1)

        with pe.Fori(0, DEPTH) as l:
            pe.wait_ge(vec_ld.sem, vec_ld.at(l, 16 * 6))
            pe.wait_ge(silu_rdy.sem, 1)
            nc.tensor.transpose(ps[:, 7, 0:NROWS], vec_nat[0:NROWS], ident[0:NROWS, 0:NROWS]) \
                .then_inc(vec_tr.sem, 1)
            sums(2 * l)

            def tile_in(n):
                pe.wait_ge(w_ld[n % WR].sem, w_ld[n % WR].at(l, 16 * (n // WR + 1)))
                return wring[:, n % WR]

            for n in range(N_ADA):
                w = tile_in(n)
                for b in range(2):
                    blk = 2 * n + b
                    for k in range(KC):
                        last = nc.tensor.matmul(ps[:, 6, 2 * blk:2 * blk + 2], w[:, k, b * P:(b + 1) * P],
                                                silu_c[:, k], start=(k == 0), stop=(k == KC - 1))
                last.then_inc(w_used.sem, 1)

            def column_blocks(tiles, first, mm, evac, src):
                for n in tiles:
                    w = tile_in(n)
                    for b in range(2):
                        m = 2 * (n - first) + b
                        pe.wait_ge(evac.sem, evac.at(l, m - 1))
                        for k in range(KC):
                            last = nc.tensor.matmul(ps[:, m % 2, 0:T], w[:, k, b * P:(b + 1) * P], src[:, k],
                                                    start=(k == 0), stop=(k == KC - 1))
                        last.then_inc(mm.sem, 1)
                    pe.wait_ge(mm.sem, mm.at(l, m + 1))
                    pe.sem_inc(w_used.sem, 1)

            pe.wait_ge(h_rdy.sem, h_rdy.at(l, 1))
            column_blocks(range(W_IN0, W_IN0 + 8), W_IN0, pj_mm, pj_evac, h)
            for n in (W_IN0 + 8, W_IN0 + 9):
                w = tile_in(n)
                for tb in range(TB):
                    m = 16 + (n - W_IN0 - 8) * TB + tb
                    pe.wait_ge(pj_evac.sem, pj_evac.at(l, m - 1))
                    for k in range(KC):
                        last = nc.tensor.matmul(ps[:, m % 2, 0:WCOLS], h[:, k, tb * P:(tb + 1) * P], w[:, k],
                                                start=(k == 0), stop=(k == KC - 1))
                    last.then_inc(pj_mm.sem, 1)
                pe.wait_ge(pj_mm.sem, pj_mm.at(l, m + 1))
                pe.sem_inc(w_used.sem, 1)
            pe.wait_ge(pj_evac.sem, pj_evac.at(l, 16))
            pe.wait_ge(std_rdy.sem, std_rdy.at(l, 1))
            for k in range(4):
                last = nc.tensor.transpose(ps[:, 5, k * P:(k + 1) * P], kT[:, k, 0:P], ident)
            last.then_inc(kc_mm.sem, 1)
            pe.wait_ge(cache_ld.sem, cache_ld.at(l, 32))
            pe.wait_ge(mods_rdy.sem, mods_rdy.at(l, 1))
            for k in range(4):
                last = nc.tensor.transpose(ps[:, 6, k * P:(k + 1) * P], cK[:, k * P:(k + 1) * P], ident)
            last.then_inc(ck_mm.sem, 1)
            pe.wait_ge(poolw_ld.sem, poolw_ld.at(l, 64))
            pe.wait_ge(vec_rdy.sem, vec_rdy.at(l, 1))
            pe.wait_ge(pd_rdy.sem, pd_rdy.at(l, 1))
            for b, bank in enumerate((4, 7)):
                last = nc.tensor.matmul(ps[:, bank, 0:T], pool_blk[:, b], pool_d[:, b], start=True, stop=True)
            last.then_inc(pool_mm.sem, 1)

            pe.wait_ge(pj_evac.sem, pj_evac.at(l, 22))
            pe.wait_ge(ck_evac.sem, ck_evac.at(l, 1))
            pe.wait_ge(kc_evac.sem, kc_evac.at(l, 1))
            pe.wait_ge(branch_rdy.sem, branch_rdy.at(l, 1))

            def scores(n):
                head, b, _, q_cols = unit(n)
                rows = slice((head % 2) * HD, (head % 2 + 1) * HD)
                q = qT[rows, head // 2, q_cols]
                pe.wait_ge(exp_rdy.sem, exp_rdy.at(l, n - 1))
                if b == 0:
                    nc.tensor.matmul(ps[:, n % 2, 0:P], q, kT[rows, head // 2, 0:TCTX], start=True, stop=True) \
                        .then_inc(s_mm.sem, 1)
                else:
                    nc.tensor.matmul(ps[:, n % 2, 0:TLAT], flip, bias[:, b - 1, head], start=True, stop=False)
                    nc.tensor.matmul(ps[:, n % 2, 0:TLAT], q, kT[rows, head // 2, TCTX:T], start=False, stop=True)
                    nc.tensor.matmul(ps[:, n % 2, TLAT:KEYS], q, cKT[rows, head // 2], start=True, stop=True) \
                        .then_inc(s_mm.sem, 1)

            pe.wait_ge(bias_rdy.sem, bias_rdy.at(l, 1))
            scores(0)
            for n in range(NU + 1):
                if n + 1 < NU:
                    scores(n + 1)
                if n < NU:
                    head, b, blocks, _ = unit(n)
                    pe.wait_ge(pr_rdy.sem, pr_rdy.at(l, n + 1))
                    pe.wait_ge(t_evac.sem, t_evac.at(l, n - 1))
                    for k in range(blocks):
                        last = nc.tensor.transpose(ps[:, 2 + n % 2, k * P:(k + 1) * P],
                                                   pr[:, n % 2, k * P:(k + 1) * P], ident)
                    last.then_inc(t_mm.sem, 1)
                if n >= 1:
                    m = n - 1
                    head, b, blocks, _ = unit(m)
                    pair = slice((head // 2) * P, (head // 2 + 1) * P)
                    values = [vN[:, 0, pair]] if b == 0 else [vN[:, 1, pair], vN[:, 2, pair], cV[:, pair]]
                    pe.wait_ge(t_evac.sem, t_evac.at(l, m + 1))
                    pe.wait_ge(o_evac.sem, o_evac.at(l, m - 1))
                    for k in range(blocks):
                        last = nc.tensor.matmul(ps[:, 5 + m % 2, 0:P], values[k], prT[:, m % 2, k],
                                                start=(k == 0), stop=(k == blocks - 1))
                    last.then_inc(o_mm.sem, 1)

            pe.wait_ge(o_evac.sem, o_evac.at(l, NU))
            column_blocks(range(W_OUT0, W_OUT0 + N_OUT), W_OUT0, xo_mm, xo_evac, y)
            sums(2 * l + 1)
            pe.wait_ge(h_rdy.sem, h_rdy.at(l, 2))
            column_blocks(range(W_WQ0, W_WQ0 + N_WQ), W_WQ0, pq_mm, pq_evac, h)
            for n in range(4):
                tile = W_SK0 + n // 2
                w = tile_in(tile)[:].rearrange("p k n -> p (k n)")
                for k in range(4):
                    at_ = ((n % 2) * 4 + k) * P
                    last = nc.tensor.transpose(ps[:, (2, 3, 4, 7)[n], k * P:(k + 1) * P], w[:, at_:at_ + P], ident)
                last.then_inc(sk_mm.sem, 1)
                if n % 2:
                    pe.wait_ge(sk_mm.sem, sk_mm.at(l, n + 1))
                    pe.sem_inc(w_used.sem, 1)

            def route_scores(tb):
                for n in range(4):
                    if tb:
                        pe.wait_ge(sc_evac.sem, sc_evac.at(l, 4 * (tb - 1) + n + 1))
                    for k in range(4):
                        hp = 4 * n + k
                        last = nc.tensor.matmul(ps[:, n, k * P:(k + 1) * P], pq[:, hp, tb * P:(tb + 1) * P],
                                                skT[:, hp], start=True, stop=True)
                    last.then_inc(sc_mm.sem, 1)

            pe.wait_ge(pq_evac.sem, pq_evac.at(l, HP))
            pe.wait_ge(sk_evac.sem, sk_evac.at(l, 4))
            route_scores(0)
            for tb in range(TB):
                pe.wait_ge(pk_rdy.sem, pk_rdy.at(l, tb + 1))
                if tb:
                    pe.wait_ge(pk_evac.sem, pk_evac.at(l, tb))
                for k in range(3):
                    last = nc.tensor.transpose(ps[:, 4, k * P:(k + 1) * P], picked[:, k], ident)
                last.then_inc(pk_mm.sem, 1)
                if tb + 1 < TB:
                    route_scores(tb + 1)
                with pe.Fori(0, P // 8) as i:
                    for a in range(2):
                        Q = l * NQ + (i * 2 + (tb * (P // 4) + a))
                        pe.wait_ge(one_rdy.sem, Q + 1)
                        pe.wait_ge(gq_evac.sem, Q + 1)
                        for k in range(4):
                            last = nc.tensor.matmul(ps[:, 5 + a, k * P:(k + 1) * P], one_a[:, 4 * a + k],
                                                    one_b[:, 4 * a + k], start=True, stop=True)
                        last.then_inc(gq_mm.sem, 1)

            def step(jm, i):
                J = l * NB + (jm + 2 * G * i)
                if has("value", jm):
                    s, group = jm % G, jm // G - 1
                    E = l * (2 * NG) + 4 * i + 2 * group
                    for k, (half, b) in enumerate(v_part(s)):
                        M = 2 * (J - G) + k
                        w_at, v_at = (group % 2) * G + b, (2 * s + k) % 4
                        pe.wait_ge(vlo_rdy.sem, M + (1 + vlo_rdy.credit))
                        pe.wait_ge(wlo_rdy.sem, J - s - G + b + 1)
                        if b == 0:
                            pe.wait_ge(ac_evac.sem, E + half + 1)
                        for tb in range(TB):
                            cols = slice(tb * P, (tb + 1) * P)
                            for n, (w, v) in enumerate(((w_hi, v_lo), (w_hi, v_hi), (w_lo, v_hi))):
                                last = nc.tensor.matmul(ps[:, tb], w[:, w_at, cols], v[:, v_at],
                                                        start=(b == 0 and n == 0),
                                                        stop=(b == G - 1 and n == 2))
                        last.then_inc(v_mm.sem, 1)
                if has("transpose", jm):
                    slot = (jm + 1) % 4
                    pe.wait_ge(u_ld[slot].sem, (l * (NB // 4) + uses(jm + 1, i, 4)) * 16)
                    for hh in range(2):
                        pe.wait_ge(ulo_rdy.sem, 2 * J + (hh + 3))
                        for k in range(4):
                            last = nc.tensor.transpose(ps[:, 3 + hh, k * P:(k + 1) * P],
                                                       u_raw[:, slot, (4 * hh + k) * P:(4 * hh + k + 1) * P],
                                                       ident)
                        last.then_inc(ut_mm.sem, 1)
                if has("hidden", jm):
                    pe.wait_ge(ulo_rdy.sem, 2 * J + (2 + ulo_rdy.credit))
                    pe.wait_ge(gelu_rdy.sem, J + 1)
                    for k in range(KC):
                        for n, (u, hx) in enumerate(((u_hi, h_lo), (u_hi, h_hi), (u_lo, h_hi))):
                            last = nc.tensor.matmul(ps[:, 5 + jm % 2, 0:T], u[:, jm % 2, k], hx[:, k],
                                                    start=(k == 0 and n == 0), stop=(k == KC - 1 and n == 2))
                    last.then_inc(h_mm.sem, 1)

            pe.wait_ge(gq_evac.sem, gq_evac.at(l, NQ))
            pe.wait_ge(sc_evac.sem, sc_evac.at(l, 4 * TB))
            pe.wait_ge(pk_evac.sem, pk_evac.at(l, TB))
            pe.wait_ge(hl_rdy.sem, hl_rdy.at(l, 1))
            expert_steps(pe, step)
            for k in range(KC):
                pe.wait_ge(ac_evac.sem, ac_evac.at(l, 2 * NG))
                pe.wait_ge(xa_evac.sem, xa_evac.at(l, k - 1))
                for tb in range(TB):
                    last = nc.tensor.transpose(ps[:, k % 2, tb * P:(tb + 1) * P], acc[:, tb, k * P:(k + 1) * P],
                                               ident)
                last.then_inc(xa_mm.sem, 1)

        sums(2 * DEPTH)
        pe.wait_ge(h_rdy.sem, 2 * DEPTH + 1)
        for n in range(2 * TB):
            tb, half = divmod(n, 2)
            bank = (0, 1, 2, 3, 4, 6)[n]
            for k in range(4):
                last = nc.tensor.transpose(ps[:, bank, k * P:(k + 1) * P], h[:, half * 4 + k, tb * P:(tb + 1) * P],
                                           ident)
            last.then_inc(fo_mm.sem, 1)

    @block.scalar
    def _(act):
        for sig in (pj_evac, exp_rdy, t_evac, o_evac, pq_evac, gq_evac, gelu_rdy):
            act.sem_inc(sig.sem, sig.credit)

        def norm(N, l, which):
            nc.scalar.activation(h[:], x[:], ACT.Square).then_inc(sq_rdy.sem, 1)
            act.wait_ge(var_rdy.sem, N + 1)
            nc.scalar.activation(norm_t[:, 1], norm_t[:, 0], ACT.Sqrt).then_inc(std_rdy.sem, 1)
            act.wait_ge(xn_rdy.sem, N + 1)
            if which is None:
                for k in range(KC):
                    last = nc.scalar.activation(h[:, k], h[:, k], ACT.Copy, scale=vecs[:, ROW_FG + k:ROW_FG + k + 1])
            else:
                act.wait_ge(mods_rdy.sem, mods_rdy.at(l, 1))
                shift = (SH1, SH2)[which]
                for k in range(KC):
                    for v in range(2):
                        last = nc.scalar.activation(h[:, k, seg_cols(v)], h[:, k, seg_cols(v)], ACT.Identity,
                                                    scale=gs[:, which, k, v:v + 1],
                                                    bias=mods[:, shift + k, v:v + 1])
            last.then_inc(h_rdy.sem, 1)

        for n in range(2 * TB):
            tb, half = divmod(n, 2)
            act.wait_ge(xi_mm.sem, n + 1)
            nc.scalar.copy(x[:, half * 4:half * 4 + 4, tb * P:(tb + 1) * P],
                           ps[:, n].rearrange("p (k t) -> p k t", t=P)).then_inc(xi_evac.sem, 1)
        act.wait_ge(c_tr.sem, 1)
        nc.scalar.activation(silu_c[:], ps[:, 7, 0:16].rearrange("p (v k) -> p k v", v=2), ACT.Silu) \
            .then_inc(silu_rdy.sem, 1)

        with act.Fori(0, DEPTH) as l:
            act.wait_ge(vec_tr.sem, vec_tr.at(l, 1))
            nc.scalar.copy(vecs[:], ps[:, 7, 0:NROWS]).then_inc(vec_rdy.sem, 1)
            act.wait_ge(xi_evac.sem, 2 * TB)
            act.wait_ge(xa_evac.sem, xa_evac.at(l, 0))
            norm(2 * l, l, 0)
            for m in range(22):
                act.wait_ge(pj_mm.sem, pj_mm.at(l, m + 1))
                src = ps[:, m % 2, 0:T]
                if m < 6:
                    last = nc.scalar.copy(branch[:, m], src)
                elif m < 8:
                    if m == 6:
                        act.wait_ge(pad_rdy.sem, pad_rdy.at(l, 1))
                    for v in range(2):
                        w = SEGS[v][1] - SEGS[v][0]
                        last = nc.scalar.copy(pool_in[:, m - 6, SEG_AT[v]:SEG_AT[v] + w], src[:, seg_cols(v)])
                elif m < 12:
                    last = nc.scalar.activation(qT[:, m - 8], src, ACT.Copy, scale=SCALE)
                elif m < 16:
                    last = nc.scalar.copy(kT[:, m - 12], src)
                else:
                    n, tb = divmod(m - 16, TB)
                    last = nc.scalar.copy(vN[:, tb, n * WCOLS:(n + 1) * WCOLS], ps[:, m % 2, 0:WCOLS])
                last.then_inc(pj_evac.sem, 1)
            act.wait_ge(kc_mm.sem, kc_mm.at(l, 1))
            nc.scalar.copy(k_out[:], ps[:, 5]).then_inc(kc_evac.sem, 1)
            act.wait_ge(ck_mm.sem, ck_mm.at(l, 1))
            nc.scalar.copy(cKT[:].rearrange("p k m -> p (k m)"), ps[:, 6]).then_inc(ck_evac.sem, 1)
            for n in range(NU + 2):
                if n < NU:
                    keys = P if unit(n)[1] == 0 else KEYS
                    act.wait_ge(nmax_rdy.sem, nmax_rdy.at(l, n + 1))
                    nc.scalar.activation(pr[:, n % 2, 0:keys], ps[:, n % 2, 0:keys], ACT.Exp,
                                         bias=stat[:, n % 2, 1:2], accum_out=stat[:, n % 2, 2:3]) \
                        .then_inc(exp_rdy.sem, 1)
                if 1 <= n <= NU:
                    m = n - 1
                    cols = unit(m)[2] * P
                    act.wait_ge(t_mm.sem, t_mm.at(l, m + 1))
                    if m >= 2:
                        act.wait_ge(o_mm.sem, o_mm.at(l, m - 1))
                    nc.scalar.copy(prT[:, m % 2].rearrange("p k q -> p (k q)")[:, 0:cols],
                                   ps[:, 2 + m % 2, 0:cols]).then_inc(t_evac.sem, 1)
                if n >= 2:
                    m = n - 2
                    head, _, _, q_cols = unit(m)
                    rows = slice((head % 2) * HD, (head % 2 + 1) * HD)
                    act.wait_ge(o_mm.sem, o_mm.at(l, m + 1))
                    nc.scalar.copy(y[rows, 4 + head // 2, q_cols], ps[rows, 5 + m % 2, 0:P]) \
                        .then_inc(o_evac.sem, 1)
            act.wait_ge(xo_evac.sem, xo_evac.at(l, KC))
            norm(2 * l + 1, l, 1)
            act.wait_ge(kv_st.sem, kv_st.at(l, 32))
            for m in range(HP):
                act.wait_ge(pq_mm.sem, pq_mm.at(l, m + 1))
                nc.scalar.copy(pq[:, m], ps[:, m % 2, 0:T]).then_inc(pq_evac.sem, 1)
            for n in range(4):
                act.wait_ge(sk_mm.sem, sk_mm.at(l, n + 1))
                nc.scalar.copy(skT[:, 4 * n:4 * n + 4].rearrange("p s k -> p (s k)"), ps[:, (2, 3, 4, 7)[n]]) \
                    .then_inc(sk_evac.sem, 1)

            def scores_out(tb):
                act.wait_ge(s_free.sem, s_free.at(l, tb))
                for n in range(4):
                    act.wait_ge(sc_mm.sem, sc_mm.at(l, 4 * tb + n + 1))
                    nc.scalar.copy(s_sb[:, 4 * n:4 * n + 4].rearrange("p s k -> p (s k)"), ps[:, n]) \
                        .then_inc(sc_evac.sem, 1)

            scores_out(0)
            for tb in range(TB):
                act.wait_ge(gexp_in.sem, gexp_in.at(l, tb + 1))
                nc.scalar.activation(picked[:, 2], picked[:, 2], ACT.Exp).then_inc(gexp_rdy.sem, 1)
                act.wait_ge(pk_mm.sem, pk_mm.at(l, tb + 1))
                nc.scalar.copy(pickT[:, :, tb * P:(tb + 1) * P], ps[:, 4, 0:3 * P].rearrange("p (k t) -> p k t", k=3)) \
                    .then_inc(pk_evac.sem, 1)
                if tb + 1 < TB:
                    scores_out(tb + 1)
                if tb:
                    act.wait_ge(g_st.sem, g_st.at(l, 16 * tb))
                with act.Fori(0, P // 8) as i:
                    for a in range(2):
                        Q = l * NQ + (i * 2 + (tb * (P // 4) + a))
                        act.wait_ge(gq_mm.sem, Q + (1 + gq_mm.credit))
                        nc.scalar.copy(g_all[:, :, bass.ds(i * 8 + 4 * a, 4)],
                                       ps[:, 5 + a].rearrange("p (t i) -> p i t", t=4)).then_inc(gq_evac.sem, 1)
            act.wait_ge(g_st.sem, g_st.at(l, 16 * TB))
            nc.scalar.copy(h_hi[:], h[:]).then_inc(hh_rdy.sem, 1)

            def step(jm, i):
                J = l * NB + (jm + 2 * G * i)
                if has("hidden", jm - 1):
                    p = (jm - 1) % 2
                    act.wait_ge(h_mm.sem, J + h_mm.credit)
                    act.wait_ge(w32_rdy.sem, J + (w32_rdy.credit - 2))
                    nc.scalar.activation(act_h[:, p], ps[:, 5 + p, 0:T], ACT.Gelu_apprx_tanh) \
                        .then_inc(gelu_rdy.sem, 1)
                if has("value", jm + 1):
                    s = (jm + 1) % G
                    for k, (half, b) in enumerate(v_part(s)):
                        M = 2 * (J + 1 - G) + k
                        laps = (2 * (jm + 1 - G) + k) // (2 * G) + 1 + 2 * i
                        slot = half * G + b
                        act.wait_ge(v_ld[slot].sem, (l * (NV // (2 * G)) + laps) * 16)
                        act.wait_ge(v_mm.sem, M + 1)
                        nc.scalar.copy(v_hi[:, slot % 4], v_raw[:, slot]).then_inc(vhi_rdy.sem, 1)
                if has("hidden", jm - 1):
                    act.wait_ge(w32_rdy.sem, J + w32_rdy.credit)
                    nc.scalar.copy(w_hi[:, (jm - 1) % (2 * G)], w32[:, p]).then_inc(whi_rdy.sem, 1)
                if has("transpose", jm):
                    for hh in range(2):
                        act.wait_ge(ut_mm.sem, 2 * J + (hh + 3 + ut_mm.credit))
                        act.wait_ge(h_mm.sem, J + h_mm.credit)
                        nc.scalar.copy(u_hi[:, (jm + 1) % 2, 4 * hh:4 * hh + 4],
                                       ps[:, 3 + hh].rearrange("p (k e) -> p k e", e=P)).then_inc(uhi_rdy.sem, 1)

            expert_steps(act, step)

        act.wait_ge(xa_evac.sem, xa_evac.at(DEPTH, 0))
        norm(2 * DEPTH, None, None)
        for n in range(2 * TB):
            tb, half = divmod(n, 2)
            bank = (0, 1, 2, 3, 4, 6)[n]
            act.wait_ge(fo_mm.sem, n + 1)
            nc.scalar.copy(y_nat[:, tb, half * 512:(half + 1) * 512], ps[:, bank]).then_inc(fo_evac.sem, 1)

    @block.vector
    def _(dve):
        for sig in (xo_evac, s_free, ulo_rdy, w32_rdy, vlo_rdy, ac_evac, xa_evac):
            dve.sem_inc(sig.sem, sig.credit)
        V = nc.vector

        def norm(N):
            ch = Chain(dve, norm_ch, N * 5, 5)
            var, std, r = norm_t[:, 0], norm_t[:, 1], norm_t[:, 2]
            dve.wait_ge(sum_mm.sem, N + 1)
            V.tensor_scalar(var, ps[:, 5, 0:T], 1.0 / D, EPS, ALU.mult, ALU.add).then_inc(var_rdy.sem, 1)
            dve.wait_ge(std_rdy.sem, N + 1)
            ch.then(V.reciprocal(r, std))
            ch.then(V.tensor_tensor(std, r, r, ALU.mult))
            ch.then(V.tensor_tensor(std, std, var, ALU.mult))
            ch.then(V.tensor_scalar(std, std, -0.5, 1.5, ALU.mult, ALU.add))
            ch.then(V.tensor_tensor(r, r, std, ALU.mult))
            ch.close()
            V.tensor_tensor(h[:], x[:], r.unsqueeze(1).to_broadcast([P, KC, T]), ALU.mult).then_inc(xn_rdy.sem, 1)

        def add_gated(gate_row, bank, k, evac):
            for v in range(2):
                last = V.scalar_tensor_tensor(x[:, k, seg_cols(v)], ps[:, bank, seg_cols(v)],
                                              mods[:, gate_row + k, v:v + 1], x[:, k, seg_cols(v)],
                                              ALU.mult, ALU.add)
            last.then_inc(evac.sem, 1)

        with dve.Fori(0, DEPTH) as l:
            norm(2 * l)
            dve.wait_ge(w_used.sem, w_used.at(l, N_ADA))
            dve.wait_ge(vec_rdy.sem, vec_rdy.at(l, 1))
            ch = Chain(dve, mods_ch, mods_ch.at(l, 0), 1)
            ch.then(V.tensor_tensor(mods[:], ps[:, 6, 0:12 * KC].rearrange("p (j v) -> p j v", v=2),
                                    vecs[:, 0:48].unsqueeze(2).to_broadcast([P, 48, 2]), ALU.add))
            ch.close()
            for which, (part_, row) in enumerate(((SC1, ROW_G1), (SC2, ROW_G2))):
                last = V.scalar_tensor_tensor(gs[:, which], mods[:, part_:part_ + KC], 1.0,
                                              vecs[:, row:row + KC].unsqueeze(2).to_broadcast([P, KC, 2]),
                                              ALU.add, ALU.mult)
            last.then_inc(mods_rdy.sem, 1)

            dve.wait_ge(pj_evac.sem, pj_evac.at(l, 6))
            ch = Chain(dve, conv_ch, conv_ch.at(l, 0), 4)
            ch.then(V.tensor_tensor(conv_u[:], branch[:, 4:6], branch[:, 0:2], ALU.mult))

            def tap(w, b):
                return vecs[:, ROW_CONV + 2 * w + b:ROW_CONV + 2 * w + b + 1]

            for b in range(2):
                last = V.tensor_scalar(y[:, b], conv_u[:, b], tap(1, b), None, ALU.mult)
            ch.then(last)
            for w, to, of in ((0, 1, 0), (2, 0, 1)):
                for b in range(2):
                    for lo, hi in SEGS:
                        n = hi - lo - 1
                        out = y[:, b, lo + to:lo + to + n]
                        last = V.scalar_tensor_tensor(out, conv_u[:, b, lo + of:lo + of + n], tap(w, b), out,
                                                      ALU.mult, ALU.add)
                ch.then(last)
            ch.close()
            V.tensor_tensor(y[:, 0:2], y[:, 0:2], branch[:, 2:4], ALU.mult)

            dve.wait_ge(pj_evac.sem, pj_evac.at(l, 8))
            ch = Chain(dve, pool_ch, pool_ch.at(l, 0), 6)
            ch.then(V.tensor_tensor(pool_s[:, :, 1:PW], pool_in[:, :, 0:PW - 1], pool_in[:, :, 1:PW], ALU.add))
            ch.then(V.tensor_tensor(pool_r[:, :, 2:PW - 1], pool_s[:, :, 1:PW - 2], pool_s[:, :, 3:PW], ALU.add))
            ch.then(V.tensor_tensor(pool_s[:, 1, 4:PW - 3], pool_r[:, 1, 2:PW - 5], pool_r[:, 1, 6:PW - 1], ALU.add))
            ch.then(V.tensor_tensor(pool_r[64:P, 1, 8:PW - 7], pool_s[64:P, 1, 4:PW - 11], pool_s[64:P, 1, 12:PW - 3],
                                    ALU.add))
            ch.then(V.tensor_copy(pool_s[64:P, :, PAD:PW - PAD], pool_r[64:P, :, PAD:PW - PAD]))
            for v, (lo, hi) in enumerate(SEGS):
                cols = slice(SEG_AT[v], SEG_AT[v] + hi - lo)
                last = V.tensor_tensor(pool_d[:, :, lo:hi], pool_s[:, :, cols], rcnt[:, :, lo:hi], ALU.mult)
            ch.then(last)
            ch.close()
            for v, (lo, hi) in enumerate(SEGS):
                cols = slice(SEG_AT[v], SEG_AT[v] + hi - lo)
                last = V.tensor_tensor(pool_d[:, :, lo:hi], pool_d[:, :, lo:hi], pool_in[:, :, cols], ALU.subtract)
            last.then_inc(pd_rdy.sem, 1)
            dve.wait_ge(pool_mm.sem, pool_mm.at(l, 1))
            for b, bank in enumerate((4, 7)):
                last = V.tensor_scalar(y[:, 2 + b], ps[:, bank, 0:T], vecs[:, ROW_PS + b:ROW_PS + b + 1], None,
                                       ALU.mult)
            last.then_inc(branch_rdy.sem, 1)

            ch = Chain(dve, att_ch, att_ch.at(l, 0), 2 * NU)
            for n in range(NU + 1):
                if n < NU:
                    head, b, _, _ = unit(n)
                    keys = P if b == 0 else KEYS
                    dve.wait_ge(s_mm.sem, s_mm.at(l, n + 1))
                    ch.then(V.reduce_max(stat[:, n % 2, 0:1], ps[:, n % 2, 0:keys], AX.X))
                    V.tensor_scalar(stat[:, n % 2, 1:2], stat[:, n % 2, 0:1], -1.0, None, ALU.mult) \
                        .then_inc(nmax_rdy.sem, 1)
                if n >= 1:
                    m = n - 1
                    keys = P if unit(m)[1] == 0 else KEYS
                    dve.wait_ge(exp_rdy.sem, exp_rdy.at(l, m + 1))
                    ch.then(V.reciprocal(stat[:, m % 2, 3:4], stat[:, m % 2, 2:3]))
                    V.tensor_scalar(pr[:, m % 2, 0:keys], pr[:, m % 2, 0:keys], stat[:, m % 2, 3:4], None,
                                    ALU.mult).then_inc(pr_rdy.sem, 1)
            ch.close()
            for k in range(KC):
                dve.wait_ge(xo_mm.sem, xo_mm.at(l, k + 1))
                add_gated(GT1, k % 2, k, xo_evac)
            norm(2 * l + 1)

            with dve.Fori(0, TB) as tb:
                B = l * TB + tb
                ch = Chain(dve, route_ch, B * ROUTE_STEPS, ROUTE_STEPS)
                dve.wait_ge(sc_evac.sem, B * 4 + 4)
                dve.sem_inc(dve_passed.sem, 1)
                for n in range(HP):
                    last = V.max(top_s[:, n, 0:8], s_sb[:, n])
                ch.then(last, dve_passed)
                for n in range(HP):
                    last = V.match_replace(left[:, n], top_s[:, n, 0:8], s_sb[:, n], NEG)
                ch.then(last, dve_passed)
                for n in range(HP):
                    V.max_index(top_iu[:, n, 0:8], top_s[:, n, 0:8], s_sb[:, n])
                for n in range(HP):
                    last = V.max(top_s[:, n, 8:16], left[:, n])
                last.then_inc(s_free.sem, 1)
                dve.wait_ge(s_free.sem, B + 2)
                dve.sem_inc(dve_passed.sem, 1)
                for n in range(HP):
                    last = V.max_index(top_iu[:, n, 8:16], top_s[:, n, 8:16], left[:, n])
                tops = top_s[:].rearrange("p (h q) k -> p h q k", q=2)
                ch.then(V.tensor_tensor(cand[:], tops[:, :, 0].unsqueeze(3).to_broadcast([P, PH, TOPK, TOPK]),
                                        tops[:, :, 1].unsqueeze(2).to_broadcast([P, PH, TOPK, TOPK]), ALU.add))
                V.tensor_copy(top_i[:], top_iu[:])
                cands = cand[:].rearrange("p h a b -> p h (a b)")
                lefts = left[:].rearrange("p (h q) k -> p h (q k)", q=2)
                for n in range(PH):
                    last = V.max(best[:, n, 0:8], cands[:, n])
                ch.then(last, dve_passed)
                for n in range(PH):
                    last = V.match_replace(lefts[:, n], best[:, n, 0:8], cands[:, n], NEG)
                ch.then(last, dve_passed)
                for n in range(PH):
                    V.max_index(best_iu[:, n, 0:8], best[:, n, 0:8], cands[:, n])
                for n in range(PH):
                    last = V.max(best[:, n, 8:16], lefts[:, n])
                ch.then(last, dve_passed)
                gates = picked[:, 2].rearrange("p (h k) -> p h k", k=TOPK)
                V.tensor_tensor(gates, best[:], best[:, :, 0:1].to_broadcast([P, PH, TOPK]), ALU.subtract) \
                    .then_inc(gexp_in.sem, 1)
                for n in range(PH):
                    last = V.max_index(best_iu[:, n, 8:16], best[:, n, 8:16], lefts[:, n])
                ch.then(last, dve_passed)
                V.tensor_scalar(part_u[:, 0], best_iu[:], 4, None, ALU.logical_shift_right)
                ch.then(V.tensor_scalar(part_u[:, 1], best_iu[:], TOPK - 1, None, ALU.bitwise_and))
                ch.then(V.tensor_copy(part[:], part_u[:]))
                left4 = left[:].rearrange("p (h q) (a b) -> p h (q a) b", q=2, b=TOPK)
                keys_i = top_i[:].rearrange("p (h q) k -> p h q k", q=2)
                picks = (cand[:], left4)
                for q in range(2):
                    last = V.tensor_tensor(picks[q].rearrange("p h a b -> p (h a) b"),
                                           part[:, q].rearrange("p h k -> p (h k)").unsqueeze(2)
                                           .to_broadcast([P, PH * TOPK, TOPK]),
                                           iota[:, 0:TOPK].unsqueeze(1).to_broadcast([P, PH * TOPK, TOPK]),
                                           ALU.is_equal)
                ch.then(last)
                for q in range(2):
                    last = V.tensor_tensor(picks[q], picks[q],
                                           keys_i[:, :, q].unsqueeze(2).to_broadcast([P, PH, TOPK, TOPK]), ALU.mult)
                ch.then(last)
                dve.wait_ge(gexp_rdy.sem, B + 1)
                ch.then(V.reduce_sum(gsum[:, 0], gates, AX.X))
                ch.then(V.reciprocal(gsum[:, 1], gsum[:, 0]))
                ch.close()
                V.tensor_tensor(gates, gates, gsum[:, 1].unsqueeze(2).to_broadcast([P, PH, TOPK]), ALU.mult)
                for q in range(2):
                    last = V.reduce_sum(picked[:, q], picks[q].rearrange("p h a b -> p (h a) b"), AX.X)
                last.then_inc(pk_rdy.sem, 1)

                dve.wait_ge(pk_evac.sem, B + 1)
                dve.sem_inc(dve_passed.sem, 1)
                with dve.Fori(0, P // 8) as i:
                    for a in range(2):
                        Q = B * (P // 4) + (i * 2 + a)
                        dve.wait_ge(gq_mm.sem, Q + 1)
                        for k in range(4):
                            t = tb * P + (i * 8 + (4 * a + k))
                            V.tensor_scalar(one_a[:, 4 * a + k], iota, pickT[:, 1, bass.ds(t, 1)], None,
                                            ALU.is_equal)
                            last = V.tensor_scalar(one_b[:, 4 * a + k], iota, pickT[:, 0, bass.ds(t, 1)],
                                                   pickT[:, 2, bass.ds(t, 1)], ALU.is_equal, ALU.mult)
                        last.then_inc(one_rdy.sem, 1)
            dve.wait_ge(hh_rdy.sem, hh_rdy.at(l, 1))
            V.tensor_tensor(h_lo[:], h[:], h_hi[:].bitcast(F32), ALU.subtract).then_inc(hl_rdy.sem, 1)
            dve.wait_ge(acc_zero.sem, acc_zero.at(l, 1))

            def step(jm, i):
                J = l * NB + (jm + 2 * G * i)
                if has("hidden", jm - 1):
                    p, slot = (jm - 1) % 2, (jm - 1) % 4
                    dve.wait_ge(gelu_rdy.sem, J + gelu_rdy.credit)
                    dve.wait_ge(g_ld[slot].sem, (l * (NB // 4) + uses(jm - 1, i, 4)) * 16)
                    V.tensor_tensor(w32[:, p], act_h[:, p], gate[:, slot], ALU.mult).then_inc(w32_rdy.sem, 1)
                if has("value", jm + 1):
                    for k in range(2):
                        slot = (2 * (jm + 1 - G) + k) % (2 * G)
                        M = 2 * (J + 1 - G) + k
                        dve.wait_ge(vhi_rdy.sem, M + 1)
                        V.tensor_tensor(v_lo[:, slot % 4], v_raw[:, slot], v_hi[:, slot % 4].bitcast(F32),
                                        ALU.subtract).then_inc(vlo_rdy.sem, 1)
                if has("hidden", jm - 1):
                    at_ = (jm - 1) % (2 * G)
                    dve.wait_ge(whi_rdy.sem, J)
                    V.tensor_tensor(w_lo[:, at_], w32[:, p], w_hi[:, at_].bitcast(F32), ALU.subtract) \
                        .then_inc(wlo_rdy.sem, 1)
                if has("value", jm) and (jm % G) % (G // 2) == G // 2 - 1:
                    half = (jm % G) // (G // 2)
                    E = l * (2 * NG) + 4 * i + (2 * (jm // G - 1) + half)
                    dve.wait_ge(v_mm.sem, 2 * (J - G) + (2 + v_mm.credit))
                    dve.wait_ge(ac_evac.sem, E + 1)
                    for tb in range(TB):
                        cols = slice(half * 512, (half + 1) * 512)
                        last = V.tensor_tensor(acc[:, tb, cols], acc[:, tb, cols], ps[:, tb], ALU.add)
                    last.then_inc(ac_evac.sem, 1)
                if has("transpose", jm):
                    for hh in range(2):
                        dve.wait_ge(uhi_rdy.sem, 2 * J + (hh + 3))
                        part_ = slice(4 * hh, 4 * hh + 4)
                        V.tensor_tensor(u_lo[:, (jm + 1) % 2, part_],
                                        ps[:, 3 + hh].rearrange("p (k e) -> p k e", e=P),
                                        u_hi[:, (jm + 1) % 2, part_].bitcast(F32), ALU.subtract) \
                            .then_inc(ulo_rdy.sem, 1)

            expert_steps(dve, step)
            for k in range(KC):
                dve.wait_ge(xa_mm.sem, xa_mm.at(l, k + 1))
                add_gated(GT2, k % 2, k, xa_evac)
        norm(2 * DEPTH)

    ctx.close()


def constants():
    out = np.zeros((P, NCONST), np.float32)
    out[:, C_ID:C_ID + P] = np.eye(P)
    m = np.arange(P)
    out[m // GRID * GRID + GRID - 1 - m % GRID, C_FLIP + m] = 1.0
    out[:, C_ONE:C_ONE + P] = 1.0
    out[:, C_IOTA:C_IOTA + P] = np.arange(P)
    q = GRID - 1 - np.arange(P)[:, None] % GRID
    k = np.arange(GRID)[None, :]
    start = np.clip(q - NCOLS // 2, 0, GRID - NCOLS)
    out[:, C_MASK:C_MASK + GRID] = np.where((k >= start) & (k < start + NCOLS), 0.0, -1e30)
    for b in range(2):
        for half in range(2):
            w = 2 ** (2 * b + half + 1)
            for lo, hi in SEGS:
                t, n = np.arange(hi - lo), hi - lo
                count = np.clip(t + w - 1 - w // 2, 0, n - 1) - np.clip(t - w // 2, 0, n - 1) + 1
                out[64 * half:64 * half + 64, C_RCNT + b * T + lo:C_RCNT + b * T + hi] = 1.0 / count
    return out


INS = ["x_prompt", "x_sample", "c", "cache_k", "cache_v", "c_ctx", "norm1_g", "norm2_g", "w_ada", "b_ada",
       "w_in", "conv_w", "pool_w", "pool_scale", "rpb", "w_out", "peer_wq", "peer_subkeys", "peer_u",
       "peer_v", "final_g"]
OUTS = [(1, TCTX, D), (1, TLAT, D), (1, DEPTH, NH, TCTX, HD), (1, DEPTH, NH, TCTX, HD)]


def kernel(**inputs):
    import numpy as _np
    import concourse.bacc as _bacc
    from concourse import mybir as _mybir
    from concourse.bass_utils import run_bass_kernel_spmd as _run

    nc = _bacc.Bacc("TRN2", target_bir_lowering=False, num_devices=1)
    arrays, args = {}, []
    for name in INS + ["consts"]:
        a = _np.ascontiguousarray(constants() if name == "consts" else inputs[name])
        arrays[f"in_{name}_dram"] = a
        args.append(nc.dram_tensor(f"in_{name}_dram", a.shape, _mybir.dt.from_np(a.dtype), kind="ExternalInput").ap())
    for i, shape in enumerate(OUTS):
        args.append(nc.dram_tensor(f"out_{i}_dram", shape, F32, kind="ExternalOutput").ap())
    build(nc, *args)
    r = _run(nc, [arrays], core_ids=[0])
    return tuple(r.results[0][f"out_{i}_dram"] for i in range(len(OUTS)))
```

```python
from contextlib import ExitStack

import numpy as np

import concourse.bass as bass
from concourse import mybir

F32 = mybir.dt.float32
F32R = mybir.dt.float32r
U32 = mybir.dt.uint32
BF16 = mybir.dt.bfloat16
ALU = mybir.AluOpType
ACT = mybir.ActivationFunctionType
AX = mybir.AxisListType

P = 128
D = 1024
KC = D // P
DEPTH = 2
TCTX, TLAT = 128, 256
T = TCTX + TLAT
TB = T // P
SEGS = ((0, TCTX), (TCTX, T))
EPS = 1e-6
WCOLS = 256
AW = D // 4
CW = D // 2
NH, HD = 8, 64
SCALE = HD ** -0.5
GRID = 64
ROWS = TLAT // GRID
NCOLS = 16
DR, DC = 15, 31
TPW = 2 * GRID - 1
KEYS = TLAT + 128
PAD = 8
PW = T + 4 * PAD
SEG_AT = (PAD, TCTX + 3 * PAD)
PH, TOPK, NK = 8, 16, 128
HP = 2 * PH
NB = NK
G = 4
NG = NB // G
NEG = -3.0e38

ROW_ADA, ROW_G1, ROW_G2, ROW_PS, ROW_CONV, ROW_FG, NROWS = 0, 48, 56, 64, 66, 72, 80
SH1, SC1, GT1, SH2, SC2, GT2 = (KC * i for i in range(6))
C_ID, C_ONE, C_IOTA, C_FLIP, C_MASK, C_RCNT = 0, 128, 256, 384, 512, 576
NCONST = C_RCNT + 2 * T
N_ADA, N_IN, N_OUT, N_WQ = 24, 10, 4, 8
W_IN0 = N_ADA
W_OUT0 = W_IN0 + N_IN
W_WQ0 = W_OUT0 + N_OUT
W_SK0 = W_WQ0 + N_WQ
W_PER = W_SK0 + 2
WR = 4
U_PER = NB // 2
V_PER = 2 * NG
assert W_PER % WR == 0 and U_PER % WR == 0 and V_PER % WR == 0
FILLS = (W_PER + U_PER + V_PER) // WR
TOPK_STEPS, GATE_STEPS = 16, 16
EXP_STEP = 11
ROUTE_STEPS = 15
BASE = 16512


class Signal:

    def __init__(self, nc, ctx, name, per, credit=0):
        self.sem = ctx.enter_context(nc.semaphore(name))
        self.per, self.credit = per, credit

    def at(self, l, k):
        return l * self.per + (self.credit + k)


class Chain:

    def __init__(self, eng, sig, base, per):
        self.eng, self.sem, self.base, self.per, self.n = eng, sig.sem, base, per, 0

    def then(self, ins, passed=None):
        self.n += 1
        ins.then_inc(self.sem, 1)
        self.eng.wait_ge(self.sem, self.base + self.n)
        if passed is not None:
            self.eng.sem_inc(passed.sem, 1)

    def close(self):
        assert self.n == self.per, (self.n, self.per)


def build(nc, x_prompt, x_sample, c, cache_k, cache_v, c_ctx, norm1_g, norm2_g, w_ada, b_ada, w_in, conv_w,
          pool_w, pool_scale, rpb, w_out, peer_wq, peer_subkeys, peer_u, peer_v, final_g, consts,
          y_prompt, y_sample, new_k, new_v):
    ctx = ExitStack()
    place = [BASE]

    def at(name, shape, dtype=F32, offset=None):
        size = (2 if dtype == BF16 else 4) * int(np.prod(shape[1:]))
        if offset is None:
            offset = place[0]
            place[0] += -(-size // 32) * 32
        assert offset + size <= nc.sbuf_usable_end, (name, offset + size)
        return nc.alloc_sbuf_tensor_at(name, list(shape), dtype, offset=offset)

    cst = at("cst", [P, C_FLIP])
    x = at("x", [P, KC, T])
    h = at("h", [P, KC, T])
    wring = at("wring", [P, WR, KC, WCOLS])
    vec_nat = at("vec_nat", [P, P])
    vecs = at("vecs", [P, NROWS])
    silu_c = at("silu_c", [P, KC, 2])
    mods = at("mods", [P, 6 * KC, 2])
    gs = at("gs", [P, 2, KC, 2])
    pool_blk = at("pool_blk", [P, 2, P])
    stat = at("stat", [P, 2, 4])
    iota4 = at("iota4", [P, P, 4], BF16)
    arena = place[0]

    x_nat = at("x_nat", [P, TB, D], offset=arena)
    branch = at("branch", [P, 6, T])
    pool_in = at("pool_in", [P, 2, PW])
    pool_s = at("pool_s", [P, 2, PW])
    pool_r = at("pool_r", [P, 2, PW])
    pool_d = at("pool_d", [P, 2, T])
    conv_u = at("conv_u", [P, 2, T])
    qT = at("qT", [P, 4, T])
    kT = at("kT", [P, 4, T])
    vN = at("vN", [P, TB, CW])
    y = at("y", [P, KC, T])
    k_out = at("k_out", [P, CW])
    cK = at("cK", [P, CW])
    cV = at("cV", [P, CW])
    cKT = at("cKT", [P, 4, P])
    bias_tab = at("bias_tab", [P, TPW])
    bias = at("bias", [P, 2, NH, TLAT])
    norm_t = at("norm_t", [P, 3, T])
    pr = at("pr", [P, 2, KEYS])
    prT = at("prT", [P, 2, 3, P])
    c_nat = at("c_nat", [16, P])
    mix_cst = at("mix_cst", [P, NCONST - C_FLIP])

    place[0] = arena
    h_hi = at("h_hi", [P, KC, T], F32R)
    h_lo = at("h_lo", [P, KC, T], F32R)
    u_hi = at("u_hi", [P, 2, KC, P], F32R)
    u_lo = at("u_lo", [P, 2, KC, P], F32R)
    act_h = at("act_h", [P, 2, T])
    s_sb = at("s_sb", [P, HP, NK])
    s_all = at("s_all", [P, TB - 1, HP, NK])
    top_s = at("top_s", [P, HP, TOPK])
    top_iu = at("top_iu", [P, HP, TOPK], U32)

    best = at("best", [P, PH, TOPK])
    best_iu = at("best_iu", [P, PH, TOPK], U32)
    part = at("part", [P, 2, PH, TOPK])
    picked = at("picked", [P, 3, PH * TOPK])
    gsum = at("gsum", [P, 2, PH])
    one_a = at("one_a", [P, 2, P, 4], BF16)
    one_e = at("one_e", [P, 2, P, 4], BF16)
    one_b = at("one_b", [P, 2, 3, P, 4], BF16)
    g_all = at("g_all", [P, NK, P])
    pq = at("pq", [P, HP, T], offset=place[0] - 4 * NK * P)
    skT = at("skT", [P, HP, NK], offset=place[0] - 4 * NK * P + 4 * HP * T)
    h_at = BASE + 4 * C_FLIP + 4 * KC * T
    left = at("left", [P, HP, NK], offset=h_at)
    pickT = at("pickT", [P, 5, P], BF16, offset=h_at + 4 * HP * NK)
    gres = at("gres", [P, 2, P], offset=h_at + 4 * HP * NK + 10 * P)
    top_i = at("top_i", [P, HP, TOPK], offset=h_at + 4 * HP * NK + 18 * P)

    place[0] = arena
    v_hi = at("v_hi", [P, 4, 512], F32R)
    v_lo = at("v_lo", [P, 4, 512], F32R)
    w_hi = at("w_hi", [P, 2 * G, T], F32R)
    w_lo = at("w_lo", [P, 2 * G, T], F32R)
    gate2 = at("gate2", [P, 2, G, T])
    act2 = at("act2", [P, 2, G, T])
    w32 = at("w32", [P, 2, T])
    acc = at("acc", [P, TB, D])
    y_nat = at("y_nat", [P, TB, D], offset=arena)

    ps = ctx.enter_context(nc.psum_tensor([P, 8, 512], F32))
    tab_dram = nc.dram_tensor("bias_scratch", (NH * DR, TPW), F32)
    gate_dram = nc.dram_tensor("gate_scratch", (NK, P, T), F32).ap()
    act_dram = nc.dram_tensor("act_scratch", (NB, P, T), F32).ap()

    ident = cst[:, C_ID:C_ID + P]
    flip = mix_cst[:, 0:P]
    ones = cst[:, C_ONE:C_ONE + P]
    iota = cst[:, C_IOTA:C_IOTA + P]
    colmask = mix_cst[:, C_MASK - C_FLIP:C_RCNT - C_FLIP]
    rcnt = mix_cst[:, C_RCNT - C_FLIP:].rearrange("p (b t) -> p b t", b=2)

    bias_v = bias[:].rearrange("p a h (r c) -> p (a h r) c", c=GRID)

    def S(name, per, credit=0):
        return Signal(nc, ctx, name, per, credit)

    const_ld = S("const_ld", 0)
    x_ld = S("x_ld", 0)
    xi_mm = S("xi_mm", 0)
    xi_evac = S("xi_evac", 0)
    c_tr = S("c_tr", 0)
    silu_rdy = S("silu_rdy", 0)
    zero_rdy = S("zero_rdy", 0)
    vec_ld = S("vec_ld", 16 * 6)
    vec_tr = S("vec_tr", 1, credit=1)
    vec_rdy = S("vec_rdy", 1)
    w_ld = [S(f"w_ld{i}", 16 * FILLS) for i in range(WR)]
    mix_ld = S("mix_ld", 16)
    iota_rdy = S("iota_rdy", 0)
    w_used = S("w_used", W_PER)
    sq_rdy = S("sq_rdy", 2)
    sum_mm = S("sum_mm", 2)
    var_rdy = S("var_rdy", 2)
    std_rdy = S("std_rdy", 2)
    xn_rdy = S("xn_rdy", 2)
    h_rdy = S("h_rdy", 2)
    norm_ch = S("norm_ch", 2 * 5)
    mods_rdy = S("mods_rdy", 1)
    mods_ch = S("mods_ch", 1)
    pj_mm = S("pj_mm", 22)
    pj_evac = S("pj_evac", 22, credit=2)
    kc_mm = S("kc_mm", 1)
    kc_evac = S("kc_evac", 1)
    kv_st = S("kv_st", 32)
    cache_ld = S("cache_ld", 32)
    ck_mm = S("ck_mm", 1)
    ck_evac = S("ck_evac", 1)
    tab_ld = S("tab_ld", 16)
    tab_st = S("tab_st", 16)
    bias_ld = S("bias_ld", 16 * ROWS * NH)
    bias_rdy = S("bias_rdy", 1)
    pad_rdy = S("pad_rdy", 1)
    poolw_ld = S("poolw_ld", 64)
    conv_ch = S("conv_ch", 4)
    pool_ch = S("pool_ch", 6)
    pd_rdy = S("pd_rdy", 1)
    pool_mm = S("pool_mm", 1)
    branch_rdy = S("branch_rdy", 1)
    NU = 3 * NH
    s_mm = S("s_mm", NU)
    att_ch = S("att_ch", 2 * NU)
    nmax_rdy = S("nmax_rdy", NU)
    exp_rdy = S("exp_rdy", NU, credit=2)
    pr_rdy = S("pr_rdy", NU)
    t_mm = S("t_mm", NU)
    t_evac = S("t_evac", NU, credit=2)
    o_mm = S("o_mm", NU)
    o_evac = S("o_evac", NU, credit=2)
    xo_mm = S("xo_mm", KC)
    xo_evac = S("xo_evac", KC, credit=2)
    pq_mm = S("pq_mm", HP)
    pq_evac = S("pq_evac", HP, credit=2)
    sk_mm = S("sk_mm", 4)
    sk_evac = S("sk_evac", 4)
    sc_mm = S("sc_mm", 4 * TB)
    sc_evac = S("sc_evac", 4 * TB)
    s_next = S("s_next", TB, credit=1)
    route_ch = S("route_ch", ROUTE_STEPS * TB)
    s_free = S("s_free", TB)
    gexp_in = S("gexp_in", TB)
    gexp_rdy = S("gexp_rdy", TB)
    pk_rdy = S("pk_rdy", TB)
    pk_mm = S("pk_mm", TB)
    pk_evac = S("pk_evac", TB)
    NQ = T // 4
    pt_ch = S("pt_ch", 4 * TB)
    oe_ch = S("oe_ch", NQ)
    one_rdy = S("one_rdy", NQ)
    gq_mm = S("gq_mm", NQ, credit=2)
    gq_evac = S("gq_evac", NQ, credit=2)
    g_st = S("g_st", 16 * TB, credit=16)
    hh_rdy = S("hh_rdy", 1)
    hl_rdy = S("hl_rdy", 1)
    ut_mm = S("ut_mm", 2 * NB)
    uhi_rdy = S("uhi_rdy", 2 * NB)
    ulo_rdy = S("ulo_rdy", 2 * NB, credit=2)
    h_mm = S("h_mm", NB, credit=2)
    gelu_rdy = S("gelu_rdy", NB, credit=2)
    act_st = S("act_st", 16 * NB)
    act_free = S("act_free", NB, credit=2)
    ga_ld = [S(f"ga_ld{i}", 32 * (NG // 2)) for i in range(2)]
    w32_rdy = S("w32_rdy", NB)
    whi_rdy = S("whi_rdy", NB)
    wlo_rdy = S("wlo_rdy", NB)
    NV = 2 * NB
    vhi_rdy = S("vhi_rdy", NV)
    vlo_rdy = S("vlo_rdy", NV, credit=4 * G)
    v_mm = S("v_mm", NV, credit=4)
    ac_evac = S("ac_evac", 2 * NG, credit=2)
    acc_zero = S("acc_zero", 1)
    xa_mm = S("xa_mm", KC)
    xa_evac = S("xa_evac", KC, credit=2)
    fo_mm = S("fo_mm", 0)
    fo_evac = S("fo_evac", 0)
    y_st = S("y_st", 0)

    dve_passed = S("dve_passed", 0)
    pool_passed = S("pool_passed", 0)
    pe_passed = S("pe_passed", 0)
    sp_passed = S("sp_passed", 0)

    block = ctx.enter_context(nc.Block())

    def seg_cols(v):
        return slice(SEGS[v][0], SEGS[v][1])

    def unit(n):
        head, b = divmod(n, 3)
        return head, b, (3 if b else 1), slice(b * P, (b + 1) * P)


    def output_units(eng, unit_step):
        with eng.Fori(0, NG // 2 - 1) as i:
            for n in range(4 * G):
                unit_step(i, n, False)
        for n in range(4 * G):
            unit_step(NG // 2 - 1, n, True)

    @block.sync
    def _(sp):
        sp.sem_inc(g_st.sem, g_st.credit)
        sp.dma_start(cst[:], consts[:, 0:C_FLIP]).then_inc(const_ld.sem, 16)
        for tb, src in ((0, x_prompt[0]), (1, x_sample[0, 0:P]), (2, x_sample[0, P:2 * P])):
            sp.dma_start(x_nat[:, tb], src).then_inc(x_ld.sem, 16)
        sp.dma_start(c_nat[0:KC], c_ctx.rearrange("(k p) -> k p", p=P)).then_inc(const_ld.sem, 16)
        sp.dma_start(c_nat[KC:16], c[0].rearrange("(k p) -> k p", p=P)).then_inc(const_ld.sem, 16)
        with sp.Fori(0, DEPTH) as l:
            sp.wait_ge(vec_tr.sem, vec_tr.at(l, 0))
            for row, n, src in ((ROW_ADA, 48, b_ada), (ROW_G1, 8, norm1_g), (ROW_G2, 8, norm2_g),
                                (ROW_PS, 2, pool_scale)):
                sp.dma_start(vec_nat[row:row + n], src[l].rearrange("(k p) -> k p", p=P)) \
                  .then_inc(vec_ld.sem, 16)
            sp.dma_start(vec_nat[ROW_CONV:ROW_CONV + 6], conv_w[l].rearrange("w (k p) -> (w k) p", p=P)) \
              .then_inc(vec_ld.sem, 16)
            sp.dma_start(vec_nat[ROW_FG:ROW_FG + 8], final_g.rearrange("(k p) -> k p", p=P)) \
              .then_inc(vec_ld.sem, 16)
            for n in range(W_PER):
                for first, count, src in ((0, N_ADA, w_ada), (W_IN0, N_IN, w_in), (W_OUT0, N_OUT, w_out),
                                          (W_WQ0, N_WQ, peer_wq)):
                    if first <= n < first + count:
                        tile = src[l].rearrange("(k p) n -> p k n", p=P)[:, :, (n - first) * WCOLS:
                                                                         (n - first + 1) * WCOLS]
                        dst = wring[:, n % WR]
                if n >= W_SK0:
                    tile = peer_subkeys[l].rearrange("h q k d -> k (h q) d")[:, (n - W_SK0) * 8:
                                                                             (n - W_SK0 + 1) * 8]
                    dst = wring[:, n % WR].rearrange("p k n -> p (k n)")[:, 0:8 * P] \
                        .rearrange("p (s d) -> p s d", s=8)
                if n < WR:
                    sp.wait_ge(vlo_rdy.sem, vlo_rdy.at(l, G * (n + 1 - WR)))
                else:
                    sp.wait_ge(w_used.sem, w_used.at(l, n + 1 - WR))
                sp.dma_start(dst, tile).then_inc(w_ld[n % WR].sem, 16)

            def load_u(n, slot):
                sp.dma_start(wring[:, slot].rearrange("p k n -> p (k n)").rearrange("p (b d) -> p b d", b=2),
                             peer_u[l, bass.ds(n * (2 * P), 2 * P)].rearrange("(b p) d -> p b d", b=2)) \
                  .then_inc(w_ld[slot].sem, 16)

            def store_gates(tb):
                sp.wait_ge(gq_evac.sem, gq_evac.at(l, 0) + (tb + 1) * (NQ // TB))
                sp.dma_start(gate_dram[:, :, bass.ds(tb * P, P)].rearrange("a b t -> b a t"), g_all[:]) \
                  .then_inc(g_st.sem, 16)

            for n in range(WR):
                sp.wait_ge(w_used.sem, w_used.at(l, W_PER + n + 1 - WR))
                load_u(n, n)

            def more_u(i):
                for s in range(WR):
                    sp.wait_ge(ut_mm.sem, ut_mm.at(l, 0) + (i * (4 * WR) + 4 * (s + 1 - WR)))
                    load_u(i * WR + s, s)

            with sp.Fori(0, TB) as tb:
                for k in range(4):
                    more_u(tb * 4 + (k + 1))
                store_gates(tb)
            for k in range(3):
                more_u(4 * TB + 1 + k)

            def load_ga(g, buf):
                for dst, src in ((gate2, gate_dram), (act2, act_dram)):
                    sp.dma_start(dst[:, buf], src[bass.ds(g * G, G)].rearrange("b e t -> e b t")) \
                      .then_inc(ga_ld[buf].sem, 16)

            def load_v(g, half, slot):
                sp.dma_start(wring[:, slot].rearrange("p k n -> p (k n)").rearrange("p (b d) -> p b d", b=G),
                             peer_v[l, bass.ds(g * (G * P), G * P), half * 512:(half + 1) * 512]
                             .rearrange("(b p) d -> p b d", b=G)).then_inc(w_ld[slot].sem, 16)

            sp.wait_ge(g_st.sem, g_st.at(l, 16 * TB))
            sp.sem_inc(sp_passed.sem, 1)
            for n in range(WR):
                sp.wait_ge(ut_mm.sem, ut_mm.at(l, 2 * NB + 4 * (n + 1 - WR)))
                load_v(n // 2, n % 2, n)
            sp.wait_ge(act_st.sem, act_st.at(l, 16 * NB))
            sp.wait_ge(h_mm.sem, h_mm.at(l, NB))
            load_ga(0, 0)
            load_ga(1, 1)

            def group_loads(g, n, ga=True):
                if ga:
                    sp.wait_ge(w32_rdy.sem, l * NB + (g - 1) * G)
                    load_ga(g, n)
                for half in range(2):
                    slot = 2 * n + half
                    sp.wait_ge(vlo_rdy.sem, l * NV + (g * (2 * G) + (G * (half - 3) + vlo_rdy.credit)))
                    load_v(g, half, slot)

            with sp.Fori(1, NG // 2) as i:
                for n in range(2):
                    group_loads(i * 2 + n, n)
        for tb, dst in ((0, y_prompt[0]), (1, y_sample[0, 0:P]), (2, y_sample[0, P:2 * P])):
            sp.wait_ge(fo_evac.sem, 2 * (tb + 1))
            sp.dma_start(dst, y_nat[:, tb]).then_inc(y_st.sem, 16)
        sp.wait_ge(y_st.sem, 16 * TB)

    @block.gpsimd
    def _(pool):
        pool.sem_inc(act_free.sem, act_free.credit)
        nc.gpsimd.memset(pool_blk[:], 0.0).then_inc(zero_rdy.sem, 1)
        pool.wait_ge(zero_rdy.sem, 1)
        pool.sem_inc(pool_passed.sem, 1)
        with pool.Fori(0, DEPTH) as l:
            pool.wait_ge(xa_evac.sem, xa_evac.at(l, 0))
            pool.sem_inc(pool_passed.sem, 1)
            pool.wait_ge(xi_evac.sem, 2 * TB)
            pool.sem_inc(pool_passed.sem, 1)
            pool.dma_start(mix_cst[:], consts[:, C_FLIP:]).then_inc(mix_ld.sem, 16)
            nc.gpsimd.memset(bias_tab[:], 0.0)
            nc.gpsimd.memset(pool_in[:], 0.0).then_inc(pad_rdy.sem, 1)
            pool.wait_ge(pad_rdy.sem, pad_rdy.at(l, 1))
            pool.sem_inc(pool_passed.sem, 1)
            pool.dma_start(bias_tab[0:NH * DR, GRID - NCOLS:GRID - NCOLS + DC],
                           rpb[l].rearrange("h r c -> (h r) c")).then_inc(tab_ld.sem, 16)
            for g in range(4):
                half = slice((g % 2) * 64, (g % 2) * 64 + 64)
                pool.dma_start(pool_blk[half, g // 2, half], pool_w[l, g]).then_inc(poolw_ld.sem, 16)
            pool.dma_start(cK[:].rearrange("m (h d) -> m h d", h=NH), cache_k[0, l].rearrange("h m d -> m h d")) \
                .then_inc(cache_ld.sem, 16)
            pool.dma_start(cV[:].rearrange("m (h d) -> m h d", h=NH), cache_v[0, l].rearrange("h m d -> m h d")) \
                .then_inc(cache_ld.sem, 16)
            pool.wait_ge(tab_ld.sem, tab_ld.at(l, 16))
            pool.sem_inc(pool_passed.sem, 1)
            pool.dma_start(tab_dram.ap(), bias_tab[0:NH * DR, :]).then_inc(tab_st.sem, 16)
            pool.wait_ge(tab_st.sem, tab_st.at(l, 16))
            pool.sem_inc(pool_passed.sem, 1)
            for r in range(ROWS):
                for hd in range(NH):
                    src = bass.AP(tab_dram, (hd * DR + 7 - r) * TPW, [[1, GRID], [TPW, ROWS], [1, GRID]])
                    dst = bias[(r % 2) * GRID:(r % 2 + 1) * GRID, r // 2, hd].rearrange(
                        "p (a b) -> p a b", a=ROWS)
                    pool.dma_start(dst, src).then_inc(bias_ld.sem, 16)
            pool.wait_ge(bias_ld.sem, bias_ld.at(l, 16 * ROWS * NH))
            pool.sem_inc(pool_passed.sem, 1)
            pool.wait_ge(mix_ld.sem, mix_ld.at(l, 16))
            pool.sem_inc(pool_passed.sem, 1)
            nc.gpsimd.tensor_tensor(bias_v, bias_v, colmask.unsqueeze(1).to_broadcast([P, 2 * NH * ROWS, GRID]),
                                    ALU.add).then_inc(bias_rdy.sem, 1)
            pool.wait_ge(pj_evac.sem, pj_evac.at(l, 22))
            pool.sem_inc(pool_passed.sem, 1)
            pool.dma_start(new_v[0, l].rearrange("h t d -> t h d"),
                           vN[:, 0].rearrange("t (h d) -> t h d", h=NH)).then_inc(kv_st.sem, 16)
            pool.wait_ge(kc_evac.sem, kc_evac.at(l, 1))
            pool.sem_inc(pool_passed.sem, 1)
            pool.dma_start(new_k[0, l].rearrange("h t d -> t h d"),
                           k_out[:].rearrange("t (h d) -> t h d", h=NH)).then_inc(kv_st.sem, 16)
            pool.wait_ge(kv_st.sem, kv_st.at(l, 32))
            pool.sem_inc(pool_passed.sem, 1)
            with pool.Fori(0, NB // 2) as i:
                for b in range(2):
                    pool.wait_ge(gelu_rdy.sem, l * NB + (i * 2 + (b + 1 + gelu_rdy.credit)))
                    pool.sem_inc(pool_passed.sem, 1)
                    pool.dma_start(act_dram[i * 2 + b], act_h[:, b]).then_inc(act_st.sem, 16)
                    pool.wait_ge(act_st.sem, (l * NB + (i * 2 + (b + 1))) * 16)
                    pool.sem_inc(act_free.sem, 1)
            pool.wait_ge(g_st.sem, g_st.at(l, 16 * TB))
            pool.sem_inc(pool_passed.sem, 1)
            nc.gpsimd.memset(acc[:], 0.0).then_inc(acc_zero.sem, 1)

    @block.tensor
    def _(pe):
        for sig in (vec_tr, gq_mm, h_mm, v_mm):
            pe.sem_inc(sig.sem, sig.credit)

        def sums(N):
            pe.wait_ge(sq_rdy.sem, N + 1)
            for k in range(KC):
                last = nc.tensor.matmul(ps[:, 5, 0:T], ones, h[:, k], start=(k == 0), stop=(k == KC - 1))
            last.then_inc(sum_mm.sem, 1)

        pe.wait_ge(const_ld.sem, 48)
        pe.wait_ge(x_ld.sem, 16 * TB)
        nc.tensor.transpose(ps[:, 7, 0:16], c_nat[:], ident[0:16, 0:16]).then_inc(c_tr.sem, 1)
        for n in range(2 * TB):
            tb, half = divmod(n, 2)
            for k in range(4):
                src = x_nat[:, tb, (half * 4 + k) * P:(half * 4 + k + 1) * P]
                last = nc.tensor.transpose(ps[:, n, k * P:(k + 1) * P], src, ident)
            last.then_inc(xi_mm.sem, 1)

        with pe.Fori(0, DEPTH) as l:
            pe.wait_ge(vec_ld.sem, vec_ld.at(l, 16 * 6))
            pe.wait_ge(silu_rdy.sem, 1)
            nc.tensor.transpose(ps[:, 7, 0:NROWS], vec_nat[0:NROWS], ident[0:NROWS, 0:NROWS]) \
                .then_inc(vec_tr.sem, 1)
            sums(2 * l)

            def tile_in(n):
                pe.wait_ge(w_ld[n % WR].sem, w_ld[n % WR].at(l, 16 * (n // WR + 1)))
                return wring[:, n % WR]

            for n in range(N_ADA):
                w = tile_in(n)
                for b in range(2):
                    blk = 2 * n + b
                    for k in range(KC):
                        last = nc.tensor.matmul(ps[:, 6, 2 * blk:2 * blk + 2], w[:, k, b * P:(b + 1) * P],
                                                silu_c[:, k], start=(k == 0), stop=(k == KC - 1))
                last.then_inc(w_used.sem, 1)

            def column_blocks(tiles, first, mm, evac, src):
                for n in tiles:
                    w = tile_in(n)
                    for b in range(2):
                        m = 2 * (n - first) + b
                        pe.wait_ge(evac.sem, evac.at(l, m - 1))
                        for k in range(KC):
                            last = nc.tensor.matmul(ps[:, m % 2, 0:T], w[:, k, b * P:(b + 1) * P], src[:, k],
                                                    start=(k == 0), stop=(k == KC - 1))
                        last.then_inc(mm.sem, 1)
                    pe.wait_ge(mm.sem, mm.at(l, m + 1))
                    pe.sem_inc(w_used.sem, 1)

            pe.wait_ge(h_rdy.sem, h_rdy.at(l, 1))
            column_blocks(range(W_IN0, W_IN0 + 8), W_IN0, pj_mm, pj_evac, h)
            for n in (W_IN0 + 8, W_IN0 + 9):
                w = tile_in(n)
                for tb in range(TB):
                    m = 16 + (n - W_IN0 - 8) * TB + tb
                    pe.wait_ge(pj_evac.sem, pj_evac.at(l, m - 1))
                    for k in range(KC):
                        last = nc.tensor.matmul(ps[:, m % 2, 0:WCOLS], h[:, k, tb * P:(tb + 1) * P], w[:, k],
                                                start=(k == 0), stop=(k == KC - 1))
                    last.then_inc(pj_mm.sem, 1)
                pe.wait_ge(pj_mm.sem, pj_mm.at(l, m + 1))
                pe.sem_inc(w_used.sem, 1)
            pe.wait_ge(pj_evac.sem, pj_evac.at(l, 16))
            pe.wait_ge(std_rdy.sem, std_rdy.at(l, 1))
            for k in range(4):
                last = nc.tensor.transpose(ps[:, 5, k * P:(k + 1) * P], kT[:, k, 0:P], ident)
            last.then_inc(kc_mm.sem, 1)
            pe.wait_ge(cache_ld.sem, cache_ld.at(l, 32))
            pe.wait_ge(mods_rdy.sem, mods_rdy.at(l, 1))
            for k in range(4):
                last = nc.tensor.transpose(ps[:, 6, k * P:(k + 1) * P], cK[:, k * P:(k + 1) * P], ident)
            last.then_inc(ck_mm.sem, 1)
            pe.wait_ge(poolw_ld.sem, poolw_ld.at(l, 64))
            pe.wait_ge(vec_rdy.sem, vec_rdy.at(l, 1))
            pe.wait_ge(pd_rdy.sem, pd_rdy.at(l, 1))
            for b, bank in enumerate((4, 7)):
                last = nc.tensor.matmul(ps[:, bank, 0:T], pool_blk[:, b], pool_d[:, b], start=True, stop=True)
            last.then_inc(pool_mm.sem, 1)

            pe.wait_ge(pj_evac.sem, pj_evac.at(l, 22))
            pe.wait_ge(ck_evac.sem, ck_evac.at(l, 1))
            pe.wait_ge(kc_evac.sem, kc_evac.at(l, 1))
            pe.wait_ge(branch_rdy.sem, branch_rdy.at(l, 1))

            def scores(n):
                head, b, _, q_cols = unit(n)
                rows = slice((head % 2) * HD, (head % 2 + 1) * HD)
                q = qT[rows, head // 2, q_cols]
                pe.wait_ge(exp_rdy.sem, exp_rdy.at(l, n - 1))
                if b == 0:
                    nc.tensor.matmul(ps[:, n % 2, 0:P], q, kT[rows, head // 2, 0:TCTX], start=True, stop=True) \
                        .then_inc(s_mm.sem, 1)
                else:
                    nc.tensor.matmul(ps[:, n % 2, 0:TLAT], flip, bias[:, b - 1, head], start=True, stop=False)
                    nc.tensor.matmul(ps[:, n % 2, 0:TLAT], q, kT[rows, head // 2, TCTX:T], start=False, stop=True)
                    nc.tensor.matmul(ps[:, n % 2, TLAT:KEYS], q, cKT[rows, head // 2], start=True, stop=True) \
                        .then_inc(s_mm.sem, 1)

            pe.wait_ge(bias_rdy.sem, bias_rdy.at(l, 1))
            scores(0)
            for n in range(NU + 1):
                if n + 1 < NU:
                    scores(n + 1)
                if n < NU:
                    head, b, blocks, _ = unit(n)
                    pe.wait_ge(pr_rdy.sem, pr_rdy.at(l, n + 1))
                    pe.wait_ge(t_evac.sem, t_evac.at(l, n - 1))
                    for k in range(blocks):
                        last = nc.tensor.transpose(ps[:, 2 + n % 2, k * P:(k + 1) * P],
                                                   pr[:, n % 2, k * P:(k + 1) * P], ident)
                    last.then_inc(t_mm.sem, 1)
                if n >= 1:
                    m = n - 1
                    head, b, blocks, _ = unit(m)
                    pair = slice((head // 2) * P, (head // 2 + 1) * P)
                    values = [vN[:, 0, pair]] if b == 0 else [vN[:, 1, pair], vN[:, 2, pair], cV[:, pair]]
                    pe.wait_ge(t_evac.sem, t_evac.at(l, m + 1))
                    pe.wait_ge(o_evac.sem, o_evac.at(l, m - 1))
                    for k in range(blocks):
                        last = nc.tensor.matmul(ps[:, 5 + m % 2, 0:P], values[k], prT[:, m % 2, k],
                                                start=(k == 0), stop=(k == blocks - 1))
                    last.then_inc(o_mm.sem, 1)

            pe.wait_ge(o_evac.sem, o_evac.at(l, NU))
            column_blocks(range(W_OUT0, W_OUT0 + N_OUT), W_OUT0, xo_mm, xo_evac, y)
            sums(2 * l + 1)
            pe.wait_ge(h_rdy.sem, h_rdy.at(l, 2))
            column_blocks(range(W_WQ0, W_WQ0 + N_WQ), W_WQ0, pq_mm, pq_evac, h)
            for n in range(4):
                tile = W_SK0 + n // 2
                w = tile_in(tile)[:].rearrange("p k n -> p (k n)")
                for k in range(4):
                    at_ = ((n % 2) * 4 + k) * P
                    last = nc.tensor.transpose(ps[:, (2, 3, 4, 7)[n], k * P:(k + 1) * P], w[:, at_:at_ + P], ident)
                last.then_inc(sk_mm.sem, 1)
                if n % 2:
                    pe.wait_ge(sk_mm.sem, sk_mm.at(l, n + 1))
                    pe.sem_inc(w_used.sem, 1)

            def route_scores(tb):
                for n in range(4):
                    if tb:
                        pe.wait_ge(sc_evac.sem, sc_evac.at(l, 4 * (tb - 1) + n + 1))
                    for k in range(4):
                        hp = 4 * n + k
                        last = nc.tensor.matmul(ps[:, n, k * P:(k + 1) * P], pq[:, hp, tb * P:(tb + 1) * P],
                                                skT[:, hp], start=True, stop=True)
                    last.then_inc(sc_mm.sem, 1)

            pe.wait_ge(pq_evac.sem, pq_evac.at(l, HP))
            pe.wait_ge(sk_evac.sem, sk_evac.at(l, 4))
            for tb in range(TB):
                route_scores(tb)

            def hidden_step(jb, s, transpose=True):
                J = l * NB + (jb * 8 + s)
                if transpose:
                    slot, b = ((s + 1) // 2) % WR, (s + 1) % 2
                    if b == 0:
                        pe.wait_ge(w_ld[slot].sem, (l * FILLS + (jb + (W_PER // WR + (s + 1) // 8 + 1))) * 16)
                    rows = wring[:, slot].rearrange("p k n -> p (k n)")
                    for hh in range(2):
                        pe.wait_ge(ulo_rdy.sem, 2 * J + (hh + 3))
                        for k in range(4):
                            at_ = b * D + (4 * hh + k) * P
                            last = nc.tensor.transpose(ps[:, 3 + hh, k * P:(k + 1) * P], rows[:, at_:at_ + P], ident)
                        last.then_inc(ut_mm.sem, 1)
                if s >= 0:
                    pe.wait_ge(ulo_rdy.sem, 2 * J + (2 + ulo_rdy.credit))
                    pe.wait_ge(gelu_rdy.sem, J + 1)
                    for k in range(KC):
                        for n, (u, hx) in enumerate(((u_hi, h_lo), (u_hi, h_hi), (u_lo, h_hi))):
                            last = nc.tensor.matmul(ps[:, 5 + s % 2, 0:T], u[:, s % 2, k], hx[:, k],
                                                    start=(k == 0 and n == 0), stop=(k == KC - 1 and n == 2))
                    last.then_inc(h_mm.sem, 1)

            pe.wait_ge(sc_evac.sem, sc_evac.at(l, 4 * TB))
            pe.wait_ge(hl_rdy.sem, hl_rdy.at(l, 1))
            hidden_step(0, -1)
            with pe.Fori(0, TB) as tb:
                for s in range(TOPK_STEPS):
                    hidden_step(tb * 4, s)
                pe.wait_ge(pk_rdy.sem, l * TB + tb + 1)
                for k in range(3):
                    last = nc.tensor.transpose(ps[:, 2, k * P:(k + 1) * P], picked[:, k], ident)
                last.then_inc(pk_mm.sem, 1)
                with pe.Fori(0, GATE_STEPS // 8) as i:
                    for s in range(8):
                        hidden_step(tb * 4 + (i + 2), s)
                        for a in range(2):
                            Q = (l * TB + tb) * (P // 4) + (i * 16 + (2 * s + a))
                            pe.wait_ge(one_rdy.sem, Q + 1)
                            pe.wait_ge(gq_evac.sem, Q + 1)
                            for k in range(4):
                                for n in range(3):
                                    last = nc.tensor.matmul(ps[:, a, k * P:(k + 1) * P], one_a[:, a, :, k],
                                                            one_b[:, a, n, :, k], start=(n == 0), stop=(n == 2))
                            last.then_inc(gq_mm.sem, 1)
            with pe.Fori(4 * TB, NB // 8 - 1) as jb:
                for s in range(8):
                    hidden_step(jb, s)
            for s in range(8):
                hidden_step(NB // 8 - 1, s, s < 7)

            def unit_step(i, n, last_units):
                M = l * NV + (i * (4 * G) + n)
                group, half, b = n // (2 * G), (n // G) % 2, n % G
                bank = 3 * half
                pe.wait_ge(vlo_rdy.sem, M + (1 + vlo_rdy.credit))
                pe.wait_ge(wlo_rdy.sem, l * NB + (i * (2 * G) + (group * G + b + 1)))
                if b == 0:
                    pe.wait_ge(ac_evac.sem, l * (2 * NG) + (i * 4 + (2 * group + half + 1)))
                for tb in range(TB):
                    cols = slice(tb * P, (tb + 1) * P)
                    for k, (w, v) in enumerate(((w_hi, v_lo), (w_hi, v_hi), (w_lo, v_hi))):
                        last = nc.tensor.matmul(ps[:, bank + tb], w[:, group * G + b, cols], v[:, n % 4],
                                                start=(b == 0 and k == 0), stop=(b == G - 1 and k == 2))
                last.then_inc(v_mm.sem, 1)

            pe.wait_ge(gelu_rdy.sem, gelu_rdy.at(l, NB))
            pe.wait_ge(gq_evac.sem, gq_evac.at(l, NQ))
            pe.wait_ge(pk_evac.sem, pk_evac.at(l, TB))
            pe.sem_inc(pe_passed.sem, 1)
            output_units(pe, unit_step)
            for k in range(KC):
                pe.wait_ge(ac_evac.sem, ac_evac.at(l, 2 * NG))
                pe.wait_ge(xa_evac.sem, xa_evac.at(l, k - 1))
                for tb in range(TB):
                    last = nc.tensor.transpose(ps[:, k % 2, tb * P:(tb + 1) * P], acc[:, tb, k * P:(k + 1) * P],
                                               ident)
                last.then_inc(xa_mm.sem, 1)

        sums(2 * DEPTH)
        pe.wait_ge(h_rdy.sem, 2 * DEPTH + 1)
        for n in range(2 * TB):
            tb, half = divmod(n, 2)
            bank = (0, 1, 2, 3, 4, 6)[n]
            for k in range(4):
                last = nc.tensor.transpose(ps[:, bank, k * P:(k + 1) * P], h[:, half * 4 + k, tb * P:(tb + 1) * P],
                                           ident)
            last.then_inc(fo_mm.sem, 1)

    @block.scalar
    def _(act):
        for sig in (pj_evac, exp_rdy, t_evac, o_evac, pq_evac, s_next, gq_evac, gelu_rdy):
            act.sem_inc(sig.sem, sig.credit)



        def norm(N, l, which):
            nc.scalar.activation(h[:], x[:], ACT.Square).then_inc(sq_rdy.sem, 1)
            act.wait_ge(var_rdy.sem, N + 1)
            nc.scalar.activation(norm_t[:, 1], norm_t[:, 0], ACT.Sqrt).then_inc(std_rdy.sem, 1)
            act.wait_ge(xn_rdy.sem, N + 1)
            if which is None:
                for k in range(KC):
                    last = nc.scalar.activation(h[:, k], h[:, k], ACT.Copy, scale=vecs[:, ROW_FG + k:ROW_FG + k + 1])
            else:
                act.wait_ge(mods_rdy.sem, mods_rdy.at(l, 1))
                shift = (SH1, SH2)[which]
                for k in range(KC):
                    for v in range(2):
                        last = nc.scalar.activation(h[:, k, seg_cols(v)], h[:, k, seg_cols(v)], ACT.Identity,
                                                    scale=gs[:, which, k, v:v + 1],
                                                    bias=mods[:, shift + k, v:v + 1])
            last.then_inc(h_rdy.sem, 1)

        for n in range(2 * TB):
            tb, half = divmod(n, 2)
            act.wait_ge(xi_mm.sem, n + 1)
            nc.scalar.copy(x[:, half * 4:half * 4 + 4, tb * P:(tb + 1) * P],
                           ps[:, n].rearrange("p (k t) -> p k t", t=P)).then_inc(xi_evac.sem, 1)
        act.wait_ge(c_tr.sem, 1)
        nc.scalar.activation(silu_c[:], ps[:, 7, 0:16].rearrange("p (v k) -> p k v", v=2), ACT.Silu) \
            .then_inc(silu_rdy.sem, 1)

        with act.Fori(0, DEPTH) as l:
            act.wait_ge(vec_tr.sem, vec_tr.at(l, 1))
            nc.scalar.copy(vecs[:], ps[:, 7, 0:NROWS]).then_inc(vec_rdy.sem, 1)
            act.wait_ge(xi_evac.sem, 2 * TB)
            act.wait_ge(xa_evac.sem, xa_evac.at(l, 0))
            norm(2 * l, l, 0)
            for m in range(22):
                act.wait_ge(pj_mm.sem, pj_mm.at(l, m + 1))
                src = ps[:, m % 2, 0:T]
                if m < 6:
                    last = nc.scalar.copy(branch[:, m], src)
                elif m < 8:
                    if m == 6:
                        act.wait_ge(pad_rdy.sem, pad_rdy.at(l, 1))
                    for v in range(2):
                        w = SEGS[v][1] - SEGS[v][0]
                        last = nc.scalar.copy(pool_in[:, m - 6, SEG_AT[v]:SEG_AT[v] + w], src[:, seg_cols(v)])
                elif m < 12:
                    last = nc.scalar.activation(qT[:, m - 8], src, ACT.Copy, scale=SCALE)
                elif m < 16:
                    last = nc.scalar.copy(kT[:, m - 12], src)
                else:
                    n, tb = divmod(m - 16, TB)
                    last = nc.scalar.copy(vN[:, tb, n * WCOLS:(n + 1) * WCOLS], ps[:, m % 2, 0:WCOLS])
                last.then_inc(pj_evac.sem, 1)
            act.wait_ge(kc_mm.sem, kc_mm.at(l, 1))
            nc.scalar.copy(k_out[:], ps[:, 5]).then_inc(kc_evac.sem, 1)
            act.wait_ge(ck_mm.sem, ck_mm.at(l, 1))
            nc.scalar.copy(cKT[:].rearrange("p k m -> p (k m)"), ps[:, 6]).then_inc(ck_evac.sem, 1)
            for n in range(NU + 2):
                if n < NU:
                    keys = P if unit(n)[1] == 0 else KEYS
                    act.wait_ge(nmax_rdy.sem, nmax_rdy.at(l, n + 1))
                    nc.scalar.activation(pr[:, n % 2, 0:keys], ps[:, n % 2, 0:keys], ACT.Exp,
                                         bias=stat[:, n % 2, 1:2], accum_out=stat[:, n % 2, 2:3]) \
                        .then_inc(exp_rdy.sem, 1)
                if 1 <= n <= NU:
                    m = n - 1
                    cols = unit(m)[2] * P
                    act.wait_ge(t_mm.sem, t_mm.at(l, m + 1))
                    if m >= 2:
                        act.wait_ge(o_mm.sem, o_mm.at(l, m - 1))
                    nc.scalar.copy(prT[:, m % 2].rearrange("p k q -> p (k q)")[:, 0:cols],
                                   ps[:, 2 + m % 2, 0:cols]).then_inc(t_evac.sem, 1)
                if n >= 2:
                    m = n - 2
                    head, _, _, q_cols = unit(m)
                    rows = slice((head % 2) * HD, (head % 2 + 1) * HD)
                    act.wait_ge(o_mm.sem, o_mm.at(l, m + 1))
                    nc.scalar.copy(y[rows, 4 + head // 2, q_cols], ps[rows, 5 + m % 2, 0:P]) \
                        .then_inc(o_evac.sem, 1)
            act.wait_ge(xo_evac.sem, xo_evac.at(l, KC))
            norm(2 * l + 1, l, 1)
            act.wait_ge(kv_st.sem, kv_st.at(l, 32))
            act.wait_ge(h_rdy.sem, h_rdy.at(l, 2))
            nc.scalar.copy(h_hi[:], h[:]).then_inc(hh_rdy.sem, 1)
            for m in range(HP):
                act.wait_ge(pq_mm.sem, pq_mm.at(l, m + 1))
                nc.scalar.copy(pq[:, m], ps[:, m % 2, 0:T]).then_inc(pq_evac.sem, 1)
            for n in range(4):
                act.wait_ge(sk_mm.sem, sk_mm.at(l, n + 1))
                nc.scalar.copy(skT[:, 4 * n:4 * n + 4].rearrange("p s k -> p (s k)"), ps[:, (2, 3, 4, 7)[n]]) \
                    .then_inc(sk_evac.sem, 1)

            for tb in range(TB):
                to = s_sb if tb == 0 else s_all[:, tb - 1]
                for n in range(4):
                    act.wait_ge(sc_mm.sem, sc_mm.at(l, 4 * tb + n + 1))
                    nc.scalar.copy(to[:, 4 * n:4 * n + 4].rearrange("p s k -> p (s k)"), ps[:, n]) \
                        .then_inc(sc_evac.sem, 1)

            def hidden_step(jb, s, transpose=True, gelu=True):
                J = l * NB + (jb * 8 + s)
                if gelu:
                    p = (s - 1) % 2
                    act.wait_ge(h_mm.sem, J + h_mm.credit)
                    act.wait_ge(act_free.sem, J)
                    nc.scalar.activation(act_h[:, p], ps[:, 5 + p, 0:T], ACT.Gelu_apprx_tanh) \
                        .then_inc(gelu_rdy.sem, 1)
                if transpose:
                    for hh in range(2):
                        act.wait_ge(ut_mm.sem, 2 * J + (hh + 3))
                        act.wait_ge(h_mm.sem, J + h_mm.credit)
                        nc.scalar.copy(u_hi[:, (s + 1) % 2, 4 * hh:4 * hh + 4],
                                       ps[:, 3 + hh].rearrange("p (k e) -> p k e", e=P)).then_inc(uhi_rdy.sem, 1)

            hidden_step(0, -1, gelu=False)

            def last_gelu(jb):
                act.wait_ge(h_mm.sem, l * NB + (jb * 8 + h_mm.credit))
                act.wait_ge(act_free.sem, l * NB + jb * 8)
                nc.scalar.activation(act_h[:, 1], ps[:, 6, 0:T], ACT.Gelu_apprx_tanh).then_inc(gelu_rdy.sem, 1)

            with act.Fori(0, TB) as tb:
                for s in range(TOPK_STEPS):
                    hidden_step(tb * 4, s, gelu=s > 0)
                    if s == EXP_STEP:
                        act.wait_ge(gexp_in.sem, l * TB + tb + 1)
                        nc.scalar.activation(picked[:, 2], picked[:, 2], ACT.Exp).then_inc(gexp_rdy.sem, 1)
                act.wait_ge(pk_mm.sem, l * TB + tb + 1)
                nc.scalar.copy(pickT[:, 0:2], ps[:, 2, 0:2 * P].rearrange("p (k t) -> p k t", k=2))
                nc.scalar.copy(gres[:, 0], ps[:, 2, 2 * P:3 * P]).then_inc(pk_evac.sem, 1)
                act.wait_ge(s_free.sem, l * TB + tb + 1)
                nc.scalar.copy(s_sb[:], s_all[:, (tb + 1) // 2]).then_inc(s_next.sem, 1)
                act.wait_ge(g_st.sem, (l * TB + (tb + 1)) * 16)
                with act.Fori(0, GATE_STEPS // 8) as i:
                    for s in range(8):
                        hidden_step(tb * 4 + (i + 2), s)
                        for a in range(2):
                            Q = (l * TB + tb) * (P // 4) + (i * 16 + (2 * s + a))
                            act.wait_ge(gq_mm.sem, Q + (1 + gq_mm.credit))
                            nc.scalar.copy(g_all[:, :, bass.ds(i * 64 + (8 * s + 4 * a), 4)],
                                           ps[:, a].rearrange("p (t i) -> p i t", t=4)).then_inc(gq_evac.sem, 1)
                last_gelu(tb * 4 + 4)
            with act.Fori(4 * TB, NB // 8 - 1) as jb:
                for s in range(8):
                    hidden_step(jb, s, gelu=s > 0)
                last_gelu(jb + 1)
            for s in range(8):
                hidden_step(NB // 8 - 1, s, transpose=s < 7, gelu=s > 0)
            last_gelu(NB // 8)

            def v_hi_step(i, n, lap=0):
                M = l * NV + (i * (4 * G) + n)
                n = n % (4 * G)
                tile = n // G
                act.wait_ge(w_ld[tile].sem, (l * FILLS + (i + ((W_PER + U_PER) // WR + 1 + lap))) * 16)
                act.wait_ge(v_mm.sem, M + 1)
                nc.scalar.copy(v_hi[:, n % 4], wring[:, tile].rearrange("p k n -> p (k n)")
                               [:, (n % G) * 512:(n % G + 1) * 512]).then_inc(vhi_rdy.sem, 1)

            def w_hi_step(B, at_, p):
                act.wait_ge(w32_rdy.sem, l * NB + (B + 1))
                nc.scalar.copy(w_hi[:, at_], w32[:, p]).then_inc(whi_rdy.sem, 1)

            act.wait_ge(g_st.sem, g_st.at(l, 16 * TB))
            act.wait_ge(act_free.sem, act_free.at(l, NB))
            v_hi_step(0, 0)
            v_hi_step(0, 1)
            for b in range(G):
                w_hi_step(b, b, b % 2)

            def unit_step(i, n, last_units):
                if not (last_units and n >= 4 * G - 2):
                    v_hi_step(i, n + 2, (n + 2) // (4 * G))
                if n % 2 == 0 and not (last_units and n >= 2 * G):
                    b = n // 2 + G
                    w_hi_step(i * (2 * G) + b, b % (2 * G), b % 2)

            output_units(act, unit_step)

        act.wait_ge(xa_evac.sem, xa_evac.at(DEPTH, 0))
        norm(2 * DEPTH, None, None)
        for n in range(2 * TB):
            tb, half = divmod(n, 2)
            bank = (0, 1, 2, 3, 4, 6)[n]
            act.wait_ge(fo_mm.sem, n + 1)
            nc.scalar.copy(y_nat[:, tb, half * 512:(half + 1) * 512], ps[:, bank]).then_inc(fo_evac.sem, 1)

    @block.vector
    def _(dve):
        for sig in (xo_evac, ulo_rdy, vlo_rdy, ac_evac, xa_evac):
            dve.sem_inc(sig.sem, sig.credit)
        V = nc.vector

        def norm(N):
            ch = Chain(dve, norm_ch, N * 5, 5)
            var, std, r = norm_t[:, 0], norm_t[:, 1], norm_t[:, 2]
            dve.wait_ge(sum_mm.sem, N + 1)
            V.tensor_scalar(var, ps[:, 5, 0:T], 1.0 / D, EPS, ALU.mult, ALU.add).then_inc(var_rdy.sem, 1)
            dve.wait_ge(std_rdy.sem, N + 1)
            ch.then(V.reciprocal(r, std))
            ch.then(V.tensor_tensor(std, r, r, ALU.mult))
            ch.then(V.tensor_tensor(std, std, var, ALU.mult))
            ch.then(V.tensor_scalar(std, std, -0.5, 1.5, ALU.mult, ALU.add))
            ch.then(V.tensor_tensor(r, r, std, ALU.mult))
            ch.close()
            V.tensor_tensor(h[:], x[:], r.unsqueeze(1).to_broadcast([P, KC, T]), ALU.mult).then_inc(xn_rdy.sem, 1)

        def add_gated(gate_row, bank, k, evac):
            for v in range(2):
                last = V.scalar_tensor_tensor(x[:, k, seg_cols(v)], ps[:, bank, seg_cols(v)],
                                              mods[:, gate_row + k, v:v + 1], x[:, k, seg_cols(v)],
                                              ALU.mult, ALU.add)
            last.then_inc(evac.sem, 1)

        dve.wait_ge(const_ld.sem, 48)
        V.tensor_copy(iota4[:], iota.unsqueeze(2).to_broadcast([P, P, 4])).then_inc(iota_rdy.sem, 1)
        with dve.Fori(0, DEPTH) as l:
            norm(2 * l)
            dve.wait_ge(w_used.sem, w_used.at(l, N_ADA))
            dve.wait_ge(vec_rdy.sem, vec_rdy.at(l, 1))
            ch = Chain(dve, mods_ch, mods_ch.at(l, 0), 1)
            ch.then(V.tensor_tensor(mods[:], ps[:, 6, 0:12 * KC].rearrange("p (j v) -> p j v", v=2),
                                    vecs[:, 0:48].unsqueeze(2).to_broadcast([P, 48, 2]), ALU.add))
            ch.close()
            for which, (part_, row) in enumerate(((SC1, ROW_G1), (SC2, ROW_G2))):
                last = V.scalar_tensor_tensor(gs[:, which], mods[:, part_:part_ + KC], 1.0,
                                              vecs[:, row:row + KC].unsqueeze(2).to_broadcast([P, KC, 2]),
                                              ALU.add, ALU.mult)
            last.then_inc(mods_rdy.sem, 1)

            dve.wait_ge(pj_evac.sem, pj_evac.at(l, 6))
            ch = Chain(dve, conv_ch, conv_ch.at(l, 0), 4)
            ch.then(V.tensor_tensor(conv_u[:], branch[:, 4:6], branch[:, 0:2], ALU.mult))

            def tap(w, b):
                return vecs[:, ROW_CONV + 2 * w + b:ROW_CONV + 2 * w + b + 1]

            for b in range(2):
                last = V.tensor_scalar(y[:, b], conv_u[:, b], tap(1, b), None, ALU.mult)
            ch.then(last)
            for w, to, of in ((0, 1, 0), (2, 0, 1)):
                for b in range(2):
                    for lo, hi in SEGS:
                        n = hi - lo - 1
                        out = y[:, b, lo + to:lo + to + n]
                        last = V.scalar_tensor_tensor(out, conv_u[:, b, lo + of:lo + of + n], tap(w, b), out,
                                                      ALU.mult, ALU.add)
                ch.then(last)
            ch.close()
            V.tensor_tensor(y[:, 0:2], y[:, 0:2], branch[:, 2:4], ALU.mult)

            dve.wait_ge(pj_evac.sem, pj_evac.at(l, 8))
            ch = Chain(dve, pool_ch, pool_ch.at(l, 0), 6)
            ch.then(V.tensor_tensor(pool_s[:, :, 1:PW], pool_in[:, :, 0:PW - 1], pool_in[:, :, 1:PW], ALU.add))
            ch.then(V.tensor_tensor(pool_r[:, :, 2:PW - 1], pool_s[:, :, 1:PW - 2], pool_s[:, :, 3:PW], ALU.add))
            ch.then(V.tensor_tensor(pool_s[:, 1, 4:PW - 3], pool_r[:, 1, 2:PW - 5], pool_r[:, 1, 6:PW - 1], ALU.add))
            ch.then(V.tensor_tensor(pool_r[64:P, 1, 8:PW - 7], pool_s[64:P, 1, 4:PW - 11], pool_s[64:P, 1, 12:PW - 3],
                                    ALU.add))
            ch.then(V.tensor_copy(pool_s[64:P, :, PAD:PW - PAD], pool_r[64:P, :, PAD:PW - PAD]))
            dve.wait_ge(mix_ld.sem, mix_ld.at(l, 16))
            for v, (lo, hi) in enumerate(SEGS):
                cols = slice(SEG_AT[v], SEG_AT[v] + hi - lo)
                last = V.tensor_tensor(pool_d[:, :, lo:hi], pool_s[:, :, cols], rcnt[:, :, lo:hi], ALU.mult)
            ch.then(last)
            ch.close()
            for v, (lo, hi) in enumerate(SEGS):
                cols = slice(SEG_AT[v], SEG_AT[v] + hi - lo)
                last = V.tensor_tensor(pool_d[:, :, lo:hi], pool_d[:, :, lo:hi], pool_in[:, :, cols], ALU.subtract)
            last.then_inc(pd_rdy.sem, 1)
            dve.wait_ge(pool_mm.sem, pool_mm.at(l, 1))
            for b, bank in enumerate((4, 7)):
                last = V.tensor_scalar(y[:, 2 + b], ps[:, bank, 0:T], vecs[:, ROW_PS + b:ROW_PS + b + 1], None,
                                       ALU.mult)
            last.then_inc(branch_rdy.sem, 1)

            ch = Chain(dve, att_ch, att_ch.at(l, 0), 2 * NU)
            for n in range(NU + 1):
                if n < NU:
                    head, b, _, _ = unit(n)
                    keys = P if b == 0 else KEYS
                    dve.wait_ge(s_mm.sem, s_mm.at(l, n + 1))
                    ch.then(V.reduce_max(stat[:, n % 2, 0:1], ps[:, n % 2, 0:keys], AX.X))
                    V.tensor_scalar(stat[:, n % 2, 1:2], stat[:, n % 2, 0:1], -1.0, None, ALU.mult) \
                        .then_inc(nmax_rdy.sem, 1)
                if n >= 1:
                    m = n - 1
                    keys = P if unit(m)[1] == 0 else KEYS
                    dve.wait_ge(exp_rdy.sem, exp_rdy.at(l, m + 1))
                    ch.then(V.reciprocal(stat[:, m % 2, 3:4], stat[:, m % 2, 2:3]))
                    V.tensor_scalar(pr[:, m % 2, 0:keys], pr[:, m % 2, 0:keys], stat[:, m % 2, 3:4], None,
                                    ALU.mult).then_inc(pr_rdy.sem, 1)
            ch.close()
            for k in range(KC):
                dve.wait_ge(xo_mm.sem, xo_mm.at(l, k + 1))
                add_gated(GT1, k % 2, k, xo_evac)
            norm(2 * l + 1)

            dve.wait_ge(hh_rdy.sem, hh_rdy.at(l, 1))
            V.tensor_tensor(h_lo[:], h[:], h_hi[:].bitcast(F32), ALU.subtract).then_inc(hl_rdy.sem, 1)

            def hidden_step(jb, s):
                J = l * NB + (jb * 8 + s)
                for hh in range(2):
                    dve.wait_ge(uhi_rdy.sem, 2 * J + (hh + 3))
                    part_ = slice(4 * hh, 4 * hh + 4)
                    V.tensor_tensor(u_lo[:, (s + 1) % 2, part_], ps[:, 3 + hh].rearrange("p (k e) -> p k e", e=P),
                                    u_hi[:, (s + 1) % 2, part_].bitcast(F32), ALU.subtract) \
                        .then_inc(ulo_rdy.sem, 1)

            hidden_step(0, -1)
            with dve.Fori(0, TB) as tb:
                B = l * TB + tb
                ch = Chain(dve, route_ch, B * ROUTE_STEPS, ROUTE_STEPS)
                dve.wait_ge(sc_evac.sem, sc_evac.at(l, 4))
                dve.wait_ge(s_next.sem, B + 1)
                dve.wait_ge(iota_rdy.sem, 1)
                dve.sem_inc(dve_passed.sem, 1)
                for n in range(HP):
                    last = V.max(top_s[:, n, 0:8], s_sb[:, n])
                ch.then(last)
                hidden_step(tb * 4, 0)
                for n in range(HP):
                    last = V.match_replace(left[:, n], top_s[:, n, 0:8], s_sb[:, n], NEG)
                ch.then(last)
                hidden_step(tb * 4, 1)
                for n in range(HP):
                    V.max_index(top_iu[:, n, 0:8], top_s[:, n, 0:8], s_sb[:, n])
                hidden_step(tb * 4, 2)
                for n in range(HP):
                    last = V.max(top_s[:, n, 8:16], left[:, n])
                ch.then(last)
                hidden_step(tb * 4, 3)
                for n in range(HP):
                    last = V.max_index(top_iu[:, n, 8:16], top_s[:, n, 8:16], left[:, n])
                ch.then(last)
                hidden_step(tb * 4, 4)
                tops = top_s[:].rearrange("p (h q) k -> p h q k", q=2)
                cand = s_sb[:].rearrange("p (h q) (a b) -> p h (q a) b", q=2, b=TOPK)
                ch.then(V.tensor_tensor(cand, tops[:, :, 0].unsqueeze(3).to_broadcast([P, PH, TOPK, TOPK]),
                                        tops[:, :, 1].unsqueeze(2).to_broadcast([P, PH, TOPK, TOPK]), ALU.add))
                V.tensor_copy(top_i[:], top_iu[:])
                hidden_step(tb * 4, 5)
                cands = s_sb[:].rearrange("p (h q) k -> p h (q k)", q=2)
                lefts = left[:].rearrange("p (h q) k -> p h (q k)", q=2)
                for n in range(PH):
                    last = V.max(best[:, n, 0:8], cands[:, n])
                ch.then(last)
                hidden_step(tb * 4, 6)
                for n in range(PH):
                    last = V.match_replace(lefts[:, n], best[:, n, 0:8], cands[:, n], NEG)
                ch.then(last)
                hidden_step(tb * 4, 7)
                for n in range(PH):
                    V.max_index(best_iu[:, n, 0:8], best[:, n, 0:8], cands[:, n])
                hidden_step(tb * 4, 8)
                for n in range(PH):
                    last = V.max(best[:, n, 8:16], lefts[:, n])
                ch.then(last)
                gates = picked[:, 2].rearrange("p (h k) -> p h k", k=TOPK)
                V.tensor_tensor(gates, best[:], best[:, :, 0:1].to_broadcast([P, PH, TOPK]), ALU.subtract) \
                    .then_inc(gexp_in.sem, 1)
                hidden_step(tb * 4, 9)
                for n in range(PH):
                    last = V.max_index(best_iu[:, n, 8:16], best[:, n, 8:16], lefts[:, n])
                ch.then(last)
                hidden_step(tb * 4, 10)
                part_u = top_iu[:].rearrange("p (q h) k -> p q h k", q=2)
                V.tensor_scalar(part_u[:, 0], best_iu[:], 4, None, ALU.logical_shift_right)
                ch.then(V.tensor_scalar(part_u[:, 1], best_iu[:], TOPK - 1, None, ALU.bitwise_and))
                ch.then(V.tensor_copy(part[:], part_u))
                left4 = left[:].rearrange("p (h q) (a b) -> p h (q a) b", q=2, b=TOPK)
                keys_i = top_i[:].rearrange("p (h q) k -> p h q k", q=2)
                picks = (cand, left4)
                for q in range(2):
                    last = V.tensor_tensor(picks[q].rearrange("p h a b -> p (h a) b"),
                                           part[:, q].rearrange("p h k -> p (h k)").unsqueeze(2)
                                           .to_broadcast([P, PH * TOPK, TOPK]),
                                           iota[:, 0:TOPK].unsqueeze(1).to_broadcast([P, PH * TOPK, TOPK]),
                                           ALU.is_equal)
                ch.then(last)
                hidden_step(tb * 4, 11)
                for q in range(2):
                    last = V.tensor_tensor(picks[q], picks[q],
                                           keys_i[:, :, q].unsqueeze(2).to_broadcast([P, PH, TOPK, TOPK]), ALU.mult)
                ch.then(last)
                hidden_step(tb * 4, 12)
                dve.wait_ge(gexp_rdy.sem, B + 1)
                ch.then(V.reduce_sum(gsum[:, 0], gates, AX.X))
                ch.then(V.reciprocal(gsum[:, 1], gsum[:, 0]))
                ch.close()
                V.tensor_tensor(gates, gates, gsum[:, 1].unsqueeze(2).to_broadcast([P, PH, TOPK]), ALU.mult)
                V.reduce_sum(picked[:, 0], picks[0].rearrange("p h a b -> p (h a) b"), AX.X) \
                    .then_inc(s_free.sem, 1)
                hidden_step(tb * 4, 13)
                V.reduce_sum(picked[:, 1], picks[1].rearrange("p h a b -> p (h a) b"), AX.X) \
                    .then_inc(pk_rdy.sem, 1)
                hidden_step(tb * 4, 14)
                hidden_step(tb * 4, 15)

                dve.wait_ge(pk_evac.sem, B + 1)
                ch = Chain(dve, pt_ch, B * 4, 4)
                ch.then(V.tensor_copy(pickT[:, 2], gres[:, 0]))
                ch.then(V.tensor_tensor(gres[:, 1], gres[:, 0], pickT[:, 2], ALU.subtract))
                ch.then(V.tensor_copy(pickT[:, 3], gres[:, 1]))
                ch.then(V.tensor_tensor(pickT[:, 4], gres[:, 1], pickT[:, 3], ALU.subtract), dve_passed)
                ch.close()
                with dve.Fori(0, GATE_STEPS // 8) as i:
                    for s in range(8):
                        for a in range(2):
                            Q = B * (P // 4) + (i * 16 + (2 * s + a))
                            tok = bass.ds(i * 64 + (8 * s + 4 * a), 4)

                            def per_token(row):
                                return pickT[:, row, tok].unsqueeze(1).to_broadcast([P, P, 4])

                            dve.wait_ge(gq_mm.sem, Q + 1)
                            V.tensor_tensor(one_e[:, a], iota4[:], per_token(0), ALU.is_equal) \
                                .then_inc(oe_ch.sem, 1)
                            V.tensor_tensor(one_a[:, a], iota4[:], per_token(1), ALU.is_equal)
                            dve.wait_ge(oe_ch.sem, Q + 1)
                            for k in range(3):
                                last = V.tensor_tensor(one_b[:, a, k], one_e[:, a], per_token(2 + k), ALU.mult)
                            last.then_inc(one_rdy.sem, 1)
                        hidden_step(tb * 4 + (i + 2), s)
            with dve.Fori(4 * TB, NB // 8 - 1) as jb:
                for s in range(8):
                    hidden_step(jb, s)
            for s in range(7):
                hidden_step(NB // 8 - 1, s)

            def v_lo_step(i, n):
                M = l * NV + (i * (4 * G) + n)
                n = n % (4 * G)
                dve.wait_ge(vhi_rdy.sem, M + 1)
                V.tensor_tensor(v_lo[:, n % 4], wring[:, n // G].rearrange("p k n -> p (k n)")
                                [:, (n % G) * 512:(n % G + 1) * 512], v_hi[:, n % 4].bitcast(F32),
                                ALU.subtract).then_inc(vlo_rdy.sem, 1)

            def w_mult(B, buf, b, p):
                V.tensor_tensor(w32[:, p], act2[:, buf, b], gate2[:, buf, b], ALU.mult).then_inc(w32_rdy.sem, 1)

            def w_lo_step(B, at_, p):
                dve.wait_ge(whi_rdy.sem, l * NB + (B + 1))
                V.tensor_tensor(w_lo[:, at_], w32[:, p], w_hi[:, at_].bitcast(F32), ALU.subtract) \
                    .then_inc(wlo_rdy.sem, 1)

            v_lo_step(0, 0)
            v_lo_step(0, 1)
            dve.wait_ge(ga_ld[0].sem, ga_ld[0].at(l, 32))
            for b in range(G):
                w_mult(b, 0, b, b % 2)
                w_lo_step(b, b, b % 2)
            dve.wait_ge(acc_zero.sem, acc_zero.at(l, 1))
            dve.sem_inc(dve_passed.sem, 1)

            def add_sums(i, e):
                half = e % 2
                dve.wait_ge(v_mm.sem, l * NV + (i * (4 * G) + (G * (e + 1) + v_mm.credit)))
                dve.wait_ge(ac_evac.sem, l * (2 * NG) + (i * 4 + (e + 1)))
                for tb in range(TB):
                    cols = slice(half * 512, (half + 1) * 512)
                    last = V.tensor_tensor(acc[:, tb, cols], acc[:, tb, cols], ps[:, 3 * half + tb], ALU.add)
                last.then_inc(ac_evac.sem, 1)

            def unit_step(i, n, last_units):
                next_w = n % 2 == 0 and not (last_units and n >= 2 * G)
                b = n // 2 + G
                B = i * (2 * G) + b
                if next_w:
                    buf = (b // G) % 2
                    if b % G == 0:
                        dve.wait_ge(ga_ld[buf].sem, (l * (NG // 2) + (i + (b // (2 * G) + 1))) * 32)
                    w_mult(B, buf, b % G, b % 2)
                if not (last_units and n >= 4 * G - 2):
                    v_lo_step(i, n + 2)
                if next_w:
                    w_lo_step(B, b % (2 * G), b % 2)
                if n % G == 1 and n >= G:
                    add_sums(i, n // G - 1)
                if n == 4 * G - 1:
                    add_sums(i, 3)

            output_units(dve, unit_step)
            for k in range(KC):
                dve.wait_ge(xa_mm.sem, xa_mm.at(l, k + 1))
                add_gated(GT2, k % 2, k, xa_evac)
        norm(2 * DEPTH)

    ctx.close()


def constants():
    out = np.zeros((P, NCONST), np.float32)
    out[:, C_ID:C_ID + P] = np.eye(P)
    m = np.arange(P)
    out[m // GRID * GRID + GRID - 1 - m % GRID, C_FLIP + m] = 1.0
    out[:, C_ONE:C_ONE + P] = 1.0
    out[:, C_IOTA:C_IOTA + P] = np.arange(P)
    q = GRID - 1 - np.arange(P)[:, None] % GRID
    k = np.arange(GRID)[None, :]
    start = np.clip(q - NCOLS // 2, 0, GRID - NCOLS)
    out[:, C_MASK:C_MASK + GRID] = np.where((k >= start) & (k < start + NCOLS), 0.0, -1e30)
    for b in range(2):
        for half in range(2):
            w = 2 ** (2 * b + half + 1)
            for lo, hi in SEGS:
                t, n = np.arange(hi - lo), hi - lo
                count = np.clip(t + w - 1 - w // 2, 0, n - 1) - np.clip(t - w // 2, 0, n - 1) + 1
                out[64 * half:64 * half + 64, C_RCNT + b * T + lo:C_RCNT + b * T + hi] = 1.0 / count
    return out


INS = ["x_prompt", "x_sample", "c", "cache_k", "cache_v", "c_ctx", "norm1_g", "norm2_g", "w_ada", "b_ada",
       "w_in", "conv_w", "pool_w", "pool_scale", "rpb", "w_out", "peer_wq", "peer_subkeys", "peer_u",
       "peer_v", "final_g"]
OUTS = [(1, TCTX, D), (1, TLAT, D), (1, DEPTH, NH, TCTX, HD), (1, DEPTH, NH, TCTX, HD)]


def kernel(**inputs):
    import numpy as _np
    import concourse.bacc as _bacc
    from concourse import mybir as _mybir
    from concourse.bass_utils import run_bass_kernel_spmd as _run

    nc = _bacc.Bacc("TRN2", target_bir_lowering=False, num_devices=1)
    arrays, args = {}, []
    for name in INS + ["consts"]:
        a = _np.ascontiguousarray(constants() if name == "consts" else inputs[name])
        arrays[f"in_{name}_dram"] = a
        args.append(nc.dram_tensor(f"in_{name}_dram", a.shape, _mybir.dt.from_np(a.dtype), kind="ExternalInput").ap())
    for i, shape in enumerate(OUTS):
        args.append(nc.dram_tensor(f"out_{i}_dram", shape, F32, kind="ExternalOutput").ap())
    build(nc, *args)
    r = _run(nc, [arrays], core_ids=[0])
    return tuple(r.results[0][f"out_{i}_dram"] for i in range(len(OUTS)))
```

```python
from contextlib import ExitStack

import numpy as np

import concourse.bass as bass
from concourse import mybir

F32 = mybir.dt.float32
F32R = mybir.dt.float32r
U32 = mybir.dt.uint32
BF16 = mybir.dt.bfloat16
ALU = mybir.AluOpType
ACT = mybir.ActivationFunctionType
AX = mybir.AxisListType

P = 128
D = 1024
KC = D // P
DEPTH = 2
TCTX, TLAT = 128, 256
T = TCTX + TLAT
TB = T // P
SEGS = ((0, TCTX), (TCTX, T))
EPS = 1e-6
WCOLS = 256
AW = D // 4
CW = D // 2
NH, HD = 8, 64
SCALE = HD ** -0.5
GRID = 64
ROWS = TLAT // GRID
NCOLS = 16
DR, DC = 15, 31
TPW = 2 * GRID - 1
KEYS = TLAT + 128
PAD = 8
PW = T + 4 * PAD
SEG_AT = (PAD, TCTX + 3 * PAD)
PH, TOPK, NK = 8, 16, 128
HP = 2 * PH
NB = NK
G = 4
NG = NB // G
NEG = -3.0e38

ROW_ADA, ROW_G1, ROW_G2, ROW_PS, ROW_CONV, ROW_FG, NROWS = 0, 48, 56, 64, 66, 72, 80
SH1, SC1, GT1, SH2, SC2, GT2 = (KC * i for i in range(6))
C_ID, C_ONE, C_IOTA, C_FLIP, C_MASK, C_RCNT = 0, 128, 256, 384, 512, 576
NCONST = C_RCNT + 2 * T
N_ADA1, N_ADA2, N_IN, N_OUT, N_WQ = 8, 16, 10, 4, 8
W_IN0 = N_ADA1
W_ADA2 = W_IN0 + N_IN
W_OUT0 = W_ADA2 + N_ADA2
W_WQ0 = W_OUT0 + N_OUT
W_SK0 = W_WQ0 + N_WQ
W_PER = W_SK0 + 2
WR = 4
U_PER = NB // 2
V_PER = 2 * NG
SP_OUT0, SP_WQ0 = 2 * N_IN, 2 * (N_IN + N_OUT)
N_SPLIT = SP_WQ0 + 2 * N_WQ
assert W_PER % WR == 0 and U_PER % WR == 0 and V_PER % WR == 0
FILLS = (W_PER + U_PER + V_PER) // WR
ADA_TURN = 18
OUT_AHEAD = 21
TOPK_STEPS, GATE_STEPS = 16, 16
EXP_STEP = 11
PIECES = 8
ALONE = NB - 8
ROUTE_STEPS = 15
BASE = 16512


class Signal:

    def __init__(self, nc, ctx, name, per, credit=0):
        self.sem = ctx.enter_context(nc.semaphore(name))
        self.per, self.credit = per, credit

    def at(self, l, k):
        return l * self.per + (self.credit + k)


class Chain:

    def __init__(self, eng, sig, base, per):
        self.eng, self.sem, self.base, self.per, self.n = eng, sig.sem, base, per, 0

    def then(self, ins, passed=None):
        self.n += 1
        ins.then_inc(self.sem, 1)
        self.eng.wait_ge(self.sem, self.base + self.n)
        if passed is not None:
            self.eng.sem_inc(passed.sem, 1)

    def close(self):
        assert self.n == self.per, (self.n, self.per)


def build(nc, x_prompt, x_sample, c, cache_k, cache_v, c_ctx, norm1_g, norm2_g, w_ada, b_ada, w_in, conv_w,
          pool_w, pool_scale, rpb, w_out, peer_wq, peer_subkeys, peer_u, peer_v, final_g, consts,
          y_prompt, y_sample, new_k, new_v):
    ctx = ExitStack()
    place = [BASE]

    def at(name, shape, dtype=F32, offset=None):
        size = (2 if dtype == BF16 else 4) * int(np.prod(shape[1:]))
        if offset is None:
            offset = place[0]
            place[0] += -(-size // 32) * 32
        assert offset + size <= nc.sbuf_usable_end, (name, offset + size)
        return nc.alloc_sbuf_tensor_at(name, list(shape), dtype, offset=offset)

    cst = at("cst", [P, C_FLIP])
    x = at("x", [P, KC, T])
    h = at("h", [P, KC, T])
    wring = at("wring", [P, WR, KC, WCOLS])
    vec_nat = at("vec_nat", [P, P])
    vecs = at("vecs", [P, NROWS])
    silu_c = at("silu_c", [P, KC, 32])
    mods = at("mods", [P, 6 * KC, 2])
    gs = at("gs", [P, 2, KC, 2])
    stat = at("stat", [P, 3, 4])
    iota4 = at("iota4", [P, P, 4], BF16)
    h_hi = at("h_hi", [P, KC, T], F32R)
    h_lo = at("h_lo", [P, KC, T], F32R)
    u_hi = at("u_hi", [P, 2, KC, P], F32R)
    u_lo = at("u_lo", [P, 2, KC, P], F32R)
    arena = place[0]

    x_nat = at("x_nat", [P, TB, D], offset=arena)
    branch = at("branch", [P, 6, T])
    pool_in = at("pool_in", [P, 2, PW])
    pool_s = at("pool_s", [P, 2, PW])
    pool_r = at("pool_r", [P, 2, PW])
    pool_d = at("pool_d", [P, 2, T])
    conv_u = at("conv_u", [P, 2, T])
    qT = at("qT", [P, 4, T])
    kT = at("kT", [P, 4, T])
    vN = at("vN", [P, TB, CW])
    y = at("y", [P, KC, T])
    k_out = at("k_out", [P, CW])
    cK = at("cK", [P, CW])
    cV = at("cV", [P, CW])
    cKT = at("cKT", [P, 4, P])
    bias_tab = at("bias_tab", [P, TPW])
    bias = at("bias", [P, 2, NH, TLAT])
    norm_t = at("norm_t", [P, 3, T])
    pool_blk = at("pool_blk", [P, 2, P])
    mod_raw = at("mod_raw", [P, 8 * P])
    pr = at("pr", [P, 3, KEYS])
    prT = at("prT", [P, 2, 3, P])
    c_nat = at("c_nat", [16, P])
    mix_cst = at("mix_cst", [P, NCONST - C_FLIP])

    place[0] = arena
    act_h = at("act_h", [P, 2, T])
    hidden_end = place[0]
    s_sb = at("s_sb", [P, HP, NK])
    s_all = at("s_all", [P, TB - 1, HP, NK])
    top_s = at("top_s", [P, HP, TOPK])
    top_iu = at("top_iu", [P, HP, TOPK], U32)

    best = at("best", [P, PH, TOPK])
    best_iu = at("best_iu", [P, PH, TOPK], U32)
    part = at("part", [P, 2, PH, TOPK])
    picked = at("picked", [P, 3, PH * TOPK])
    gsum = at("gsum", [P, 2, PH])
    one_a = at("one_a", [P, 2, P, 4], BF16)
    one_e = at("one_e", [P, 2, P, 4], BF16)
    one_b = at("one_b", [P, 2, 3, P, 4], BF16)
    g_all = at("g_all", [P, NK, P])
    pq = at("pq", [P, HP, T], offset=place[0] - 4 * NK * P)
    skT = at("skT", [P, HP, NK], offset=place[0] - 4 * NK * P + 4 * HP * T)
    h_at = BASE + 4 * C_FLIP + 4 * KC * T
    left = at("left", [P, HP, NK], offset=h_at)
    pickT = at("pickT", [P, 5, P], BF16, offset=h_at + 4 * HP * NK)
    gres = at("gres", [P, 2, P], offset=h_at + 4 * HP * NK + 10 * P)
    top_i = at("top_i", [P, HP, TOPK], offset=h_at + 4 * HP * NK + 18 * P)

    place[0] = hidden_end
    v_hi = at("v_hi", [P, 4, 512], F32R)
    v_lo = at("v_lo", [P, 4, 512], F32R)
    w_hi = at("w_hi", [P, 2 * G, T], F32R)
    w_lo = at("w_lo", [P, 2 * G, T], F32R)
    gate2 = at("gate2", [P, 2, G, T])
    act2 = at("act2", [P, 2, G, T])
    w32 = at("w32", [P, 2, T])
    acc = at("acc", [P, TB, D])
    y_nat = at("y_nat", [P, TB, D], offset=arena)

    ps = ctx.enter_context(nc.psum_tensor([P, 8, 512], F32))
    tab_dram = nc.dram_tensor("bias_scratch", (NH * DR, TPW), F32)
    gate_dram = nc.dram_tensor("gate_scratch", (NK, P, T), F32).ap()
    act_dram = nc.dram_tensor("act_scratch", (NB, P, T), F32).ap()

    ident = cst[:, C_ID:C_ID + P]
    flip = mix_cst[:, 0:P]
    ones = cst[:, C_ONE:C_ONE + P]
    iota = cst[:, C_IOTA:C_IOTA + P]
    colmask = mix_cst[:, C_MASK - C_FLIP:C_RCNT - C_FLIP]
    rcnt = mix_cst[:, C_RCNT - C_FLIP:].rearrange("p (b t) -> p b t", b=2)

    bias_v = bias[:].rearrange("p a h (r c) -> p (a h r) c", c=GRID)

    def S(name, per, credit=0):
        return Signal(nc, ctx, name, per, credit)

    const_ld = S("const_ld", 0)
    x_ld = S("x_ld", 0)
    xi_mm = S("xi_mm", 0)
    xi_evac = S("xi_evac", 0)
    c_tr = S("c_tr", 0)
    silu_rdy = S("silu_rdy", 0)
    zero_rdy = S("zero_rdy", 0)
    vec_ld = S("vec_ld", 16 * 6)
    vec_tr = S("vec_tr", 1, credit=1)
    vec_rdy = S("vec_rdy", 1)
    w_ld = [S(f"w_ld{i}", 16 * FILLS) for i in range(WR)]
    mix_ld = S("mix_ld", 16)
    iota_rdy = S("iota_rdy", 0)
    w_used = S("w_used", W_PER)
    sq_rdy = S("sq_rdy", 2 * KC)
    sum_mm = S("sum_mm", 2)
    var_rdy = S("var_rdy", 2)
    std_rdy = S("std_rdy", 2)
    xn_rdy = S("xn_rdy", 2 * 4)
    h_rdy = S("h_rdy", 2 * 4)
    hv_rdy = S("hv_rdy", 2 * 4)
    norm_ch = S("norm_ch", 2 * 5)
    ada_evac = S("ada_evac", 2)
    ada_tr = S("ada_tr", 2)
    mods_rdy = S("mods_rdy", 2)
    mods_ch = S("mods_ch", 2)
    sh_rdy = S("sh_rdy", 3 * 4)
    sl_rdy = S("sl_rdy", 3 * 4)
    ch_rdy = S("ch_rdy", N_SPLIT)
    cl_rdy = S("cl_rdy", N_SPLIT)
    pj_mm = S("pj_mm", 22)
    pj_evac = S("pj_evac", 22, credit=2)
    kc_mm = S("kc_mm", 1)
    kc_evac = S("kc_evac", 1)
    kv_st = S("kv_st", 32)
    cache_ld = S("cache_ld", 32)
    ck_mm = S("ck_mm", 1)
    ck_evac = S("ck_evac", 1)
    tab_ld = S("tab_ld", 16)
    tab_st = S("tab_st", 16)
    bias_ld = S("bias_ld", 16 * ROWS * NH)
    bias_rdy = S("bias_rdy", 1)
    pad_rdy = S("pad_rdy", 1)
    poolw_ld = S("poolw_ld", 64)
    conv_ch = S("conv_ch", 4)
    pool_ch = S("pool_ch", 6)
    pd_rdy = S("pd_rdy", 1)
    pool_mm = S("pool_mm", 1)
    branch_rdy = S("branch_rdy", 1)
    NU = 3 * NH
    s_mm = S("s_mm", NU)
    att_ch = S("att_ch", 2 * NU)
    nmax_rdy = S("nmax_rdy", NU)
    exp_rdy = S("exp_rdy", NU, credit=3)
    pr_rdy = S("pr_rdy", NU)
    t_mm = S("t_mm", NU)
    t_evac = S("t_evac", NU, credit=2)
    o_mm = S("o_mm", NU)
    o_evac = S("o_evac", NU, credit=1)
    xo_mm = S("xo_mm", KC)
    xo_evac = S("xo_evac", KC, credit=2)
    pq_mm = S("pq_mm", HP)
    pq_evac = S("pq_evac", HP, credit=2)
    sk_mm = S("sk_mm", 4)
    sk_evac = S("sk_evac", 4)
    sc_mm = S("sc_mm", 4 * TB)
    sc_evac = S("sc_evac", 4 * TB)
    s_next = S("s_next", TB, credit=1)
    route_ch = S("route_ch", ROUTE_STEPS * TB)
    s_free = S("s_free", TB)
    gexp_in = S("gexp_in", TB)
    gexp_rdy = S("gexp_rdy", TB)
    pk_rdy = S("pk_rdy", TB)
    pk_mm = S("pk_mm", TB)
    pk_evac = S("pk_evac", TB)
    NQ = T // 4
    pt_ch = S("pt_ch", 4 * TB)
    oe_ch = S("oe_ch", NQ)
    one_rdy = S("one_rdy", NQ)
    gq_mm = S("gq_mm", NQ, credit=2)
    gq_evac = S("gq_evac", NQ, credit=2)
    g_st = S("g_st", 16 * PIECES * TB, credit=16)

    ut_mm = S("ut_mm", 2 * NB)
    uhi_rdy = S("uhi_rdy", 2 * NB)
    ulo_rdy = S("ulo_rdy", 2 * NB, credit=2)
    h_mm = S("h_mm", NB, credit=2)
    gelu_rdy = S("gelu_rdy", NB, credit=2)
    act_st = S("act_st", 16 * NB)
    act_free = S("act_free", NB, credit=2)
    ga_ld = [S(f"ga_ld{i}", 32 * (NG // 2)) for i in range(2)]
    w32_rdy = S("w32_rdy", NB)
    whi_rdy = S("whi_rdy", NB)
    wlo_rdy = S("wlo_rdy", NB)
    NV = 2 * NB
    vhi_rdy = S("vhi_rdy", NV)
    vlo_rdy = S("vlo_rdy", NV, credit=4 * G)
    v_mm = S("v_mm", NV, credit=4)
    ac_evac = S("ac_evac", 2 * NG, credit=2)
    acc_zero = S("acc_zero", 1)
    xa_mm = S("xa_mm", KC)
    xa_evac = S("xa_evac", KC, credit=KC)
    fo_mm = S("fo_mm", 0)
    fo_evac = S("fo_evac", 0)
    y_st = S("y_st", 0)

    dve_passed = S("dve_passed", 0)
    pool_passed = S("pool_passed", 0)
    pe_passed = S("pe_passed", 0)
    sp_passed = S("sp_passed", 0)

    block = ctx.enter_context(nc.Block())

    def seg_cols(v):
        return slice(SEGS[v][0], SEGS[v][1])

    def ada_tile(slot):
        return wring[:, slot].rearrange("p k n -> p (k n)").rearrange("p (k n) -> p k n", k=KC // 2)

    def split_tile(M):
        if M < SP_OUT0:
            return W_IN0 + M // 2
        if M < SP_WQ0:
            return W_OUT0 + (M - SP_OUT0) // 2
        return W_WQ0 + (M - SP_WQ0) // 2

    def split_source(M):
        return wring[:, split_tile(M) % WR, :, (M % 2) * P:(M % 2 + 1) * P]

    def unit(n):
        head, b = divmod(n, 3)
        return head, b, (3 if b else 1), slice(b * P, (b + 1) * P)

    def s_bank(n):
        return (0, 1, 6)[n % 3]




    def output_units(eng, unit_step):
        with eng.Fori(0, NG // 2 - 1) as i:
            for n in range(4 * G):
                unit_step(i, n, False)
        for n in range(4 * G):
            unit_step(NG // 2 - 1, n, True)

    @block.sync
    def _(sp):
        sp.sem_inc(g_st.sem, g_st.credit)
        sp.dma_start(cst[:], consts[:, 0:C_FLIP]).then_inc(const_ld.sem, 16)
        for tb, src in ((0, x_prompt[0]), (1, x_sample[0, 0:P]), (2, x_sample[0, P:2 * P])):
            sp.dma_start(x_nat[:, tb], src).then_inc(x_ld.sem, 16)
        sp.dma_start(c_nat[0:KC], c_ctx.rearrange("(k p) -> k p", p=P)).then_inc(const_ld.sem, 16)
        sp.dma_start(c_nat[KC:16], c[0].rearrange("(k p) -> k p", p=P)).then_inc(const_ld.sem, 16)
        with sp.Fori(0, DEPTH) as l:
            sp.wait_ge(vec_tr.sem, vec_tr.at(l, 0))
            for row, n, src in ((ROW_ADA, 48, b_ada), (ROW_G1, 8, norm1_g), (ROW_G2, 8, norm2_g),
                                (ROW_PS, 2, pool_scale)):
                sp.dma_start(vec_nat[row:row + n], src[l].rearrange("(k p) -> k p", p=P)) \
                  .then_inc(vec_ld.sem, 16)
            sp.dma_start(vec_nat[ROW_CONV:ROW_CONV + 6], conv_w[l].rearrange("w (k p) -> (w k) p", p=P)) \
              .then_inc(vec_ld.sem, 16)
            sp.dma_start(vec_nat[ROW_FG:ROW_FG + 8], final_g.rearrange("(k p) -> k p", p=P)) \
              .then_inc(vec_ld.sem, 16)
            for n in range(W_PER):
                for first, count, ada in ((0, N_ADA1, 0), (W_ADA2, N_ADA2, N_ADA1)):
                    if first <= n < first + count:
                        cols, half = divmod(n - first + ada, 2)
                        tile = w_ada[l, half * (D // 2):(half + 1) * (D // 2)].rearrange(
                            "(k p) n -> p k n", p=P)[:, :, cols * 512:(cols + 1) * 512]
                        dst = ada_tile(n % WR)
                for first, count, src in ((W_IN0, N_IN, w_in), (W_OUT0, N_OUT, w_out), (W_WQ0, N_WQ, peer_wq)):
                    if first <= n < first + count:
                        tile = src[l].rearrange("(k p) n -> p k n", p=P)[:, :, (n - first) * WCOLS:
                                                                         (n - first + 1) * WCOLS]
                        dst = wring[:, n % WR]
                if n >= W_SK0:
                    tile = peer_subkeys[l].rearrange("h q k d -> k (h q) d")[:, (n - W_SK0) * 8:
                                                                             (n - W_SK0 + 1) * 8]
                    dst = wring[:, n % WR].rearrange("p k n -> p (k n)")[:, 0:8 * P] \
                        .rearrange("p (s d) -> p s d", s=8)
                if n < WR:
                    sp.wait_ge(vlo_rdy.sem, vlo_rdy.at(l, G * (n + 1 - WR)))
                else:
                    sp.wait_ge(w_used.sem, w_used.at(l, n + 1 - WR))
                sp.dma_start(dst, tile).then_inc(w_ld[n % WR].sem, 16)

            def load_u(n, slot):
                sp.dma_start(wring[:, slot].rearrange("p k n -> p (k n)").rearrange("p (b d) -> p b d", b=2),
                             peer_u[l, bass.ds(n * (2 * P), 2 * P)].rearrange("(b p) d -> p b d", b=2)) \
                  .then_inc(w_ld[slot].sem, 16)

            def store_gates(tb, piece):
                keys = slice(piece * (NK // PIECES), (piece + 1) * (NK // PIECES))
                sp.dma_start(gate_dram[keys, :, bass.ds(tb * P, P)].rearrange("a b t -> b a t"), g_all[:, keys]) \
                  .then_inc(g_st.sem, 16)

            for n in range(WR):
                sp.wait_ge(w_used.sem, w_used.at(l, W_PER + n + 1 - WR))
                load_u(n, n)

            def more_u(i, gates_of=None, piece=0):
                for s in range(WR):
                    sp.wait_ge(ut_mm.sem, ut_mm.at(l, 0) + (i * (4 * WR) + 4 * (s + 1 - WR)))
                    load_u(i * WR + s, s)
                    if gates_of is not None:
                        sp.wait_ge(ut_mm.sem, ut_mm.at(l, 0) + (i * (4 * WR) + 4 * (s + 1 - WR) + 2))
                        store_gates(gates_of, piece + s)

            more_u(1)
            more_u(2)
            with sp.Fori(0, TB) as tb:
                more_u(tb * 4 + 3)
                more_u(tb * 4 + 4)
                sp.wait_ge(gq_evac.sem, gq_evac.at(l, 0) + (tb + 1) * (NQ // TB))
                more_u(tb * 4 + 5, tb, 0)
                more_u(tb * 4 + 6, tb, WR)
            more_u(4 * TB + 3)

            def load_ga(g, buf):
                for dst, src in ((gate2, gate_dram), (act2, act_dram)):
                    sp.dma_start(dst[:, buf], src[bass.ds(g * G, G)].rearrange("b e t -> e b t")) \
                      .then_inc(ga_ld[buf].sem, 16)

            def load_v(g, half, slot):
                sp.dma_start(wring[:, slot].rearrange("p k n -> p (k n)").rearrange("p (b d) -> p b d", b=G),
                             peer_v[l, bass.ds(g * (G * P), G * P), half * 512:(half + 1) * 512]
                             .rearrange("(b p) d -> p b d", b=G)).then_inc(w_ld[slot].sem, 16)

            sp.wait_ge(g_st.sem, g_st.at(l, 16 * PIECES * TB))
            sp.wait_ge(act_st.sem, act_st.at(l, 16 * 2 * G))
            sp.sem_inc(sp_passed.sem, 1)
            load_ga(0, 0)
            load_ga(1, 1)
            for n in range(WR):
                sp.wait_ge(ut_mm.sem, ut_mm.at(l, 2 * NB + 4 * (n + 1 - WR)))
                load_v(n // 2, n % 2, n)
            sp.wait_ge(act_st.sem, act_st.at(l, 16 * NB))
            sp.sem_inc(sp_passed.sem, 1)

            def group_loads(g, n, ga=True):
                if ga:
                    sp.wait_ge(w32_rdy.sem, l * NB + (g - 1) * G)
                    load_ga(g, n)
                for half in range(2):
                    slot = 2 * n + half
                    sp.wait_ge(vlo_rdy.sem, l * NV + (g * (2 * G) + (G * (half - 3) + vlo_rdy.credit)))
                    load_v(g, half, slot)

            with sp.Fori(1, NG // 2) as i:
                for n in range(2):
                    group_loads(i * 2 + n, n)
        for tb, dst in ((0, y_prompt[0]), (1, y_sample[0, 0:P]), (2, y_sample[0, P:2 * P])):
            sp.wait_ge(fo_evac.sem, 2 * (tb + 1))
            sp.dma_start(dst, y_nat[:, tb]).then_inc(y_st.sem, 16)
        sp.wait_ge(y_st.sem, 16 * TB)

    @block.gpsimd
    def _(pool):
        pool.sem_inc(act_free.sem, act_free.credit)
        nc.gpsimd.memset(silu_c[:], 0.0).then_inc(zero_rdy.sem, 1)
        with pool.Fori(0, DEPTH) as l:
            pool.wait_ge(xa_evac.sem, xa_evac.at(l, 0))
            pool.sem_inc(pool_passed.sem, 1)
            pool.wait_ge(xi_evac.sem, 2 * TB)
            pool.sem_inc(pool_passed.sem, 1)
            pool.dma_start(mix_cst[:], consts[:, C_FLIP:]).then_inc(mix_ld.sem, 16)
            nc.gpsimd.memset(bias_tab[:], 0.0)
            nc.gpsimd.memset(pool_blk[:], 0.0)
            nc.gpsimd.memset(pool_in[:], 0.0).then_inc(pad_rdy.sem, 1)
            pool.wait_ge(pad_rdy.sem, pad_rdy.at(l, 1))
            pool.sem_inc(pool_passed.sem, 1)
            pool.dma_start(bias_tab[0:NH * DR, GRID - NCOLS:GRID - NCOLS + DC],
                           rpb[l].rearrange("h r c -> (h r) c")).then_inc(tab_ld.sem, 16)
            for g in range(4):
                half = slice((g % 2) * 64, (g % 2) * 64 + 64)
                pool.dma_start(pool_blk[half, g // 2, half], pool_w[l, g]).then_inc(poolw_ld.sem, 16)
            pool.dma_start(cK[:].rearrange("m (h d) -> m h d", h=NH), cache_k[0, l].rearrange("h m d -> m h d")) \
                .then_inc(cache_ld.sem, 16)
            pool.dma_start(cV[:].rearrange("m (h d) -> m h d", h=NH), cache_v[0, l].rearrange("h m d -> m h d")) \
                .then_inc(cache_ld.sem, 16)
            pool.wait_ge(tab_ld.sem, tab_ld.at(l, 16))
            pool.sem_inc(pool_passed.sem, 1)
            pool.dma_start(tab_dram.ap(), bias_tab[0:NH * DR, :]).then_inc(tab_st.sem, 16)
            pool.wait_ge(tab_st.sem, tab_st.at(l, 16))
            pool.sem_inc(pool_passed.sem, 1)
            for r in range(ROWS):
                for hd in range(NH):
                    src = bass.AP(tab_dram, (hd * DR + 7 - r) * TPW, [[1, GRID], [TPW, ROWS], [1, GRID]])
                    dst = bias[(r % 2) * GRID:(r % 2 + 1) * GRID, r // 2, hd].rearrange(
                        "p (a b) -> p a b", a=ROWS)
                    pool.dma_start(dst, src).then_inc(bias_ld.sem, 16)
            pool.wait_ge(bias_ld.sem, bias_ld.at(l, 16 * ROWS * NH))
            pool.sem_inc(pool_passed.sem, 1)
            pool.wait_ge(mix_ld.sem, mix_ld.at(l, 16))
            pool.sem_inc(pool_passed.sem, 1)
            nc.gpsimd.tensor_tensor(bias_v, bias_v, colmask.unsqueeze(1).to_broadcast([P, 2 * NH * ROWS, GRID]),
                                    ALU.add).then_inc(bias_rdy.sem, 1)
            pool.wait_ge(pj_evac.sem, pj_evac.at(l, 22))
            pool.sem_inc(pool_passed.sem, 1)
            pool.dma_start(new_v[0, l].rearrange("h t d -> t h d"),
                           vN[:, 0].rearrange("t (h d) -> t h d", h=NH)).then_inc(kv_st.sem, 16)
            pool.wait_ge(kc_evac.sem, kc_evac.at(l, 1))
            pool.sem_inc(pool_passed.sem, 1)
            pool.dma_start(new_k[0, l].rearrange("h t d -> t h d"),
                           k_out[:].rearrange("t (h d) -> t h d", h=NH)).then_inc(kv_st.sem, 16)
            pool.wait_ge(kv_st.sem, kv_st.at(l, 32))
            pool.sem_inc(pool_passed.sem, 1)
            def store_acts(first, last):
                with pool.Fori(first // 2, last // 2) as i:
                    for b in range(2):
                        pool.wait_ge(gelu_rdy.sem, l * NB + (i * 2 + (b + 1 + gelu_rdy.credit)))
                        pool.sem_inc(pool_passed.sem, 1)
                        pool.dma_start(act_dram[i * 2 + b], act_h[:, b]).then_inc(act_st.sem, 16)
                        pool.wait_ge(act_st.sem, (l * NB + (i * 2 + (b + 1))) * 16)
                        pool.sem_inc(act_free.sem, 1)

            store_acts(0, ALONE)
            pool.wait_ge(g_st.sem, g_st.at(l, 16 * PIECES * TB))
            pool.sem_inc(pool_passed.sem, 1)
            nc.gpsimd.memset(acc[:], 0.0).then_inc(acc_zero.sem, 1)
            store_acts(ALONE, NB)

    @block.tensor
    def _(pe):
        for sig in (vec_tr, gq_mm, h_mm, v_mm):
            pe.sem_inc(sig.sem, sig.credit)

        def sums(N, blocks):
            for k in blocks:
                pe.wait_ge(sq_rdy.sem, N * KC + (k + 1))
                last = nc.tensor.matmul(ps[:, 5, 0:T], ones, h[:, k], start=(k == 0), stop=(k == KC - 1))
                if k == KC - 1:
                    last.then_inc(sum_mm.sem, 1)

        pe.wait_ge(const_ld.sem, 48)
        pe.wait_ge(x_ld.sem, 16 * TB)
        nc.tensor.transpose(ps[:, 7, 0:16], c_nat[:], ident[0:16, 0:16]).then_inc(c_tr.sem, 1)
        for n in range(2 * TB):
            tb, half = divmod(n, 2)
            for k in range(4):
                src = x_nat[:, tb, (half * 4 + k) * P:(half * 4 + k + 1) * P]
                last = nc.tensor.transpose(ps[:, n, k * P:(k + 1) * P], src, ident)
            last.then_inc(xi_mm.sem, 1)

        with pe.Fori(0, DEPTH) as l:
            pe.wait_ge(vec_ld.sem, vec_ld.at(l, 16 * 6))
            pe.wait_ge(silu_rdy.sem, 1)
            nc.tensor.transpose(ps[:, 7, 0:NROWS], vec_nat[0:NROWS], ident[0:NROWS, 0:NROWS]) \
                .then_inc(vec_tr.sem, 1)
            sums(2 * l, range(KC))

            def tile_in(n):
                pe.wait_ge(w_ld[n % WR].sem, w_ld[n % WR].at(l, 16 * (n // WR + 1)))
                return wring[:, n % WR]

            def modulation(n, t, banks):
                tile_in(n)
                w = ada_tile(n % WR)
                cols, half = divmod(t, 2)
                out = slice((cols % 4) * P, (cols % 4 + 1) * P)
                for k in range(KC // 2):
                    for j in range(4):
                        last = nc.tensor.matmul(ps[32 * j:32 * j + 32, banks[cols // 4], out],
                                                silu_c[:, half * (KC // 2) + k], w[:, k, j * P:(j + 1) * P],
                                                start=(half == 0 and k == 0),
                                                stop=(half == 1 and k == KC // 2 - 1))
                last.then_inc(w_used.sem, 1)

            def modulation_turned(part_, banks):
                pe.wait_ge(ada_evac.sem, ada_evac.at(l, part_ + 1))
                for i, bank in enumerate(banks):
                    for k in range(4):
                        at_ = (4 * i + k) * P
                        last = nc.tensor.transpose(ps[:, bank, k * P:(k + 1) * P], mod_raw[:, at_:at_ + P], ident)
                last.then_inc(ada_tr.sem, 1)

            for n in range(N_ADA1):
                modulation(n, n, (6,))
            modulation_turned(0, (6,))

            def columns_split(M):
                pe.wait_ge(cl_rdy.sem, cl_rdy.at(l, M + 1))
                if M % 2:
                    pe.sem_inc(w_used.sem, 1)

            def column_blocks(first, count, mm, evac, moving, after=None):
                for m in range(count):
                    columns_split(first + m)
                    pe.wait_ge(evac.sem, evac.at(l, m - 1))
                    for k in range(KC):
                        if m == 0 and k % 2 == 0:
                            pe.wait_ge(sl_rdy.sem, sl_rdy.at(l, 4 * moving + k // 2 + 1))
                        for n, (w, hx) in enumerate(((u_hi, h_lo), (u_hi, h_hi), (u_lo, h_hi))):
                            last = nc.tensor.matmul(ps[:, m % 2, 0:T], w[:, m % 2, k], hx[:, k],
                                                    start=(k == 0 and n == 0), stop=(k == KC - 1 and n == 2))
                    last.then_inc(mm.sem, 1)
                    if after is not None:
                        after(m)

            column_blocks(0, 16, pj_mm, pj_evac, 0)
            for n in range(2):
                columns_split(16 + 2 * n)
                columns_split(17 + 2 * n)
                for tb in range(TB):
                    m = 16 + n * TB + tb
                    cols = slice(tb * P, (tb + 1) * P)
                    out = ps[:, m % 2, 0:WCOLS].rearrange("p (b n) -> p b n", b=2)
                    pe.wait_ge(pj_evac.sem, pj_evac.at(l, m - 1))
                    for k in range(KC):
                        for i, (hx, w) in enumerate(((h_lo, u_hi), (h_hi, u_hi), (h_hi, u_lo))):
                            last = nc.tensor.matmul(out, hx[:, k, cols], w[:, :, k],
                                                    start=(k == 0 and i == 0), stop=(k == KC - 1 and i == 2))
                    last.then_inc(pj_mm.sem, 1)
            pe.wait_ge(pj_evac.sem, pj_evac.at(l, 16))
            pe.wait_ge(xn_rdy.sem, xn_rdy.at(l, 1))
            for k in range(4):
                last = nc.tensor.transpose(ps[:, 5, k * P:(k + 1) * P], kT[:, k, 0:P], ident)
            last.then_inc(kc_mm.sem, 1)
            pe.wait_ge(cache_ld.sem, cache_ld.at(l, 32))
            pe.wait_ge(mods_rdy.sem, mods_rdy.at(l, 1))
            for k in range(4):
                last = nc.tensor.transpose(ps[:, 6, k * P:(k + 1) * P], cK[:, k * P:(k + 1) * P], ident)
            last.then_inc(ck_mm.sem, 1)
            pe.wait_ge(poolw_ld.sem, poolw_ld.at(l, 64))
            pe.wait_ge(vec_rdy.sem, vec_rdy.at(l, 1))
            pe.wait_ge(pd_rdy.sem, pd_rdy.at(l, 1))
            for b, bank in enumerate((4, 7)):
                last = nc.tensor.matmul(ps[:, bank, 0:T], pool_blk[:, b], pool_d[:, b], start=True, stop=True)
            last.then_inc(pool_mm.sem, 1)

            pe.wait_ge(pj_evac.sem, pj_evac.at(l, 22))
            pe.wait_ge(ck_evac.sem, ck_evac.at(l, 1))
            pe.wait_ge(kc_evac.sem, kc_evac.at(l, 1))
            pe.wait_ge(branch_rdy.sem, branch_rdy.at(l, 1))

            def scores(n):
                head, b, _, q_cols = unit(n)
                rows = slice((head % 2) * HD, (head % 2 + 1) * HD)
                q = qT[rows, head // 2, q_cols]
                pe.wait_ge(exp_rdy.sem, exp_rdy.at(l, n - 2))
                bank = s_bank(n)
                if b == 0:
                    nc.tensor.matmul(ps[:, bank, 0:P], q, kT[rows, head // 2, 0:TCTX], start=True, stop=True) \
                        .then_inc(s_mm.sem, 1)
                else:
                    nc.tensor.matmul(ps[:, bank, 0:TLAT], flip, bias[:, b - 1, head], start=True, stop=False)
                    nc.tensor.matmul(ps[:, bank, 0:TLAT], q, kT[rows, head // 2, TCTX:T], start=False, stop=True)
                    nc.tensor.matmul(ps[:, bank, TLAT:KEYS], q, cKT[rows, head // 2], start=True, stop=True) \
                        .then_inc(s_mm.sem, 1)

            pe.wait_ge(bias_rdy.sem, bias_rdy.at(l, 1))
            scores(0)
            scores(1)
            for n in range(NU + 1):
                if n + 2 < NU:
                    scores(n + 2)
                if n < N_ADA2:
                    modulation(W_ADA2 + n, n, (4, 7))
                if n == ADA_TURN:
                    modulation_turned(1, (4, 7))
                if n < NU:
                    head, b, blocks, _ = unit(n)
                    pe.wait_ge(pr_rdy.sem, pr_rdy.at(l, n + 1))
                    pe.wait_ge(t_evac.sem, t_evac.at(l, n - 1))
                    for k in range(blocks):
                        last = nc.tensor.transpose(ps[:, 2 + n % 2, k * P:(k + 1) * P],
                                                   pr[:, n % 3, k * P:(k + 1) * P], ident)
                    last.then_inc(t_mm.sem, 1)
                if n >= 1:
                    m = n - 1
                    head, b, blocks, _ = unit(m)
                    pair = slice((head // 2) * P, (head // 2 + 1) * P)
                    values = [vN[:, 0, pair]] if b == 0 else [vN[:, 1, pair], vN[:, 2, pair], cV[:, pair]]
                    pe.wait_ge(t_evac.sem, t_evac.at(l, m + 1))
                    pe.wait_ge(o_evac.sem, o_evac.at(l, m))
                    for k in range(blocks):
                        last = nc.tensor.matmul(ps[:, 5, 0:P], values[k], prT[:, m % 2, k],
                                                start=(k == 0), stop=(k == blocks - 1))
                    last.then_inc(o_mm.sem, 1)

            pe.wait_ge(o_evac.sem, o_evac.at(l, NU))
            column_blocks(SP_OUT0, KC, xo_mm, xo_evac, 1,
                          after=lambda m: sums(2 * l + 1, [m - 2] if m >= 2 else []))
            sums(2 * l + 1, (KC - 2, KC - 1))
            column_blocks(SP_WQ0, HP, pq_mm, pq_evac, 2)
            for n in range(4):
                tile = W_SK0 + n // 2
                w = tile_in(tile)[:].rearrange("p k n -> p (k n)")
                for k in range(4):
                    at_ = ((n % 2) * 4 + k) * P
                    last = nc.tensor.transpose(ps[:, (2, 3, 4, 7)[n], k * P:(k + 1) * P], w[:, at_:at_ + P], ident)
                last.then_inc(sk_mm.sem, 1)
                if n % 2:
                    pe.wait_ge(sk_mm.sem, sk_mm.at(l, n + 1))
                    pe.sem_inc(w_used.sem, 1)

            def route_scores(tb):
                for n in range(4):
                    if tb:
                        pe.wait_ge(sc_evac.sem, sc_evac.at(l, 4 * (tb - 1) + n + 1))
                    for k in range(4):
                        hp = 4 * n + k
                        last = nc.tensor.matmul(ps[:, n, k * P:(k + 1) * P], pq[:, hp, tb * P:(tb + 1) * P],
                                                skT[:, hp], start=True, stop=True)
                    last.then_inc(sc_mm.sem, 1)

            pe.wait_ge(pq_evac.sem, pq_evac.at(l, HP))
            pe.wait_ge(sk_evac.sem, sk_evac.at(l, 4))
            for tb in range(TB):
                route_scores(tb)

            def hidden_step(jb, s, transpose=True):
                J = l * NB + (jb * 8 + s)
                if transpose:
                    slot, b = ((s + 1) // 2) % WR, (s + 1) % 2
                    if b == 0:
                        pe.wait_ge(w_ld[slot].sem, (l * FILLS + (jb + (W_PER // WR + (s + 1) // 8 + 1))) * 16)
                    rows = wring[:, slot].rearrange("p k n -> p (k n)")
                    for hh in range(2):
                        pe.wait_ge(ulo_rdy.sem, 2 * J + (hh + 3))
                        for k in range(4):
                            at_ = b * D + (4 * hh + k) * P
                            last = nc.tensor.transpose(ps[:, 3 + hh, k * P:(k + 1) * P], rows[:, at_:at_ + P], ident)
                        last.then_inc(ut_mm.sem, 1)
                if s >= 0:
                    pe.wait_ge(ulo_rdy.sem, 2 * J + (2 + ulo_rdy.credit))
                    pe.wait_ge(gelu_rdy.sem, J + 1)
                    for k in range(KC):
                        for n, (u, hx) in enumerate(((u_hi, h_lo), (u_hi, h_hi), (u_lo, h_hi))):
                            last = nc.tensor.matmul(ps[:, 5 + s % 2, 0:T], u[:, s % 2, k], hx[:, k],
                                                    start=(k == 0 and n == 0), stop=(k == KC - 1 and n == 2))
                    last.then_inc(h_mm.sem, 1)

            pe.wait_ge(sc_evac.sem, sc_evac.at(l, 4 * TB))
            hidden_step(0, -1)
            with pe.Fori(0, TB) as tb:
                for s in range(TOPK_STEPS):
                    hidden_step(tb * 4, s)
                pe.wait_ge(pk_rdy.sem, l * TB + tb + 1)
                for k in range(3):
                    last = nc.tensor.transpose(ps[:, 2, k * P:(k + 1) * P], picked[:, k], ident)
                last.then_inc(pk_mm.sem, 1)
                with pe.Fori(0, GATE_STEPS // 8) as i:
                    for s in range(8):
                        hidden_step(tb * 4 + (i + 2), s)
                        for a in range(2):
                            Q = (l * TB + tb) * (P // 4) + (i * 16 + (2 * s + a))
                            pe.wait_ge(one_rdy.sem, Q + 1)
                            pe.wait_ge(gq_evac.sem, Q + 1)
                            for k in range(4):
                                for n in range(3):
                                    last = nc.tensor.matmul(ps[:, a, k * P:(k + 1) * P], one_a[:, a, :, k],
                                                            one_b[:, a, n, :, k], start=(n == 0), stop=(n == 2))
                            last.then_inc(gq_mm.sem, 1)
            with pe.Fori(4 * TB, NB // 8 - 1) as jb:
                for s in range(8):
                    hidden_step(jb, s)
            for s in range(8):
                hidden_step(NB // 8 - 1, s, s < 7)

            def unit_step(i, n, last_units):
                M = l * NV + (i * (4 * G) + n)
                group, half, b = n // (2 * G), (n // G) % 2, n % G
                bank = 3 * half
                pe.wait_ge(vlo_rdy.sem, M + (1 + vlo_rdy.credit))
                pe.wait_ge(wlo_rdy.sem, l * NB + (i * (2 * G) + (group * G + b + 1)))
                if n == G:
                    pe.wait_ge(gelu_rdy.sem, gelu_rdy.at(l, NB))
                if b == 0:
                    pe.wait_ge(ac_evac.sem, l * (2 * NG) + (i * 4 + (2 * group + half + 1)))
                for tb in range(TB):
                    cols = slice(tb * P, (tb + 1) * P)
                    for k, (w, v) in enumerate(((w_hi, v_lo), (w_hi, v_hi), (w_lo, v_hi))):
                        last = nc.tensor.matmul(ps[:, bank + tb], w[:, group * G + b, cols], v[:, n % 4],
                                                start=(b == 0 and k == 0), stop=(b == G - 1 and k == 2))
                last.then_inc(v_mm.sem, 1)

            pe.wait_ge(gq_evac.sem, gq_evac.at(l, NQ))
            pe.wait_ge(pk_evac.sem, pk_evac.at(l, TB))
            pe.sem_inc(pe_passed.sem, 1)
            output_units(pe, unit_step)
            for k in range(KC):
                pe.wait_ge(ac_evac.sem, ac_evac.at(l, 2 * NG))
                pe.wait_ge(xa_evac.sem, xa_evac.at(l, k - 1))
                for tb in range(TB):
                    last = nc.tensor.transpose(ps[:, k % 2, tb * P:(tb + 1) * P], acc[:, tb, k * P:(k + 1) * P],
                                               ident)
                last.then_inc(xa_mm.sem, 1)

        sums(2 * DEPTH, range(KC))
        pe.wait_ge(h_rdy.sem, 4 * (2 * DEPTH + 1))
        pe.wait_ge(hv_rdy.sem, 4 * (2 * DEPTH + 1))
        for n in range(2 * TB):
            tb, half = divmod(n, 2)
            bank = (0, 1, 2, 3, 4, 6)[n]
            for k in range(4):
                last = nc.tensor.transpose(ps[:, bank, k * P:(k + 1) * P], h[:, half * 4 + k, tb * P:(tb + 1) * P],
                                           ident)
            last.then_inc(fo_mm.sem, 1)

    @block.scalar
    def _(act):
        for sig in (pj_evac, exp_rdy, t_evac, o_evac, pq_evac, s_next, gq_evac, gelu_rdy):
            act.sem_inc(sig.sem, sig.credit)



        def squares(x_in, l, rise, blocks=range(KC)):
            for k in blocks:
                act.wait_ge(x_in.sem, x_in.at(l, rise + k + 1))
                nc.scalar.activation(h[:, k], x[:, k], ACT.Square).then_inc(sq_rdy.sem, 1)



        def root(N):
            act.wait_ge(var_rdy.sem, N + 1)
            nc.scalar.activation(norm_t[:, 1], norm_t[:, 0], ACT.Sqrt).then_inc(std_rdy.sem, 1)

        def high(l, i, src, pair):
            blocks = slice(2 * pair, 2 * pair + 2)
            nc.scalar.copy(h_hi[:, blocks], src[:, blocks]).then_inc(sh_rdy.sem, 1)

        def columns_high(l, M):
            n = split_tile(M)
            act.wait_ge(w_ld[n % WR].sem, w_ld[n % WR].at(l, 16 * (n // WR + 1)))
            nc.scalar.copy(u_hi[:, M % 2], split_source(M)).then_inc(ch_rdy.sem, 1)

        def norm(N, l, which):
            if which is not None:
                act.wait_ge(mods_rdy.sem, mods_rdy.at(l, which + 1))
            for pair in range(4):
                k = 2 * pair
                act.wait_ge(xn_rdy.sem, N * 4 + (pair + 1))
                if which is None:
                    last = nc.scalar.activation(h[:, k], h[:, k], ACT.Copy, scale=vecs[:, ROW_FG + k:ROW_FG + k + 1])
                else:
                    shift = (SH1, SH2)[which]
                    for v in range(2):
                        last = nc.scalar.activation(h[:, k, seg_cols(v)], h[:, k, seg_cols(v)], ACT.Identity,
                                                    scale=gs[:, which, k, v:v + 1],
                                                    bias=mods[:, shift + k, v:v + 1])
                last.then_inc(h_rdy.sem, 1)
                if which is not None:
                    act.wait_ge(h_rdy.sem, N * 4 + (pair + 1))
                    act.wait_ge(hv_rdy.sem, N * 4 + (pair + 1))
                    high(l, 2 * which, h, pair)

        for n in range(2 * TB):
            tb, half = divmod(n, 2)
            act.wait_ge(xi_mm.sem, n + 1)
            nc.scalar.copy(x[:, half * 4:half * 4 + 4, tb * P:(tb + 1) * P],
                           ps[:, n].rearrange("p (k t) -> p k t", t=P)).then_inc(xi_evac.sem, 1)
        act.wait_ge(c_tr.sem, 1)
        act.wait_ge(zero_rdy.sem, 1)
        nc.scalar.activation(silu_c[:, :, 0:2], ps[:, 7, 0:16].rearrange("p (v k) -> p k v", v=2), ACT.Silu) \
            .then_inc(silu_rdy.sem, 1)

        with act.Fori(0, DEPTH) as l:
            act.wait_ge(xi_evac.sem, 2 * TB)
            squares(xa_evac, l, -KC)
            act.wait_ge(vec_tr.sem, vec_tr.at(l, 1))
            nc.scalar.copy(vecs[:], ps[:, 7, 0:NROWS]).then_inc(vec_rdy.sem, 1)
            root(2 * l)
            act.wait_ge(w_used.sem, w_used.at(l, N_ADA1))
            nc.scalar.copy(mod_raw[:, 0:4 * P], ps[:, 6]).then_inc(ada_evac.sem, 1)
            columns_high(l, 0)
            columns_high(l, 1)
            norm(2 * l, l, 0)
            for m in range(22):
                act.wait_ge(pj_mm.sem, pj_mm.at(l, m + 1))
                src = ps[:, m % 2, 0:T]
                if m < 6:
                    last = nc.scalar.copy(branch[:, m], src)
                elif m < 8:
                    if m == 6:
                        act.wait_ge(pad_rdy.sem, pad_rdy.at(l, 1))
                    for v in range(2):
                        w = SEGS[v][1] - SEGS[v][0]
                        last = nc.scalar.copy(pool_in[:, m - 6, SEG_AT[v]:SEG_AT[v] + w], src[:, seg_cols(v)])
                elif m < 12:
                    last = nc.scalar.activation(qT[:, m - 8], src, ACT.Copy, scale=SCALE)
                elif m < 16:
                    last = nc.scalar.copy(kT[:, m - 12], src)
                else:
                    n, tb = divmod(m - 16, TB)
                    last = nc.scalar.copy(vN[:, tb, n * WCOLS:(n + 1) * WCOLS], ps[:, m % 2, 0:WCOLS])
                last.then_inc(pj_evac.sem, 1)
                if m < 16:
                    columns_high(l, m + 2)
                if m == 18:
                    columns_high(l, 18)
                    columns_high(l, 19)
            act.wait_ge(kc_mm.sem, kc_mm.at(l, 1))
            nc.scalar.copy(k_out[:], ps[:, 5]).then_inc(kc_evac.sem, 1)
            act.wait_ge(ck_mm.sem, ck_mm.at(l, 1))
            nc.scalar.copy(cKT[:].rearrange("p k m -> p (k m)"), ps[:, 6]).then_inc(ck_evac.sem, 1)
            for n in range(NU + 2):
                if n == 0:
                    act.wait_ge(branch_rdy.sem, branch_rdy.at(l, 1))
                    high(l, 1, y, 0)
                    high(l, 1, y, 1)
                if n == OUT_AHEAD:
                    columns_high(l, SP_OUT0)
                    columns_high(l, SP_OUT0 + 1)
                if n < NU:
                    keys = P if unit(n)[1] == 0 else KEYS
                    act.wait_ge(nmax_rdy.sem, nmax_rdy.at(l, n + 1))
                    nc.scalar.activation(pr[:, n % 3, 0:keys], ps[:, s_bank(n), 0:keys], ACT.Exp,
                                         bias=stat[:, n % 3, 1:2], accum_out=stat[:, n % 3, 2:3]) \
                        .then_inc(exp_rdy.sem, 1)
                if n == ADA_TURN:
                    act.wait_ge(w_used.sem, w_used.at(l, W_ADA2 + N_ADA2))
                    for i, bank in enumerate((4, 7)):
                        last = nc.scalar.copy(mod_raw[:, i * 4 * P:(i + 1) * 4 * P], ps[:, bank])
                    last.then_inc(ada_evac.sem, 1)
                if 1 <= n <= NU:
                    m = n - 1
                    cols = unit(m)[2] * P
                    act.wait_ge(t_mm.sem, t_mm.at(l, m + 1))
                    if m >= 2:
                        act.wait_ge(o_mm.sem, o_mm.at(l, m - 1))
                    nc.scalar.copy(prT[:, m % 2].rearrange("p k q -> p (k q)")[:, 0:cols],
                                   ps[:, 2 + m % 2, 0:cols]).then_inc(t_evac.sem, 1)
                if n >= 2:
                    m = n - 2
                    head, _, _, q_cols = unit(m)
                    rows = slice((head % 2) * HD, (head % 2 + 1) * HD)
                    act.wait_ge(o_mm.sem, o_mm.at(l, m + 1))
                    nc.scalar.copy(y[rows, 4 + head // 2, q_cols], ps[rows, 5, 0:P]) \
                        .then_inc(o_evac.sem, 1)
                if n in (NU // 2 + 1, NU + 1):
                    act.wait_ge(o_evac.sem, o_evac.at(l, n - 1))
                    high(l, 1, y, 2 if n < NU else 3)
            for m in range(KC):
                act.wait_ge(xo_mm.sem, xo_mm.at(l, m + 1))
                columns_high(l, SP_OUT0 + 2 + m)
                squares(xo_evac, l, 0, (m,))
            root(2 * l + 1)
            norm(2 * l + 1, l, 1)
            act.wait_ge(kv_st.sem, kv_st.at(l, 32))
            for m in range(HP):
                act.wait_ge(pq_mm.sem, pq_mm.at(l, m + 1))
                nc.scalar.copy(pq[:, m], ps[:, m % 2, 0:T]).then_inc(pq_evac.sem, 1)
                if m < HP - 2:
                    columns_high(l, SP_WQ0 + 2 + m)
            for n in range(4):
                act.wait_ge(sk_mm.sem, sk_mm.at(l, n + 1))
                nc.scalar.copy(skT[:, 4 * n:4 * n + 4].rearrange("p s k -> p (s k)"), ps[:, (2, 3, 4, 7)[n]]) \
                    .then_inc(sk_evac.sem, 1)

            for tb in range(TB):
                to = s_sb if tb == 0 else s_all[:, tb - 1]
                for n in range(4):
                    act.wait_ge(sc_mm.sem, sc_mm.at(l, 4 * tb + n + 1))
                    nc.scalar.copy(to[:, 4 * n:4 * n + 4].rearrange("p s k -> p (s k)"), ps[:, n]) \
                        .then_inc(sc_evac.sem, 1)

            def hidden_step(jb, s, transpose=True, gelu=True):
                J = l * NB + (jb * 8 + s)
                if gelu:
                    p = (s - 1) % 2
                    act.wait_ge(h_mm.sem, J + h_mm.credit)
                    act.wait_ge(act_free.sem, J)
                    nc.scalar.activation(act_h[:, p], ps[:, 5 + p, 0:T], ACT.Gelu_apprx_tanh) \
                        .then_inc(gelu_rdy.sem, 1)
                if transpose:
                    for hh in range(2):
                        act.wait_ge(ut_mm.sem, 2 * J + (hh + 3))
                        act.wait_ge(h_mm.sem, J + h_mm.credit)
                        nc.scalar.copy(u_hi[:, (s + 1) % 2, 4 * hh:4 * hh + 4],
                                       ps[:, 3 + hh].rearrange("p (k e) -> p k e", e=P)).then_inc(uhi_rdy.sem, 1)

            hidden_step(0, -1, gelu=False)

            def last_gelu(jb):
                act.wait_ge(h_mm.sem, l * NB + (jb * 8 + h_mm.credit))
                act.wait_ge(act_free.sem, l * NB + jb * 8)
                nc.scalar.activation(act_h[:, 1], ps[:, 6, 0:T], ACT.Gelu_apprx_tanh).then_inc(gelu_rdy.sem, 1)

            with act.Fori(0, TB) as tb:
                for s in range(TOPK_STEPS):
                    hidden_step(tb * 4, s, gelu=s > 0)
                    if s == EXP_STEP:
                        act.wait_ge(gexp_in.sem, l * TB + tb + 1)
                        nc.scalar.activation(picked[:, 2], picked[:, 2], ACT.Exp).then_inc(gexp_rdy.sem, 1)
                act.wait_ge(pk_mm.sem, l * TB + tb + 1)
                nc.scalar.copy(pickT[:, 0:2], ps[:, 2, 0:2 * P].rearrange("p (k t) -> p k t", k=2))
                nc.scalar.copy(gres[:, 0], ps[:, 2, 2 * P:3 * P]).then_inc(pk_evac.sem, 1)
                act.wait_ge(s_free.sem, l * TB + tb + 1)
                nc.scalar.copy(s_sb[:], s_all[:, (tb + 1) // 2]).then_inc(s_next.sem, 1)
                act.wait_ge(g_st.sem, (l * TB + tb) * (16 * PIECES) + g_st.credit)
                with act.Fori(0, GATE_STEPS // 8) as i:
                    for s in range(8):
                        hidden_step(tb * 4 + (i + 2), s)
                        for a in range(2):
                            Q = (l * TB + tb) * (P // 4) + (i * 16 + (2 * s + a))
                            act.wait_ge(gq_mm.sem, Q + (1 + gq_mm.credit))
                            nc.scalar.copy(g_all[:, :, bass.ds(i * 64 + (8 * s + 4 * a), 4)],
                                           ps[:, a].rearrange("p (t i) -> p i t", t=4)).then_inc(gq_evac.sem, 1)
                last_gelu(tb * 4 + 4)
            with act.Fori(4 * TB, NB // 8 - 1) as jb:
                for s in range(8):
                    hidden_step(jb, s, gelu=s > 0)
                last_gelu(jb + 1)
            def v_hi_step(i, n, lap=0):
                M = l * NV + (i * (4 * G) + n)
                n = n % (4 * G)
                tile = n // G
                act.wait_ge(w_ld[tile].sem, (l * FILLS + (i + ((W_PER + U_PER) // WR + 1 + lap))) * 16)
                act.wait_ge(v_mm.sem, M + 1)
                nc.scalar.copy(v_hi[:, n % 4], wring[:, tile].rearrange("p k n -> p (k n)")
                               [:, (n % G) * 512:(n % G + 1) * 512]).then_inc(vhi_rdy.sem, 1)

            def w_hi_step(B, at_, p):
                act.wait_ge(w32_rdy.sem, l * NB + (B + 1))
                nc.scalar.copy(w_hi[:, at_], w32[:, p]).then_inc(whi_rdy.sem, 1)

            for s in range(8):
                hidden_step(NB // 8 - 1, s, transpose=s < 7, gelu=s > 0)
                if s < G:
                    w_hi_step(s, s, s % 2)
                if s in (5, 6):
                    v_hi_step(0, s - 5)
            last_gelu(NB // 8)

            def unit_step(i, n, last_units):
                if not (last_units and n >= 4 * G - 2):
                    v_hi_step(i, n + 2, (n + 2) // (4 * G))
                if n % 2 == 0 and not (last_units and n >= 2 * G):
                    b = n // 2 + G
                    w_hi_step(i * (2 * G) + b, b % (2 * G), b % 2)

            output_units(act, unit_step)

        squares(xa_evac, DEPTH, -KC)
        root(2 * DEPTH)

        norm(2 * DEPTH, None, None)
        for n in range(2 * TB):
            tb, half = divmod(n, 2)
            bank = (0, 1, 2, 3, 4, 6)[n]
            act.wait_ge(fo_mm.sem, n + 1)
            nc.scalar.copy(y_nat[:, tb, half * 512:(half + 1) * 512], ps[:, bank]).then_inc(fo_evac.sem, 1)

    @block.vector
    def _(dve):
        for sig in (xo_evac, ulo_rdy, vlo_rdy, ac_evac, xa_evac):
            dve.sem_inc(sig.sem, sig.credit)
        V = nc.vector

        def norm(N, which, before=None):
            ch = Chain(dve, norm_ch, N * 5, 5)
            var, t, r = norm_t[:, 0], norm_t[:, 1], norm_t[:, 2]
            dve.wait_ge(sum_mm.sem, N + 1)
            V.tensor_scalar(var, ps[:, 5, 0:T], 1.0 / D, EPS, ALU.mult, ALU.add).then_inc(var_rdy.sem, 1)
            dve.wait_ge(std_rdy.sem, N + 1)
            ch.then(V.reciprocal(r, t))
            ch.then(V.tensor_tensor(t, r, r, ALU.mult))
            ch.then(V.tensor_tensor(t, t, var, ALU.mult))
            ch.then(V.tensor_scalar(t, t, -0.5, 1.5, ALU.mult, ALU.add))
            ch.then(V.tensor_tensor(r, r, t, ALU.mult))
            ch.close()

            def gains(pair):
                k = 2 * pair + 1
                dve.wait_ge(xn_rdy.sem, N * 4 + (pair + 1))
                if which is None:
                    last = V.tensor_scalar(h[:, k], h[:, k], vecs[:, ROW_FG + k:ROW_FG + k + 1], None, ALU.mult)
                else:
                    dve.wait_ge(mods_rdy.sem, N + 1)
                    shift = (SH1, SH2)[which]
                    for v in range(2):
                        last = V.tensor_scalar(h[:, k, seg_cols(v)], h[:, k, seg_cols(v)], gs[:, which, k, v:v + 1],
                                               mods[:, shift + k, v:v + 1], ALU.mult, ALU.add)
                last.then_inc(hv_rdy.sem, 1)

            for pair in range(4):
                k = 2 * pair
                V.tensor_tensor(h[:, k:k + 2], x[:, k:k + 2], r.unsqueeze(1).to_broadcast([P, 2, T]), ALU.mult) \
                    .then_inc(xn_rdy.sem, 1)
                if before is None and pair >= 1:
                    gains(pair - 1)
            if before is not None:
                before()
                for pair in range(3):
                    gains(pair)
            gains(3)

        def add_gated(gate_row, bank, k, evac):
            for v in range(2):
                last = V.scalar_tensor_tensor(x[:, k, seg_cols(v)], ps[:, bank, seg_cols(v)],
                                              mods[:, gate_row + k, v:v + 1], x[:, k, seg_cols(v)],
                                              ALU.mult, ALU.add)
            last.then_inc(evac.sem, 1)

        dve.wait_ge(const_ld.sem, 48)
        V.tensor_copy(iota4[:], iota.unsqueeze(2).to_broadcast([P, P, 4])).then_inc(iota_rdy.sem, 1)
        with dve.Fori(0, DEPTH) as l:
            def modulation(which, banks, scale, gain):
                dve.wait_ge(ada_tr.sem, ada_tr.at(l, which + 1))
                dve.wait_ge(vec_rdy.sem, vec_rdy.at(l, 1))
                ch = Chain(dve, mods_ch, mods_ch.at(l, which), 1)
                for i, bank in enumerate(banks):
                    rows = slice(16 * (which + i), 16 * (which + i + 1))
                    last = V.tensor_tensor(mods[:, rows], ps[:, bank].rearrange("p (j v) -> p j v", v=32)[:, :, 0:2],
                                           vecs[:, rows].unsqueeze(2).to_broadcast([P, 16, 2]), ALU.add)
                ch.then(last)
                ch.close()
                V.scalar_tensor_tensor(gs[:, which], mods[:, scale:scale + KC], 1.0,
                                       vecs[:, gain:gain + KC].unsqueeze(2).to_broadcast([P, KC, 2]),
                                       ALU.add, ALU.mult).then_inc(mods_rdy.sem, 1)



            def low(i, src, pair):
                blocks = slice(2 * pair, 2 * pair + 2)
                dve.wait_ge(sh_rdy.sem, sh_rdy.at(l, 4 * i + pair + 1))
                V.tensor_tensor(h_lo[:, blocks], src[:, blocks], h_hi[:, blocks].bitcast(F32), ALU.subtract) \
                    .then_inc(sl_rdy.sem, 1)

            def columns_low(M):
                dve.wait_ge(ch_rdy.sem, ch_rdy.at(l, M + 1))
                V.tensor_tensor(u_lo[:, M % 2], split_source(M), u_hi[:, M % 2].bitcast(F32), ALU.subtract) \
                    .then_inc(cl_rdy.sem, 1)

            def ahead():
                modulation(0, (6,), SC1, ROW_G1)
                columns_low(0)
                columns_low(1)

            norm(2 * l, 0, before=ahead)
            for pair in range(4):
                low(0, h, pair)
            for M in range(2, 10):
                columns_low(M)

            dve.wait_ge(pj_evac.sem, pj_evac.at(l, 6))
            ch = Chain(dve, conv_ch, conv_ch.at(l, 0), 4)
            ch.then(V.tensor_tensor(conv_u[:], branch[:, 4:6], branch[:, 0:2], ALU.mult))
            columns_low(10)

            def tap(w, b):
                return vecs[:, ROW_CONV + 2 * w + b:ROW_CONV + 2 * w + b + 1]

            for b in range(2):
                last = V.tensor_scalar(y[:, b], conv_u[:, b], tap(1, b), None, ALU.mult)
            ch.then(last)
            columns_low(11)
            for w, to, of in ((0, 1, 0), (2, 0, 1)):
                for b in range(2):
                    for lo, hi in SEGS:
                        n = hi - lo - 1
                        out = y[:, b, lo + to:lo + to + n]
                        last = V.scalar_tensor_tensor(out, conv_u[:, b, lo + of:lo + of + n], tap(w, b), out,
                                                      ALU.mult, ALU.add)
                ch.then(last)
                columns_low(12 if w == 0 else 13)
            ch.close()
            V.tensor_tensor(y[:, 0:2], y[:, 0:2], branch[:, 2:4], ALU.mult)

            dve.wait_ge(pj_evac.sem, pj_evac.at(l, 8))
            ch = Chain(dve, pool_ch, pool_ch.at(l, 0), 6)
            ch.then(V.tensor_tensor(pool_s[:, :, 1:PW], pool_in[:, :, 0:PW - 1], pool_in[:, :, 1:PW], ALU.add))
            columns_low(14)
            ch.then(V.tensor_tensor(pool_r[:, :, 2:PW - 1], pool_s[:, :, 1:PW - 2], pool_s[:, :, 3:PW], ALU.add))
            columns_low(15)
            ch.then(V.tensor_tensor(pool_s[:, 1, 4:PW - 3], pool_r[:, 1, 2:PW - 5], pool_r[:, 1, 6:PW - 1], ALU.add))
            ch.then(V.tensor_tensor(pool_r[64:P, 1, 8:PW - 7], pool_s[64:P, 1, 4:PW - 11], pool_s[64:P, 1, 12:PW - 3],
                                    ALU.add))
            columns_low(16)
            ch.then(V.tensor_copy(pool_s[64:P, :, PAD:PW - PAD], pool_r[64:P, :, PAD:PW - PAD]))
            dve.wait_ge(mix_ld.sem, mix_ld.at(l, 16))
            for v, (lo, hi) in enumerate(SEGS):
                cols = slice(SEG_AT[v], SEG_AT[v] + hi - lo)
                last = V.tensor_tensor(pool_d[:, :, lo:hi], pool_s[:, :, cols], rcnt[:, :, lo:hi], ALU.mult)
            ch.then(last)
            ch.close()
            columns_low(17)
            for v, (lo, hi) in enumerate(SEGS):
                cols = slice(SEG_AT[v], SEG_AT[v] + hi - lo)
                last = V.tensor_tensor(pool_d[:, :, lo:hi], pool_d[:, :, lo:hi], pool_in[:, :, cols], ALU.subtract)
            last.then_inc(pd_rdy.sem, 1)
            columns_low(18)
            columns_low(19)
            dve.wait_ge(pool_mm.sem, pool_mm.at(l, 1))
            for b, bank in enumerate((4, 7)):
                last = V.tensor_scalar(y[:, 2 + b], ps[:, bank, 0:T], vecs[:, ROW_PS + b:ROW_PS + b + 1], None,
                                       ALU.mult)
            last.then_inc(branch_rdy.sem, 1)

            ch = Chain(dve, att_ch, att_ch.at(l, 0), 2 * NU)
            for n in range(NU + 1):
                if n < NU:
                    head, b, _, _ = unit(n)
                    keys = P if b == 0 else KEYS
                    dve.wait_ge(s_mm.sem, s_mm.at(l, n + 1))
                    ch.then(V.reduce_max(stat[:, n % 3, 0:1], ps[:, s_bank(n), 0:keys], AX.X))
                    V.tensor_scalar(stat[:, n % 3, 1:2], stat[:, n % 3, 0:1], -1.0, None, ALU.mult) \
                        .then_inc(nmax_rdy.sem, 1)
                if n == ADA_TURN + 2:
                    modulation(1, (4, 7), SC2, ROW_G2)
                if n == 2:
                    low(1, y, 0)
                    low(1, y, 1)
                if n == NU // 2 + 2:
                    low(1, y, 2)
                if n == OUT_AHEAD:
                    columns_low(SP_OUT0)
                    columns_low(SP_OUT0 + 1)
                if n >= 1:
                    m = n - 1
                    keys = P if unit(m)[1] == 0 else KEYS
                    dve.wait_ge(exp_rdy.sem, exp_rdy.at(l, m + 1))
                    ch.then(V.reciprocal(stat[:, m % 3, 3:4], stat[:, m % 3, 2:3]))
                    V.tensor_scalar(pr[:, m % 3, 0:keys], pr[:, m % 3, 0:keys], stat[:, m % 3, 3:4], None,
                                    ALU.mult).then_inc(pr_rdy.sem, 1)
            ch.close()
            low(1, y, 3)
            for k in range(KC):
                dve.wait_ge(xo_mm.sem, xo_mm.at(l, k + 1))
                add_gated(GT1, k % 2, k, xo_evac)
                columns_low(SP_OUT0 + 2 + k)
            norm(2 * l + 1, 1)
            for pair in range(4):
                low(2, h, pair)
            for M in range(SP_WQ0 + 2, N_SPLIT):
                columns_low(M)

            def hidden_step(jb, s):
                J = l * NB + (jb * 8 + s)
                for hh in range(2):
                    dve.wait_ge(uhi_rdy.sem, 2 * J + (hh + 3))
                    part_ = slice(4 * hh, 4 * hh + 4)
                    V.tensor_tensor(u_lo[:, (s + 1) % 2, part_], ps[:, 3 + hh].rearrange("p (k e) -> p k e", e=P),
                                    u_hi[:, (s + 1) % 2, part_].bitcast(F32), ALU.subtract) \
                        .then_inc(ulo_rdy.sem, 1)

            hidden_step(0, -1)
            with dve.Fori(0, TB) as tb:
                B = l * TB + tb
                ch = Chain(dve, route_ch, B * ROUTE_STEPS, ROUTE_STEPS)
                dve.wait_ge(sc_evac.sem, sc_evac.at(l, 4))
                dve.wait_ge(s_next.sem, B + 1)
                dve.wait_ge(iota_rdy.sem, 1)
                dve.sem_inc(dve_passed.sem, 1)
                for n in range(HP):
                    last = V.max(top_s[:, n, 0:8], s_sb[:, n])
                ch.then(last)
                hidden_step(tb * 4, 0)
                for n in range(HP):
                    last = V.match_replace(left[:, n], top_s[:, n, 0:8], s_sb[:, n], NEG)
                ch.then(last)
                hidden_step(tb * 4, 1)
                for n in range(HP):
                    V.max_index(top_iu[:, n, 0:8], top_s[:, n, 0:8], s_sb[:, n])
                hidden_step(tb * 4, 2)
                for n in range(HP):
                    last = V.max(top_s[:, n, 8:16], left[:, n])
                ch.then(last)
                hidden_step(tb * 4, 3)
                for n in range(HP):
                    last = V.max_index(top_iu[:, n, 8:16], top_s[:, n, 8:16], left[:, n])
                ch.then(last)
                hidden_step(tb * 4, 4)
                tops = top_s[:].rearrange("p (h q) k -> p h q k", q=2)
                cand = s_sb[:].rearrange("p (h q) (a b) -> p h (q a) b", q=2, b=TOPK)
                ch.then(V.tensor_tensor(cand, tops[:, :, 0].unsqueeze(3).to_broadcast([P, PH, TOPK, TOPK]),
                                        tops[:, :, 1].unsqueeze(2).to_broadcast([P, PH, TOPK, TOPK]), ALU.add))
                V.tensor_copy(top_i[:], top_iu[:])
                hidden_step(tb * 4, 5)
                cands = s_sb[:].rearrange("p (h q) k -> p h (q k)", q=2)
                lefts = left[:].rearrange("p (h q) k -> p h (q k)", q=2)
                for n in range(PH):
                    last = V.max(best[:, n, 0:8], cands[:, n])
                ch.then(last)
                hidden_step(tb * 4, 6)
                for n in range(PH):
                    last = V.match_replace(lefts[:, n], best[:, n, 0:8], cands[:, n], NEG)
                ch.then(last)
                hidden_step(tb * 4, 7)
                for n in range(PH):
                    V.max_index(best_iu[:, n, 0:8], best[:, n, 0:8], cands[:, n])
                hidden_step(tb * 4, 8)
                for n in range(PH):
                    last = V.max(best[:, n, 8:16], lefts[:, n])
                ch.then(last)
                gates = picked[:, 2].rearrange("p (h k) -> p h k", k=TOPK)
                V.tensor_tensor(gates, best[:], best[:, :, 0:1].to_broadcast([P, PH, TOPK]), ALU.subtract) \
                    .then_inc(gexp_in.sem, 1)
                hidden_step(tb * 4, 9)
                for n in range(PH):
                    last = V.max_index(best_iu[:, n, 8:16], best[:, n, 8:16], lefts[:, n])
                ch.then(last)
                hidden_step(tb * 4, 10)
                part_u = top_iu[:].rearrange("p (q h) k -> p q h k", q=2)
                V.tensor_scalar(part_u[:, 0], best_iu[:], 4, None, ALU.logical_shift_right)
                ch.then(V.tensor_scalar(part_u[:, 1], best_iu[:], TOPK - 1, None, ALU.bitwise_and))
                ch.then(V.tensor_copy(part[:], part_u))
                left4 = left[:].rearrange("p (h q) (a b) -> p h (q a) b", q=2, b=TOPK)
                keys_i = top_i[:].rearrange("p (h q) k -> p h q k", q=2)
                picks = (cand, left4)
                for q in range(2):
                    last = V.tensor_tensor(picks[q].rearrange("p h a b -> p (h a) b"),
                                           part[:, q].rearrange("p h k -> p (h k)").unsqueeze(2)
                                           .to_broadcast([P, PH * TOPK, TOPK]),
                                           iota[:, 0:TOPK].unsqueeze(1).to_broadcast([P, PH * TOPK, TOPK]),
                                           ALU.is_equal)
                ch.then(last)
                hidden_step(tb * 4, 11)
                for q in range(2):
                    last = V.tensor_tensor(picks[q], picks[q],
                                           keys_i[:, :, q].unsqueeze(2).to_broadcast([P, PH, TOPK, TOPK]), ALU.mult)
                ch.then(last)
                hidden_step(tb * 4, 12)
                dve.wait_ge(gexp_rdy.sem, B + 1)
                ch.then(V.reduce_sum(gsum[:, 0], gates, AX.X))
                ch.then(V.reciprocal(gsum[:, 1], gsum[:, 0]))
                ch.close()
                V.tensor_tensor(gates, gates, gsum[:, 1].unsqueeze(2).to_broadcast([P, PH, TOPK]), ALU.mult)
                V.reduce_sum(picked[:, 0], picks[0].rearrange("p h a b -> p (h a) b"), AX.X) \
                    .then_inc(s_free.sem, 1)
                hidden_step(tb * 4, 13)
                V.reduce_sum(picked[:, 1], picks[1].rearrange("p h a b -> p (h a) b"), AX.X) \
                    .then_inc(pk_rdy.sem, 1)
                hidden_step(tb * 4, 14)
                hidden_step(tb * 4, 15)

                dve.wait_ge(pk_evac.sem, B + 1)
                ch = Chain(dve, pt_ch, B * 4, 4)
                ch.then(V.tensor_copy(pickT[:, 2], gres[:, 0]))
                ch.then(V.tensor_tensor(gres[:, 1], gres[:, 0], pickT[:, 2], ALU.subtract))
                ch.then(V.tensor_copy(pickT[:, 3], gres[:, 1]))
                ch.then(V.tensor_tensor(pickT[:, 4], gres[:, 1], pickT[:, 3], ALU.subtract), dve_passed)
                ch.close()
                with dve.Fori(0, GATE_STEPS // 8) as i:
                    for s in range(8):
                        for a in range(2):
                            Q = B * (P // 4) + (i * 16 + (2 * s + a))
                            tok = bass.ds(i * 64 + (8 * s + 4 * a), 4)

                            def per_token(row):
                                return pickT[:, row, tok].unsqueeze(1).to_broadcast([P, P, 4])

                            dve.wait_ge(gq_mm.sem, Q + 1)
                            V.tensor_tensor(one_e[:, a], iota4[:], per_token(0), ALU.is_equal) \
                                .then_inc(oe_ch.sem, 1)
                            V.tensor_tensor(one_a[:, a], iota4[:], per_token(1), ALU.is_equal)
                            dve.wait_ge(oe_ch.sem, Q + 1)
                            for k in range(3):
                                last = V.tensor_tensor(one_b[:, a, k], one_e[:, a], per_token(2 + k), ALU.mult)
                            last.then_inc(one_rdy.sem, 1)
                        hidden_step(tb * 4 + (i + 2), s)
            with dve.Fori(4 * TB, NB // 8 - 1) as jb:
                for s in range(8):
                    hidden_step(jb, s)
            def v_lo_step(i, n):
                M = l * NV + (i * (4 * G) + n)
                n = n % (4 * G)
                dve.wait_ge(vhi_rdy.sem, M + 1)
                V.tensor_tensor(v_lo[:, n % 4], wring[:, n // G].rearrange("p k n -> p (k n)")
                                [:, (n % G) * 512:(n % G + 1) * 512], v_hi[:, n % 4].bitcast(F32),
                                ALU.subtract).then_inc(vlo_rdy.sem, 1)

            def w_mult(B, buf, b, p):
                V.tensor_tensor(w32[:, p], act2[:, buf, b], gate2[:, buf, b], ALU.mult).then_inc(w32_rdy.sem, 1)

            def w_lo_step(B, at_, p):
                dve.wait_ge(whi_rdy.sem, l * NB + (B + 1))
                V.tensor_tensor(w_lo[:, at_], w32[:, p], w_hi[:, at_].bitcast(F32), ALU.subtract) \
                    .then_inc(wlo_rdy.sem, 1)

            for s in range(8):
                if s < 7:
                    hidden_step(NB // 8 - 1, s)
                if s == 0:
                    dve.wait_ge(ga_ld[0].sem, ga_ld[0].at(l, 32))
                if s < G:
                    w_mult(s, 0, s, s % 2)
                    w_lo_step(s, s, s % 2)
                if s in (5, 6):
                    v_lo_step(0, s - 5)
            dve.wait_ge(acc_zero.sem, acc_zero.at(l, 1))
            dve.sem_inc(dve_passed.sem, 1)

            def add_sums(i, e):
                half = e % 2
                dve.wait_ge(v_mm.sem, l * NV + (i * (4 * G) + (G * (e + 1) + v_mm.credit)))
                dve.wait_ge(ac_evac.sem, l * (2 * NG) + (i * 4 + (e + 1)))
                for tb in range(TB):
                    cols = slice(half * 512, (half + 1) * 512)
                    last = V.tensor_tensor(acc[:, tb, cols], acc[:, tb, cols], ps[:, 3 * half + tb], ALU.add)
                last.then_inc(ac_evac.sem, 1)

            def unit_step(i, n, last_units):
                next_w = n % 2 == 0 and not (last_units and n >= 2 * G)
                b = n // 2 + G
                B = i * (2 * G) + b
                if next_w:
                    buf = (b // G) % 2
                    if b % G == 0:
                        dve.wait_ge(ga_ld[buf].sem, (l * (NG // 2) + (i + (b // (2 * G) + 1))) * 32)
                    w_mult(B, buf, b % G, b % 2)
                if not (last_units and n >= 4 * G - 2):
                    v_lo_step(i, n + 2)
                if next_w:
                    w_lo_step(B, b % (2 * G), b % 2)
                if n % G == 1 and n >= G:
                    add_sums(i, n // G - 1)
                if n == 4 * G - 1:
                    add_sums(i, 3)

            output_units(dve, unit_step)
            for k in range(KC):
                dve.wait_ge(xa_mm.sem, xa_mm.at(l, k + 1))
                add_gated(GT2, k % 2, k, xa_evac)
        norm(2 * DEPTH, None)

    ctx.close()


def constants():
    out = np.zeros((P, NCONST), np.float32)
    out[:, C_ID:C_ID + P] = np.eye(P)
    m = np.arange(P)
    out[m // GRID * GRID + GRID - 1 - m % GRID, C_FLIP + m] = 1.0
    out[:, C_ONE:C_ONE + P] = 1.0
    out[:, C_IOTA:C_IOTA + P] = np.arange(P)
    q = GRID - 1 - np.arange(P)[:, None] % GRID
    k = np.arange(GRID)[None, :]
    start = np.clip(q - NCOLS // 2, 0, GRID - NCOLS)
    out[:, C_MASK:C_MASK + GRID] = np.where((k >= start) & (k < start + NCOLS), 0.0, -1e30)
    for b in range(2):
        for half in range(2):
            w = 2 ** (2 * b + half + 1)
            for lo, hi in SEGS:
                t, n = np.arange(hi - lo), hi - lo
                count = np.clip(t + w - 1 - w // 2, 0, n - 1) - np.clip(t - w // 2, 0, n - 1) + 1
                out[64 * half:64 * half + 64, C_RCNT + b * T + lo:C_RCNT + b * T + hi] = 1.0 / count
    return out


INS = ["x_prompt", "x_sample", "c", "cache_k", "cache_v", "c_ctx", "norm1_g", "norm2_g", "w_ada", "b_ada",
       "w_in", "conv_w", "pool_w", "pool_scale", "rpb", "w_out", "peer_wq", "peer_subkeys", "peer_u",
       "peer_v", "final_g"]
OUTS = [(1, TCTX, D), (1, TLAT, D), (1, DEPTH, NH, TCTX, HD), (1, DEPTH, NH, TCTX, HD)]


def kernel(**inputs):
    import numpy as _np
    import concourse.bacc as _bacc
    from concourse import mybir as _mybir
    from concourse.bass_utils import run_bass_kernel_spmd as _run

    nc = _bacc.Bacc("TRN2", target_bir_lowering=False, num_devices=1)
    arrays, args = {}, []
    for name in INS + ["consts"]:
        a = _np.ascontiguousarray(constants() if name == "consts" else inputs[name])
        arrays[f"in_{name}_dram"] = a
        args.append(nc.dram_tensor(f"in_{name}_dram", a.shape, _mybir.dt.from_np(a.dtype), kind="ExternalInput").ap())
    for i, shape in enumerate(OUTS):
        args.append(nc.dram_tensor(f"out_{i}_dram", shape, F32, kind="ExternalOutput").ap())
    build(nc, *args)
    r = _run(nc, [arrays], core_ids=[0])
    return tuple(r.results[0][f"out_{i}_dram"] for i in range(len(OUTS)))
```
